# Optimizing a Trainium2 kernel written in Bass

```python
import jax, jax.numpy as jnp
from jax import lax
import numpy as np

D_MODEL = 1024
BATCH = 1
SEQ = 512
DEPTH = 2

N_MEM = 256
ROPE_THETA = 500000.0
EPS = 1e-6
BLOCK = 128
NEG = -1e30

MLA_HEADS = 8
MLA_NOPE = 64
MLA_ROPE = 32
MLA_V = 64
MLA_Q_LORA = 256
MLA_KV_LORA = 128

ML_HEADS = 4
ML_DK = 64
ML_DV = 64
ML_CONV = 4
ML_CHUNK = 128

SW_HEADS = 4
SW_HD = 64
SW_ROT = SW_HD // 4
SW_CONFIGS = ((128, 1), (512, 4), (2048, 16))

X_HEADS = 4
X_HD = D_MODEL // X_HEADS

D_FF = 256 * (-(-(8 * D_MODEL) // (3 * 256)))

MLA_W = MLA_HEADS * MLA_V
ML_W = ML_HEADS * ML_DV
SW_W = SW_HEADS * SW_HD
D_MIX = MLA_W + ML_W + SW_W

IN_SIZES = (MLA_Q_LORA, MLA_KV_LORA, MLA_ROPE,
            ML_HEADS * ML_DK, ML_HEADS * ML_DK, ML_W, ML_W, ML_HEADS, ML_HEADS,
            SW_W, SW_W, SW_W)
D_IN = sum(IN_SIZES)

kernel_name = "hybrid_mla_mlstm_dilated_swa_trunk"

def rms_norm(x, g):
    xf = x.astype(jnp.float32)
    y = xf * lax.rsqrt(jnp.mean(xf * xf, axis=-1, keepdims=True) + EPS)
    return (y * g.astype(jnp.float32)).astype(x.dtype)

def rope_tables(seq, d_rot):
    inv = ROPE_THETA ** (-jnp.arange(0, d_rot, 2, dtype=jnp.float32) / d_rot)
    ang = jnp.arange(seq, dtype=jnp.float32)[:, None] * inv[None, :]
    return jnp.cos(ang), jnp.sin(ang)

def apply_rope(x, cos, sin):
    xf = x.astype(jnp.float32)
    half = xf.shape[-1] // 2
    x1, x2 = xf[..., :half], xf[..., half:]
    c = cos[None, :, None, :]
    s = sin[None, :, None, :]
    return jnp.concatenate([x1 * c - x2 * s, x2 * c + x1 * s], axis=-1).astype(x.dtype)

def partial_rope(x, cos, sin):
    return jnp.concatenate([apply_rope(x[..., :SW_ROT], cos, sin), x[..., SW_ROT:]], axis=-1)

def causal_block_attention(q, k, v, scale):
    B, S, H, Dk = q.shape
    Dv = v.shape[-1]
    nb = S // BLOCK
    qb = q.reshape(B, nb, BLOCK, H, Dk).transpose(1, 0, 2, 3, 4)
    kpos = jnp.arange(S)

    def one(args):
        q_blk, blk = args
        s = jnp.einsum('bqhd,bkhd->bhqk', q_blk, k, preferred_element_type=jnp.float32) * scale
        qpos = blk * BLOCK + jnp.arange(BLOCK)
        s = jnp.where(kpos[None, :] <= qpos[:, None], s, NEG)
        p = jax.nn.softmax(s, axis=-1)
        return jnp.einsum('bhqk,bkhd->bqhd', p.astype(v.dtype), v)

    out = lax.map(one, (qb, jnp.arange(nb)))
    return out.transpose(1, 0, 2, 3, 4).reshape(B, S, H, Dv)

def mla_mixer(c_q, c_kv, k_rope, q_norm_g, w_uq, kv_norm_g, w_ukv, cos, sin):
    B, S, _ = c_q.shape
    q = (rms_norm(c_q, q_norm_g) @ w_uq).reshape(B, S, MLA_HEADS, MLA_NOPE + MLA_ROPE)
    q = jnp.concatenate([q[..., :MLA_NOPE], apply_rope(q[..., MLA_NOPE:], cos, sin)], axis=-1)
    kv = (rms_norm(c_kv, kv_norm_g) @ w_ukv).reshape(B, S, MLA_HEADS, MLA_NOPE + MLA_V)
    k_pe = apply_rope(k_rope[:, :, None, :], cos, sin)
    k = jnp.concatenate([kv[..., :MLA_NOPE], jnp.broadcast_to(k_pe, (B, S, MLA_HEADS, MLA_ROPE))], axis=-1)
    v = kv[..., MLA_NOPE:]
    out = causal_block_attention(q, k, v, (MLA_NOPE + MLA_ROPE) ** -0.5)
    return out.reshape(B, S, MLA_W)

def causal_depthwise_conv(x, w, b):
    K = w.shape[0]
    y = lax.conv_general_dilated(x, w[:, None, :].astype(x.dtype), window_strides=(1,),
                                 padding=[(K - 1, 0)], dimension_numbers=('NWC', 'WIO', 'NWC'),
                                 feature_group_count=x.shape[-1])
    return y + b

def mlstm_mixer(q_pre, k_pre, v_in, o_pre, i_pre, f_pre, conv_w, conv_b, b_i, b_f):
    B, S, _ = v_in.shape
    f32 = jnp.float32
    qk = jax.nn.silu(causal_depthwise_conv(jnp.concatenate([q_pre, k_pre], axis=-1), conv_w, conv_b))
    q = qk[..., :ML_HEADS * ML_DK].reshape(B, S, ML_HEADS, ML_DK).astype(f32)
    k = qk[..., ML_HEADS * ML_DK:].reshape(B, S, ML_HEADS, ML_DK).astype(f32) * ML_DK ** -0.5
    v = v_in.reshape(B, S, ML_HEADS, ML_DV).astype(f32)
    log_i = (i_pre + b_i).astype(f32)
    log_f = jax.nn.log_sigmoid((f_pre + b_f).astype(f32))
    L = ML_CHUNK
    nc = S // L

    def to_chunks(a):
        return a.reshape(B, nc, L, ML_HEADS, -1).transpose(1, 0, 3, 2, 4)

    def gate_chunks(a):
        return a.reshape(B, nc, L, ML_HEADS).transpose(1, 0, 3, 2)

    causal = jnp.tril(jnp.ones((L, L), dtype=bool))

    def step(carry, inp):
        C, n, m = carry
        qc, kc, vc, li, lf = inp
        b = jnp.cumsum(lf, axis=-1)
        D = jnp.where(causal, b[..., :, None] - b[..., None, :] + li[..., None, :], NEG)
        inter = b + m[..., None]
        m_t = jnp.maximum(inter, jnp.max(D, axis=-1))
        w_intra = jnp.exp(D - m_t[..., None])
        w_inter = jnp.exp(inter - m_t)
        s = jnp.einsum('bhtd,bhsd->bhts', qc, kc) * w_intra
        num = jnp.einsum('bhts,bhsv->bhtv', s, vc) + w_inter[..., None] * jnp.einsum('bhtk,bhkv->bhtv', qc, C)
        nq = jnp.sum(s, axis=-1) + w_inter * jnp.einsum('bhtk,bhk->bht', qc, n)
        h = num / jnp.maximum(jnp.abs(nq), jnp.exp(-m_t))[..., None]
        bL = b[..., -1]
        g = bL[..., None] - b + li
        m_new = jnp.maximum(bL + m, jnp.max(g, axis=-1))
        decay = jnp.exp(bL + m - m_new)
        ws = jnp.exp(g - m_new[..., None])
        C = decay[..., None, None] * C + jnp.einsum('bhs,bhsk,bhsv->bhkv', ws, kc, vc)
        n = decay[..., None] * n + jnp.einsum('bhs,bhsk->bhk', ws, kc)
        return (C, n, m_new), h

    init = (jnp.zeros((B, ML_HEADS, ML_DK, ML_DV), f32),
            jnp.zeros((B, ML_HEADS, ML_DK), f32),
            jnp.full((B, ML_HEADS), NEG, f32))
    _, h = lax.scan(step, init, (to_chunks(q), to_chunks(k), to_chunks(v), gate_chunks(log_i), gate_chunks(log_f)))
    h = h.transpose(1, 0, 3, 2, 4).reshape(B, S, ML_W)
    return (jax.nn.sigmoid(o_pre.astype(f32)) * h).astype(v_in.dtype)

def dilated_branch(q, k, v, dil, n_back, scale):
    B, S, H, D = q.shape
    Ls = S // dil

    def sub(a):
        return a.reshape(B, Ls, dil, H, D).transpose(0, 2, 3, 1, 4)

    nb = -(-Ls // BLOCK)
    Lp = nb * BLOCK
    qs = jnp.pad(sub(q), ((0, 0), (0, 0), (0, 0), (0, Lp - Ls), (0, 0))).reshape(B, dil, H, nb, BLOCK, D)
    kpad = ((0, 0), (0, 0), (0, 0), (BLOCK, Lp - Ls), (0, 0))
    kp = jnp.pad(sub(k), kpad).reshape(B, dil, H, nb + 1, BLOCK, D)
    vp = jnp.pad(sub(v), kpad).reshape(B, dil, H, nb + 1, BLOCK, D)
    kw = jnp.concatenate([kp[:, :, :, :-1], kp[:, :, :, 1:]], axis=4)
    vw = jnp.concatenate([vp[:, :, :, :-1], vp[:, :, :, 1:]], axis=4)
    s = jnp.einsum('brhnqd,brhnkd->brhnqk', qs, kw, preferred_element_type=jnp.float32) * scale
    qi = jnp.arange(BLOCK)[:, None]
    kj = jnp.arange(2 * BLOCK)[None, :] - BLOCK
    dist = qi - kj
    kidx = jnp.arange(nb)[:, None, None] * BLOCK + kj[None]
    valid = ((dist >= 0) & (dist <= n_back))[None] & (kidx >= 0)
    s = jnp.where(valid, s, NEG)
    mx = jnp.max(s, axis=-1, keepdims=True)
    e = jnp.exp(s - mx)
    den = jnp.sum(e, axis=-1)
    o = jnp.einsum('brhnqk,brhnkd->brhnqd', e, vw.astype(jnp.float32)) / den[..., None]
    lse = mx[..., 0] + jnp.log(den)
    o = o.reshape(B, dil, H, Lp, D)[:, :, :, :Ls].transpose(0, 3, 1, 2, 4).reshape(B, S, H, D)
    lse = lse.reshape(B, dil, H, Lp)[..., :Ls].transpose(0, 3, 1, 2).reshape(B, S, H)
    return o, lse

def dilated_swa_mixer(q_in, k_in, v_in, cos, sin):
    B, S, _ = q_in.shape
    q = partial_rope(q_in.reshape(B, S, SW_HEADS, SW_HD), cos, sin)
    k = partial_rope(k_in.reshape(B, S, SW_HEADS, SW_HD), cos, sin)
    v = v_in.reshape(B, S, SW_HEADS, SW_HD)
    outs, lses = [], []
    for window, dil in SW_CONFIGS:
        o, lse = dilated_branch(q, k, v, dil, window // dil, SW_HD ** -0.5)
        outs.append(o)
        lses.append(lse)
    wts = jax.nn.softmax(jnp.stack(lses, axis=0), axis=0)
    out = jnp.einsum('gbsh,gbshd->bshd', wts, jnp.stack(outs, axis=0))
    return out.reshape(B, S, SW_W).astype(q_in.dtype)

def memory_cross_attention(h, mem_n, w_q, w_kv, w_o):
    B, S, _ = h.shape
    q = (h @ w_q).reshape(B, S, X_HEADS, X_HD)
    kv = (mem_n @ w_kv).reshape(B, mem_n.shape[1], 2, X_HEADS, X_HD)
    k, v = kv[:, :, 0], kv[:, :, 1]
    s = jnp.einsum('bshd,bmhd->bhsm', q, k, preferred_element_type=jnp.float32) * X_HD ** -0.5
    p = jax.nn.softmax(s, axis=-1)
    o = jnp.einsum('bhsm,bmhd->bshd', p.astype(v.dtype), v).reshape(B, S, D_MODEL)
    return o @ w_o

def swiglu(h, w_gate_up, w_down):
    g, u = jnp.split(h @ w_gate_up, 2, axis=-1)
    return (jax.nn.silu(g) * u) @ w_down

def setup_inputs(seed: int = 0) -> dict:
    key = jax.random.key(seed)
    ks = list(jax.random.split(key, 32))
    f32 = jnp.float32

    def w(shape, fan_in):
        return jax.random.normal(ks.pop(), shape, f32) * fan_in ** -0.5

    def gain(shape):
        return 1.0 + 0.02 * jax.random.normal(ks.pop(), shape, f32)

    def bias(shape, scale=0.01):
        return scale * jax.random.normal(ks.pop(), shape, f32)

    return {
        "x": jax.random.normal(ks.pop(), (BATCH, SEQ, D_MODEL), f32),
        "mem": jax.random.normal(ks.pop(), (BATCH, N_MEM, D_MODEL), f32),
        "w_in": w((DEPTH, D_MODEL, D_IN), D_MODEL),
        "mla_q_norm": gain((DEPTH, MLA_Q_LORA)),
        "mla_w_uq": w((DEPTH, MLA_Q_LORA, MLA_HEADS * (MLA_NOPE + MLA_ROPE)), MLA_Q_LORA),
        "mla_kv_norm": gain((DEPTH, MLA_KV_LORA)),
        "mla_w_ukv": w((DEPTH, MLA_KV_LORA, MLA_HEADS * (MLA_NOPE + MLA_V)), MLA_KV_LORA),
        "ml_conv_w": w((DEPTH, ML_CONV, 2 * ML_HEADS * ML_DK), ML_CONV),
        "ml_conv_b": bias((DEPTH, 2 * ML_HEADS * ML_DK)),
        "ml_b_i": bias((DEPTH, ML_HEADS), 0.1),
        "ml_b_f": jnp.linspace(3.0, 6.0, ML_HEADS, dtype=f32)[None, :] + bias((DEPTH, ML_HEADS)),
        "w_out": w((DEPTH, D_MIX, D_MODEL), D_MIX),
        "x_w_q": w((DEPTH, D_MODEL, D_MODEL), D_MODEL),
        "x_w_kv": w((DEPTH, D_MODEL, 2 * D_MODEL), D_MODEL),
        "x_w_o": w((DEPTH, D_MODEL, D_MODEL), D_MODEL),
        "w_gate_up": w((DEPTH, D_MODEL, 2 * D_FF), D_MODEL),
        "w_down": w((DEPTH, D_FF, D_MODEL), D_FF),
        "norm_mix_pre": gain((DEPTH, D_MODEL)),
        "norm_mix_post": gain((DEPTH, D_MODEL)),
        "norm_mem": gain((DEPTH, D_MODEL)),
        "norm_x_pre": gain((DEPTH, D_MODEL)),
        "norm_x_post": gain((DEPTH, D_MODEL)),
        "norm_ffn_pre": gain((DEPTH, D_MODEL)),
        "norm_ffn_post": gain((DEPTH, D_MODEL)),
    }

def reference(x, mem, w_in, mla_q_norm, mla_w_uq, mla_kv_norm, mla_w_ukv, ml_conv_w, ml_conv_b,
              ml_b_i, ml_b_f, w_out, x_w_q, x_w_kv, x_w_o, w_gate_up, w_down,
              norm_mix_pre, norm_mix_post, norm_mem, norm_x_pre, norm_x_post, norm_ffn_pre, norm_ffn_post):
    S = x.shape[1]
    cos_mla, sin_mla = rope_tables(S, MLA_ROPE)
    cos_sw, sin_sw = rope_tables(S, SW_ROT)
    splits = np.cumsum(IN_SIZES)[:-1].tolist()
    for l in range(DEPTH):
        h = rms_norm(x, norm_mix_pre[l])
        (c_q, c_kv, k_rope, ml_q, ml_k, ml_v, ml_o, ml_i, ml_f,
         sw_q, sw_k, sw_v) = jnp.split(h @ w_in[l], splits, axis=-1)
        y_a = mla_mixer(c_q, c_kv, k_rope, mla_q_norm[l], mla_w_uq[l], mla_kv_norm[l], mla_w_ukv[l],
                        cos_mla, sin_mla)
        y_b = mlstm_mixer(ml_q, ml_k, ml_v, ml_o, ml_i, ml_f, ml_conv_w[l], ml_conv_b[l], ml_b_i[l], ml_b_f[l])
        y_c = dilated_swa_mixer(sw_q, sw_k, sw_v, cos_sw, sin_sw)
        y = jnp.concatenate([y_a, y_b, y_c], axis=-1) @ w_out[l]
        x = x + rms_norm(y, norm_mix_post[l])
        h = rms_norm(x, norm_x_pre[l])
        y = memory_cross_attention(h, rms_norm(mem, norm_mem[l]), x_w_q[l], x_w_kv[l], x_w_o[l])
        x = x + rms_norm(y, norm_x_post[l])
        h = rms_norm(x, norm_ffn_pre[l])
        y = swiglu(h, w_gate_up[l], w_down[l])
        x = x + rms_norm(y, norm_ffn_post[l])
    return x


_drawn_inputs = setup_inputs


def setup_inputs(seed=0):
    import zlib

    import numpy as np

    out = dict(_drawn_inputs(seed))
    spreads = {}
    factors = {'mla_q_norm': 4.307,
     'mla_kv_norm': 2.897,
     'ml_b_i': 3.158,
     'norm_x_pre': 3.219,
     'norm_x_post': 3.007,
     'norm_ffn_pre': 2.696,
     'norm_ffn_post': 3.547,
     'ml_conv_b': 4.594}
    for name, (base, spread) in spreads.items():
        noise = np.random.default_rng([zlib.crc32(name.encode()), seed]).standard_normal(out[name].shape)
        drawn = base * np.exp(spread * noise) if base else spread * noise
        out[name] = __import__('jax').numpy.asarray(drawn.astype(out[name].dtype))
    for name, factor in factors.items():
        out[name] = (out[name] * factor).astype(out[name].dtype)
    return out
```

```python
from contextlib import ExitStack

import numpy as np
import concourse.bass as bass
from concourse import mybir

F32 = mybir.dt.float32
F32R = mybir.dt.float32r
ALU = mybir.AluOpType
ACT = mybir.ActivationFunctionType

P = 128
D_MODEL = 1024
SEQ = 512
DEPTH = 2
N_MEM = 256
ROPE_THETA = 500000.0
EPS = 1e-6
NEG = -1e30

MLA_HEADS, MLA_NOPE, MLA_ROPE, MLA_V = 8, 64, 32, 64
MLA_Q_LORA, MLA_KV_LORA = 256, 128
ML_HEADS, ML_DK, ML_CONV = 4, 64, 4
SW_HEADS, SW_HD = 4, 64
SW_ROT = SW_HD // 4
SW_CONFIGS = ((128, 1), (512, 4), (2048, 16))
X_HEADS = 4
X_HD = D_MODEL // X_HEADS
D_FF = 2816

KT = D_MODEL // P
TB = SEQ // P
FT = D_FF // P
UNIT = KT * P

U_IN = 0
IN_FM = 14
CQ, CKV, MISC, MLQK, SWQK, OG = 0, 2, 3, 4, 8, 12
U_INV = U_IN + IN_FM
U_UQ = U_INV + 4
U_UK = U_UQ + 2
U_UV = U_UK + 1
U_OUT = U_UV + 1
U_XK = U_OUT + 8
U_XV = U_XK + 8
U_XQ = U_XV + 8
U_XO = U_XQ + 8
U_FF = U_XO + 8
U_DOWN = U_FF + 2 * FT
N_UNITS = U_DOWN + FT
RING = 4

G_MIX_PRE, G_MIX_POST, G_MEM, G_X_PRE, G_X_POST, G_FFN_PRE, G_FFN_POST = (KT * i for i in range(7))
G_Q = 7 * KT
G_KV = G_Q + 2
G_CONV_W = G_KV + 1
G_CONV_B = G_CONV_W + 4 * ML_CONV
G_GATE_B = G_CONV_B + 4
N_GAINS = G_GATE_B + 1

C_ROPE_Q = 0
C_SW_COS = C_ROPE_Q + SEQ
C_SW_SIN = C_SW_COS + SEQ
C_CAUSAL = C_SW_SIN + SEQ
C_DILATED = C_CAUSAL + SEQ
C_CAUSAL_T = C_DILATED + SEQ
C_IDENT = C_CAUSAL_T + SEQ
C_ROT = C_IDENT + P
C_ONES = C_ROT + P
C_ONE_ROWS = C_ROPE_Q
N_CONST = C_ONES + P

ROW_I, ROW_F, ROW_R, ROW_RS = 0, 32, 64, 96


def tile_plan():
    plan, uses = {}, []

    def add(name, tiles, engine):
        plan[name] = []
        for sub in tiles:
            plan[name].append((len(uses), sub))
            uses.append((sub, engine))

    def whole(u0, n):
        return [[(u0 + m, k * P) for k in range(KT)] for m in range(n)]

    add("in", whole(U_IN, IN_FM), "act")
    add("uq", [[(U_UQ + h // 4, ((h % 4) * 2 + k) * P) for k in range(2)] for h in range(MLA_HEADS)], "dve")
    add("uk", [[(U_UK, m * P)] for m in range(4)], "act")
    add("uv", [[(U_UV, 0)] for _ in range(TB)], "dve")
    add("out", whole(U_OUT, KT), "act")
    add("xk", whole(U_XK, KT), "act")
    add("xq", whole(U_XQ, KT), "act")
    add("xo", whole(U_XO, KT), "act")
    add("down", [[(U_DOWN + (m * FT + k) // KT, (m * FT + k) % KT * P) for k in range(FT)] for m in range(KT)], "act")
    return plan, uses


PLAN, USES = tile_plan()


def ends_unit(use):
    unit = USES[use][0][-1][0]
    return all(sub[0][0] > unit for sub, _ in USES[use + 1:]) if use + 1 < len(USES) else True


def tiles_done(use):
    return sum(not ends_unit(u) for u in range(use + 1))


def emptied(use):
    engine = USES[use][1]
    return engine, sum(e == engine for _, e in USES[:use + 1])


NORMS = [("mix_pre", KT), ("q", 2), ("kv", 1), ("mem", KT), ("mix_post", KT), ("x_pre", KT), ("x_post", KT),
         ("ffn_pre", KT), ("ffn_post", KT)]
NORM_AT = {name: i for i, (name, _) in enumerate(NORMS)}
POST = ("mix_post", "x_post", "ffn_post")


def squares_before(name):
    return sum(k for _, k in NORMS[:NORM_AT[name]])


def normed_before(name):
    return sum(k for n, k in NORMS[:NORM_AT[name]] if n not in POST)


def scaled_before(name):
    return sum(k for n, k in NORMS[:NORM_AT[name]] if n in POST)


def build(nc, x_in, mem_in, w_in, g_in, c_in, out):
    with ExitStack() as ctx:
        layer_sems = []

        def sb(name, shape, dt=F32, stack=ctx):
            return stack.enter_context(nc.sbuf_tensor(name, shape, dt))

        def sem(name):
            s = ctx.enter_context(nc.semaphore(name))
            layer_sems.append(s)
            return s

        x = sb("x", [P, KT, SEQ])
        consts = sb("consts", [P, N_CONST])
        eps = sb("eps", [P, 1])
        one = sb("one", [P, 1])
        gains = sb("gains", [P, N_GAINS])
        raw = sb("raw", [P, RING, UNIT])
        w_hi = sb("w_hi", [P, RING, UNIT], F32R)
        w_lo = sb("w_lo", [P, RING, UNIT], F32R)
        with ExitStack() as late:
            y_f = sb("y_f", [P, KT, SEQ], F32, late)
        h_hi = sb("h_hi", [P, KT, SEQ], F32R)
        h_lo = sb("h_lo", [P, KT, SEQ], F32R)
        sq = sb("sq", [P, 2, SEQ])
        acc = sb("acc", [P, SEQ])
        rstd = sb("rstd", [P, SEQ])
        stat = sb("stat", [P, 3, 64])
        acol = sb("acol", [P, TB, ML_HEADS])

        with ExitStack() as room:
            q_mla = sb("q_mla", [P, MLA_HEADS, SEQ], F32, room)
            with ExitStack() as early:
                ml_qk = sb("ml_qk", [P, 4, SEQ], F32, early)
                ml_v = sb("ml_v", [P, TB, ML_HEADS, 2, ML_DK], F32, early)
                gate = sb("gate", [P, 4, SEQ], F32, early)
            k_mla = sb("k_mla", [P, MLA_HEADS, SEQ], F32, room)
            v_mla = sb("v_mla", [P, TB, MLA_HEADS * MLA_V], F32, room)
            k_pe = sb("k_pe", [P, SEQ], F32, room)
            sw_qk = sb("sw_qk", [P, 4, SEQ], F32, room)
            sw_v = sb("sw_v", [P, TB, SW_HEADS * SW_HD], F32, room)
            o_gate = sb("o_gate", [P, 2, SEQ], F32, room)
            with ExitStack() as early:
                c_hi = sb("c_hi", [P, 3, SEQ], F32R, early)
                c_lo = sb("c_lo", [P, 3, SEQ], F32R, early)
                conv_in = sb("conv_in", [P, 2, SEQ + 4], F32, early)
                w_ml = sb("w_ml", [P, 2, SEQ], F32, early)
            p_mix = sb("p_mix", [P, 3, SEQ], F32, room)
            pt_mix = sb("pt_mix", [P, 2, TB, SEQ], F32, room)
        with ExitStack() as room:
            y_x = sb("y_x", [P, KT, SEQ], F32, room)
            mem = sb("mem", [P, KT, N_MEM], F32, room)
            m_hi = sb("m_hi", [P, KT, N_MEM], F32R, room)
            m_lo = sb("m_lo", [P, KT, N_MEM], F32R, room)
            q_x = sb("q_x", [P, KT, SEQ], F32, room)
            k_x = sb("k_x", [P, KT, N_MEM], F32, room)
            v_x = sb("v_x", [P, 2, D_MODEL], F32, room)
            p_x = sb("p_x", [P, 3, SEQ], F32, room)
            pt_x = sb("pt_x", [P, 2, 2, SEQ], F32, room)
        with ExitStack() as room:
            a_hi = sb("a_hi", [P, FT * SEQ], F32R, room)
            a_lo = sb("a_lo", [P, FT * SEQ], F32R, room)
        f_e, f_a = [acc, rstd], sq

        bank = [ctx.enter_context(nc.psum_tensor(f"bank{i}", [P, SEQ], F32)) for i in range(8)]
        dense = bank[0:2]
        wide = bank[2:6]
        scores, turned = bank[2:4], bank[4:6]
        outs = bank[6:8]
        norm_bank = bank[7]
        rot_bank = [wide[0], outs[0]]
        ff_bank = bank[0:4]

        fixed_loaded = ctx.enter_context(nc.semaphore("fixed_loaded"))
        fixed_set = ctx.enter_context(nc.semaphore("fixed_set"))
        stored = ctx.enter_context(nc.semaphore("stored"))
        raw_loaded = [sem(f"raw_loaded{i}") for i in range(RING)]
        gains_loaded, mem_loaded = sem("gains_loaded"), sem("mem_loaded")
        split_hi, split_lo = sem("split_hi"), sem("split_lo")
        unit_used, tile_done = sem("unit_used"), sem("tile_done")
        emptied_act, emptied_dve = sem("emptied_act"), sem("emptied_dve")
        squared, squares_added = sem("squared"), sem("squares_added")
        norm_summed, ln_done, rstd_ready = sem("norm_summed"), sem("ln_done"), sem("rstd_ready")
        normed, normed_hi, normed_lo = sem("normed"), sem("normed_hi"), sem("normed_lo")
        y_scaled, x_updated = sem("y_scaled"), sem("x_updated")
        dve_step, act_step = sem("dve_step"), sem("act_step")
        pads_set = sem("pads_set")
        conv_done, conv_exp, ml_qk_ready = sem("conv_done"), sem("conv_exp"), sem("ml_qk_ready")
        gate_biased, gate_log, gate_rows = sem("gate_biased"), sem("gate_log"), sem("gate_rows")
        acol_turned, acol_ready = sem("acol_turned"), sem("acol_ready")
        k_pe_ready, k_pe_spread = sem("k_pe_ready"), sem("k_pe_spread")
        rotated, rot_read, roped = sem("rotated"), sem("rot_read"), sem("roped")
        o_ready, v_ready = sem("o_ready"), sem("v_ready")
        spread, ml_scored, ml_weight, ml_exp, ml_prob, ml_num = (
            sem("spread"), sem("ml_scored"), sem("ml_weight"), sem("ml_exp"), sem("ml_prob"), sem("ml_num"))
        ml_floor, ml_abs, ml_out, ml_hi, ml_lo = (
            sem("ml_floor"), sem("ml_abs"), sem("ml_out"), sem("ml_hi"), sem("ml_lo"))
        mix_at, x_at = ({n: sem(f"{c}_{n}") for n in ("scored", "masked", "exped", "probs", "turned", "copied",
                                                      "out", "out_hi", "out_lo")} for c in ("mix", "x"))
        xv_ready = sem("xv_ready")
        ff_exp, ff_step, ff_a, ff_hi, ff_lo = sem("ff_exp"), sem("ff_step"), sem("ff_a"), sem("ff_hi"), sem("ff_lo")

        def const(col, n=P, rows=slice(0, P)):
            return consts[rows, col:col + n]

        def gain(col, rows=slice(0, P)):
            return gains[rows, col:col + 1]

        def use_of(name, m):
            return PLAN[name][m][0]

        def wait_tile(eng, use):
            if ends_unit(use):
                eng.wait_ge(unit_used, USES[use][0][-1][0] + 1)
            else:
                eng.wait_ge(tile_done, tiles_done(use))

        def wait_emptied(eng, use):
            engine, count = emptied(use)
            eng.wait_ge(emptied_act if engine == "act" else emptied_dve, count)

        def counter(eng):
            counts = {}

            def done(ins, s):
                counts[s.name] = counts.get(s.name, 0) + 1
                ins.then_inc(s, 1)
                eng.wait_ge(s, counts[s.name])
            return done

        MIX_HEADS = MLA_HEADS + SW_HEADS

        def mix_head(n):
            if n < MLA_HEADS:
                return dict(q=q_mla[:, n, :], k=k_mla[:, n, :], v=lambda kb: v_mla[:, kb, n * MLA_V:(n + 1) * MLA_V],
                            mask=C_CAUSAL, scale=(MLA_NOPE + MLA_ROPE) ** -0.5, tile=n // 2, row=64 * (n % 2))
            h = n - MLA_HEADS
            r = slice(64 * (h % 2), 64 * (h % 2) + 64)
            return dict(q=sw_qk[r, h // 2, :], k=sw_qk[r, 2 + h // 2, :],
                        v=lambda kb: sw_v[:, kb, h * SW_HD:(h + 1) * SW_HD],
                        mask=C_DILATED, scale=SW_HD ** -0.5, tile=6 + h // 2, row=64 * (h % 2))

        def causal_len(qb):
            return (qb + 1) * P

        with nc.Block() as block:
            @block.sync
            def _(sp):
                sp.dma_start(x[:, :, :], x_in).then_inc(fixed_loaded, 16)
                sp.dma_start(consts[:, :], c_in).then_inc(fixed_loaded, 16)
                sp.wait_ge(fixed_loaded, 32)

            @block.vector
            def _(dve):
                dve.memset(eps[:, :], EPS).then_inc(fixed_set, 1)
                dve.memset(one[:, :], 1.0).then_inc(fixed_set, 1)
                dve.wait_ge(fixed_set, 2)

        with nc.Fori(0, DEPTH) as layer:
            with nc.Block() as block:

                @block.sync
                def _(sp):
                    sp.dma_start(gains[:, :], g_in[layer, :, :]).then_inc(gains_loaded, 16)
                    for s in range(RING):
                        sp.dma_start(raw[:, s, :], w_in[layer, s, :, :]).then_inc(raw_loaded[s], 16)

                    def stream(a, b):
                        with sp.Fori(a // RING, b // RING) as j:
                            for s in range(RING):
                                sp.wait_ge(split_lo, j * RING + (s + 1 - RING))
                                sp.dma_start(raw[:, s, :], w_in[layer, j * RING + s, :, :])\
                                  .then_inc(raw_loaded[s], 16)
                    mid = -(-U_OUT // RING) * RING + RING
                    stream(RING, mid)
                    sp.wait_ge(mix_at["out_lo"], MIX_HEADS)
                    sp.dma_start(mem[:, :, :], mem_in).then_inc(mem_loaded, 16)
                    stream(mid, N_UNITS)

                @block.gpsimd
                def _(pool):
                    with pool.Fori(0, N_UNITS // RING) as j:
                        for s in range(RING):
                            pool.wait_ge(split_hi, j * RING + (s + 1))
                            pool.tensor_tensor(w_lo[:, s, :], raw[:, s, :], w_hi[:, s, :].bitcast(F32),
                                               ALU.subtract).then_inc(split_lo, 1)

                @block.tensor
                def _(pe):
                    def three(out_ap, l_hi, l_lo, r_hi, r_lo, start, stop):
                        pe.matmul(out_ap, l_hi, r_hi, start=start, stop=False)
                        pe.matmul(out_ap, l_hi, r_lo, start=False, stop=False)
                        return pe.matmul(out_ap, l_lo, r_hi, start=False, stop=stop)

                    def project(name, m, act_hi, act_lo, width=SEQ, before=None):
                        use, subs = PLAN[name][m]
                        bank_ap = dense[use % 2][:, 0:width]
                        if use >= 2:
                            wait_emptied(pe, use - 2)
                        unit = None
                        for k, (u, col) in enumerate(subs):
                            if before is not None:
                                before(k)
                            if u != unit:
                                pe.wait_ge(split_lo, u + 1)
                                unit = u
                            w = slice(col, col + P)
                            mm = three(bank_ap, w_hi[:, u % RING, w], w_lo[:, u % RING, w], act_hi(k), act_lo(k),
                                       k == 0, k == len(subs) - 1)
                            if k + 1 < len(subs) and subs[k + 1][0] != u:
                                mm.then_inc(unit_used, 1)
                        mm.then_inc(unit_used if ends_unit(use) else tile_done, 1)

                    def project_tokens(u0, banks, act_hi, act_lo):
                        for j in range(4):
                            s = (u0 + j) % RING
                            pe.wait_ge(split_lo, u0 + j + 1)
                            for i in range(2):
                                k, w = 2 * j + i, slice(i * SEQ, (i + 1) * SEQ)
                                for b, bank_t in enumerate(banks):
                                    mm = three(bank_t[:, :], act_hi(k, b), act_lo(k, b), w_hi[:, s, w],
                                               w_lo[:, s, w], k == 0, k == KT - 1)
                            mm.then_inc(unit_used, 1)

                    def norm_sum(name, width=SEQ):
                        i = NORM_AT[name]
                        pe.wait_ge(squares_added, squares_before(name) + NORMS[i][1])
                        if i >= 1:
                            pe.wait_ge(ln_done, i)
                        pe.matmul(norm_bank[:, 0:width], const(C_ONES), acc[:, 0:width], start=True, stop=True)\
                          .then_inc(norm_summed, 1)

                    def after_norm(name):
                        return lambda k: pe.wait_ge(normed_lo, normed_before(name) + k + 1)

                    def tiles(t):
                        return lambda k: t[:, k, :]

                    norm_sum("mix_pre")
                    for m in range(IN_FM):
                        project("in", m, tiles(h_hi), tiles(h_lo), before=after_norm("mix_pre") if m == 0 else None)
                        if m == MISC + 1:
                            norm_sum("q")
                        if m == MISC + 3:
                            norm_sum("kv")
                        if SWQK + 1 <= m <= SWQK + 4:
                            j = m - SWQK - 1
                            pe.wait_ge(emptied_act, SWQK + j + 1)
                            if j >= 2:
                                pe.wait_ge(rot_read, j - 1)
                            pe.matmul(rot_bank[j % 2][:, :], const(C_ROT), sw_qk[:, j, :], start=True, stop=True)\
                              .then_inc(rotated, 1)
                    pe.wait_ge(rot_read, 4)
                    project_tokens(U_INV, wide, lambda k, b: h_hi[:, k, b * P:(b + 1) * P],
                                   lambda k, b: h_lo[:, k, b * P:(b + 1) * P])

                    for h in range(MLA_HEADS):
                        project("uq", h, tiles(c_hi), tiles(c_lo), before=after_norm("q") if h == 0 else None)
                    g4 = slice(0, ML_HEADS)
                    pe.wait_ge(gate_rows, 3)
                    pe.wait_ge(v_ready, TB)
                    for kb in range(TB):
                        mm = pe.matmul(outs[0][:, 4 * kb:4 * kb + 4], gate[g4, 0, kb * P:(kb + 1) * P],
                                       const(C_IDENT, 4, g4), start=True, stop=True)
                    mm.then_inc(acol_turned, 1)
                    pe.wait_ge(acol_ready, 1)
                    pe.wait_ge(ln_done, 3)
                    pe.wait_ge(ml_qk_ready, 4)
                    units = [(h, kb) for h in range(ML_HEADS) for kb in range(TB)]

                    def ml_scores(u):
                        h, kb = units[u]
                        r = slice(64 * (h % 2), 64 * (h % 2) + 64)
                        if kb == 0:
                            if h:
                                pe.wait_ge(ml_weight, TB * h)
                                pe.wait_ge(ml_floor, h)
                            sel = const(C_IDENT + h, 1, g4).broadcast_to([ML_HEADS, P])
                            pe.matmul(outs[0][:, :], sel, gate[g4, 1, :], start=True, stop=True)
                            pe.matmul(outs[1][:, :], sel, gate[g4, 2, :], start=True, stop=True)\
                              .then_inc(spread, 1)
                        if u >= 2:
                            pe.wait_ge(ml_prob, u - 1)
                        pe.matmul(scores[u % 2][:, 0:SEQ - kb * P], ml_qk[r, 2 + h // 2, kb * P:(kb + 1) * P],
                                  ml_qk[r, h // 2, kb * P:SEQ], start=True, stop=True).then_inc(ml_scored, 1)

                    def ml_numerator(u):
                        h, kb = units[u]
                        pe.wait_ge(ml_prob, u + 1)
                        if kb == 0 and h >= 2:
                            pe.wait_ge(ml_out, h - 1)
                        pe.matmul(turned[h % 2][:, kb * P:SEQ], ml_v[:, kb, h, :, :].rearrange("p a d -> p (a d)"),
                                  w_ml[:, u % 2, 0:SEQ - kb * P], start=(kb == 0), stop=(kb == TB - 1))\
                          .then_inc(ml_num, 1)

                    for u in range(len(units) + 1):
                        if u < len(units):
                            ml_scores(u)
                        if u >= 1:
                            ml_numerator(u - 1)

                    for m in range(4):
                        project("uk", m, lambda k: c_hi[:, 2, :], lambda k: c_lo[:, 2, :],
                                before=after_norm("kv") if m == 0 else None)
                    pe.wait_ge(split_lo, U_UV + 1)
                    for b in range(TB):
                        use, s, t = use_of("uv", b), U_UV % RING, slice(b * P, (b + 1) * P)
                        wait_emptied(pe, use - 2)
                        mm = three(dense[use % 2][:, :], c_hi[:, 2, t], c_lo[:, 2, t], w_hi[:, s, 0:SEQ],
                                   w_lo[:, s, 0:SEQ], True, True)
                        mm.then_inc(unit_used if ends_unit(use) else tile_done, 1)

                    def attention(a, heads, probs, klen, emit_scores, emit_out):
                        n_units = heads * TB
                        for u in range(n_units + 4):
                            if u < n_units:
                                if u >= 2:
                                    pe.wait_ge(a["masked"], u - 1)
                                emit_scores(u // TB, u % TB, scores[u % 2]).then_inc(a["scored"], 1)
                            v = u - 2
                            if 0 <= v < n_units:
                                pe.wait_ge(a["probs"], v + 1)
                                if v >= 2:
                                    pe.wait_ge(a["copied"], v - 1)
                                for kb in range(klen(v % TB) // P):
                                    mm = pe.transpose(turned[v % 2][:, kb * P:(kb + 1) * P],
                                                      probs[:, v % 3, kb * P:(kb + 1) * P], const(C_IDENT))
                                mm.then_inc(a["turned"], 1)
                            w = u - 4
                            if w >= 0 and w % TB == TB - 1:
                                pe.wait_ge(a["copied"], w + 1)
                                emit_out(w // TB)

                    def mix_scores(head, qb, bank_t):
                        hd = mix_head(head)
                        if head == 0 and qb == 0:
                            wait_emptied(pe, use_of("uq", MLA_HEADS - 1))
                            wait_emptied(pe, use_of("uk", 3))
                            wait_emptied(pe, use_of("uv", TB - 1))
                            pe.wait_ge(k_pe_spread, 2)
                            pe.wait_ge(roped, 4)
                            pe.wait_ge(ml_out, ML_HEADS)
                        n = causal_len(qb)
                        return pe.matmul(bank_t[:, 0:n], hd["q"][:, qb * P:n], hd["k"][:, 0:n], start=True, stop=True)

                    def mix_out(head):
                        if head >= 2:
                            pe.wait_ge(mix_at["out_lo"], head - 1)
                        for kb in range(TB):
                            mm = pe.matmul(outs[head % 2][0:64, kb * P:SEQ], mix_head(head)["v"](kb),
                                           pt_mix[:, head % 2, kb, kb * P:SEQ], start=(kb == 0), stop=(kb == TB - 1))
                        mm.then_inc(mix_at["out"], 1)

                    attention(mix_at, MIX_HEADS, p_mix, causal_len, mix_scores, mix_out)

                    pe.wait_ge(mix_at["out_lo"], MIX_HEADS)
                    pe.wait_ge(ml_lo, 2)
                    for m in range(KT):
                        project("out", m, tiles(h_hi), tiles(h_lo))
                        if m == 1:
                            norm_sum("mem", N_MEM)
                    norm_sum("mix_post")
                    for m in range(KT):
                        project("xk", m, tiles(m_hi), tiles(m_lo), N_MEM, before=after_norm("mem") if m == 0 else None)
                    for half in range(2):
                        project_tokens(U_XV + 4 * half, wide[2 * half:2 * half + 2],
                                       lambda k, b: m_hi[:, k, b * P:(b + 1) * P],
                                       lambda k, b: m_lo[:, k, b * P:(b + 1) * P])
                        if half == 0:
                            norm_sum("x_pre")
                    for m in range(KT):
                        project("xq", m, tiles(h_hi), tiles(h_lo), before=after_norm("x_pre") if m == 0 else None)

                    def x_scores(head, qb, bank_t):
                        if head == 0 and qb == 0:
                            wait_emptied(pe, use_of("xq", KT - 1))
                            pe.wait_ge(xv_ready, 4)
                        for c in range(2):
                            mm = pe.matmul(bank_t[:, 0:N_MEM], q_x[:, 2 * head + c, qb * P:(qb + 1) * P],
                                           k_x[:, 2 * head + c, :], start=(c == 0), stop=(c == 1))
                        return mm

                    def x_out(head):
                        for c in range(2):
                            if head >= 1:
                                pe.wait_ge(x_at["out_lo"], 2 * head - 1 + c)
                            for kb in range(2):
                                col = head * X_HD + c * P
                                mm = pe.matmul(outs[c][:, :], v_x[:, kb, col:col + P], pt_x[:, head % 2, kb, :],
                                               start=(kb == 0), stop=(kb == 1))
                            mm.then_inc(x_at["out"], 1)

                    attention(x_at, X_HEADS, p_x, lambda qb: N_MEM, x_scores, x_out)
                    pe.wait_ge(x_at["out_lo"], KT)
                    for m in range(KT):
                        project("xo", m, tiles(h_hi), tiles(h_lo))
                    norm_sum("x_post")
                    norm_sum("ffn_pre")

                    def gate_up(j, first_turn):
                        for i in range(4):
                            s = (U_FF + i) % RING
                            if not first_turn and i % 2 == 0:
                                pe.wait_ge(ff_a, j * 2 + (i // 2 - 1))
                            pe.wait_ge(split_lo, j * 4 + (U_FF + i + 1))
                            for k in range(KT):
                                if first_turn and i == 0:
                                    after_norm("ffn_pre")(k)
                                w = slice(k * P, (k + 1) * P)
                                mm = three(ff_bank[i][:, :], w_hi[:, s, w], w_lo[:, s, w], h_hi[:, k, :],
                                           h_lo[:, k, :], k == 0, k == KT - 1)
                            mm.then_inc(unit_used, 1)

                    wait_emptied(pe, use_of("xo", KT - 1))
                    gate_up(0, True)
                    with pe.Fori(1, FT // 2) as j:
                        gate_up(j, False)

                    pe.wait_ge(ff_lo, FT)
                    for m in range(KT):
                        project("down", m, lambda k: a_hi[:, k * SEQ:(k + 1) * SEQ],
                                lambda k: a_lo[:, k * SEQ:(k + 1) * SEQ])
                    norm_sum("ffn_post")

                @block.scalar
                def _(act):
                    done = counter(act)
                    act.preload_act_table_set("natural_log_exp_and_others")
                    made = [0]

                    def split_unit(n, j=0):
                        s = n % RING
                        act.wait_ge(raw_loaded[s], j * 16 + 16 * (n // RING + 1))
                        if n >= RING:
                            act.wait_ge(unit_used, j * RING + (n - RING + 1))
                        act.activation(w_hi[:, s, :], raw[:, s, :], ACT.Copy).then_inc(split_hi, 1)

                    def split_until(n):
                        while made[0] < min(n, N_UNITS):
                            split_unit(made[0])
                            made[0] += 1

                    def square(name, k, src, width=SEQ):
                        c = squares_before(name) + k
                        if c >= 2:
                            act.wait_ge(squares_added, c - 1)
                        if k == 0 and normed_before(name):
                            act.wait_ge(normed_lo, normed_before(name))
                        act.activation(sq[:, c % 2, 0:width], src, ACT.Square).then_inc(squared, 1)

                    def make_rstd(name, features, width=SEQ):
                        act.wait_ge(norm_summed, NORM_AT[name] + 1)
                        if normed_before(name):
                            act.wait_ge(normed, normed_before(name))
                        if scaled_before(name):
                            act.wait_ge(y_scaled, scaled_before(name))
                        done(act.activation(rstd[:, 0:width], norm_bank[:, 0:width], ACT.Ln, bias=eps[:, :],
                                            scale=1.0 / features), ln_done)
                        act.activation(rstd[:, 0:width], rstd[:, 0:width], ACT.Exp, scale=-0.5)\
                           .then_inc(rstd_ready, 1)

                    def norm_hi(name, k, dst, width=SEQ):
                        c = normed_before(name) + k
                        act.wait_ge(normed, c + 1)
                        act.activation(dst, sq[:, c % 2, 0:width], ACT.Copy).then_inc(normed_hi, 1)

                    def empty(name, m, dst, width=SEQ, func=ACT.Copy, scale=1.0):
                        use = use_of(name, m)
                        wait_tile(act, use)
                        done(act.activation(dst, dense[use % 2][:, 0:width], func, scale=scale), emptied_act)

                    for k in range(KT):
                        square("mix_pre", k, x[:, k, :])
                    split_until(2)
                    make_rstd("mix_pre", D_MODEL)
                    split_until(3)
                    for k in range(KT):
                        norm_hi("mix_pre", k, h_hi[:, k, :])

                    g4 = slice(0, ML_HEADS)
                    for m in range(IN_FM):
                        split_until(m + 4)
                        if m < MLQK:
                            empty("in", m, q_mla[:, m, :])
                        elif m < SWQK:
                            j = m - MLQK
                            if j == 0:
                                act.wait_ge(pads_set, 2)
                            if j >= 2:
                                act.wait_ge(ml_qk_ready, j - 1)
                            empty("in", m, conv_in[:, j % 2, 3:3 + SEQ])
                        elif m < OG:
                            empty("in", m, sw_qk[:, m - SWQK, :])
                        else:
                            empty("in", m, o_gate[:, m - OG, :], func=ACT.Exp, scale=-1.0)
                        if m == MISC:
                            for k in range(2):
                                square("q", k, q_mla[:, CQ + k, :])
                        if m == MISC + 1:
                            make_rstd("q", MLA_Q_LORA)
                            for k in range(2):
                                norm_hi("q", k, c_hi[:, k, :])
                            square("kv", 0, q_mla[:, CKV, :])
                        if m == MISC + 2:
                            act.wait_ge(gate_biased, 2)
                            done(act.activation(gate[g4, 3, :], gate[g4, 1, :], ACT.Abs), gate_log)
                            done(act.activation(gate[g4, 3, :], gate[g4, 3, :], ACT.Exp, scale=-1.0), gate_log)
                            done(act.activation(gate[g4, 3, :], gate[g4, 3, :], ACT.Ln, bias=one[g4, :]), gate_log)
                        if MLQK + 1 <= m <= MLQK + 4:
                            j = m - MLQK - 1
                            act.wait_ge(conv_done, j + 1)
                            act.activation(conv_in[:, j % 2, 3:3 + SEQ], ml_qk[:, j, :], ACT.Exp, scale=-1.0)\
                               .then_inc(conv_exp, 1)
                        if m == MISC + 3:
                            make_rstd("kv", MLA_KV_LORA)
                            norm_hi("kv", 0, c_hi[:, 2, :])
                    split_until(U_UK + 4)

                    ml_units = ML_HEADS * TB
                    for u in range(ml_units + 4):
                        h = u // TB
                        if u < ml_units:
                            n = SEQ - u % TB * P
                            act.wait_ge(ml_weight, u + 1)
                            act.activation(w_ml[:, u % 2, 0:n], w_ml[:, u % 2, 0:n], ACT.Exp).then_inc(ml_exp, 1)
                            if u % TB == TB - 1:
                                act.wait_ge(spread, h + 1)
                                if h:
                                    act.wait_ge(ml_out, h)
                                act.activation(conv_in[64:128, 0, 0:SEQ], outs[1][64:128, :], ACT.Exp)\
                                   .then_inc(ml_floor, 1)
                        if u >= TB and u % TB == 1:
                            act.wait_ge(ml_num, TB * h)
                            act.activation(conv_in[64:128, 1, 0:SEQ], turned[(h - 1) % 2][64:128, :], ACT.Abs)\
                               .then_inc(ml_abs, 1)
                        if u >= TB and u % TB == 3 and h % 2 == 0:
                            act.wait_ge(ml_out, h)
                            act.activation(h_hi[:, 3 + h // 2, :], o_gate[:, h // 2 - 1, :], ACT.Copy)\
                               .then_inc(ml_hi, 1)
                    for m in range(4):
                        use = use_of("uk", m)
                        wait_tile(act, use)
                        for i in range(2):
                            done(act.activation(k_mla[0:64, 2 * m + i, :], dense[use % 2][64 * i:64 * i + 64, :],
                                                ACT.Copy), emptied_act if i else act_step)
                    split_until(U_UV + 4)

                    def attention(a, heads, probs, probs_t, klen, banks, emit_hi):
                        n_units = heads * TB
                        for u in range(n_units + 4):
                            if u < n_units:
                                n = klen(u % TB)
                                act.wait_ge(a["masked"], u + 1)
                                act.activation(probs[:, u % 3, 0:n], probs[:, u % 3, 0:n], ACT.Exp, scale=-1.0,
                                               bias=stat[:, 0, u:u + 1], accum_out=stat[:, 1, u:u + 1])\
                                   .then_inc(a["exped"], 1)
                            v = u - 2
                            if 0 <= v < n_units:
                                head, qb, m = v // TB, v % TB, klen(v % TB) // P
                                act.wait_ge(a["turned"], v + 1)
                                if qb == 0 and head >= 2:
                                    act.wait_ge(a["out"], banks * (head - 1))
                                act.activation(probs_t[:, head % 2, 0:m, qb * P:(qb + 1) * P],
                                               turned[v % 2][:, 0:m * P].rearrange("p (b q) -> p b q", q=P),
                                               ACT.Copy).then_inc(a["copied"], 1)
                            w = u - 4
                            if w >= 0 and w % TB == TB - 1:
                                emit_hi(w // TB)

                    def mix_hi(head):
                        hd = mix_head(head)
                        act.wait_ge(mix_at["out"], head + 1)
                        act.activation(h_hi[hd["row"]:hd["row"] + 64, hd["tile"], :], outs[head % 2][0:64, :],
                                       ACT.Copy).then_inc(mix_at["out_hi"], 1)

                    attention(mix_at, MIX_HEADS, p_mix, pt_mix, causal_len, 1, mix_hi)

                    def post(name, plan, y):
                        for m in range(KT):
                            use = use_of(plan, m)
                            split_until(USES[use][0][-1][0] + 4)
                            wait_tile(act, use)
                            done(act.activation(y[:, m, :], dense[use % 2][:, :], ACT.Copy), emptied_act)
                            square(name, m, y[:, m, :])

                    split_until(U_OUT + 3)
                    act.wait_ge(mem_loaded, 16)
                    for k in range(KT):
                        square("mem", k, mem[:, k, :], N_MEM)
                    split_until(U_OUT + 5)
                    make_rstd("mem", D_MODEL, N_MEM)
                    for k in range(KT):
                        norm_hi("mem", k, m_hi[:, k, :], N_MEM)
                    post("mix_post", "out", y_x)
                    make_rstd("mix_post", D_MODEL)
                    for m in range(KT):
                        split_until(U_XK + m + 4)
                        empty("xk", m, k_x[:, m, :], width=N_MEM)
                    for k in range(KT):
                        act.wait_ge(x_updated, k + 1)
                        square("x_pre", k, x[:, k, :])
                    split_until(U_XV + 4 + 3)
                    make_rstd("x_pre", D_MODEL)
                    for k in range(KT):
                        norm_hi("x_pre", k, h_hi[:, k, :])
                    split_until(U_XQ + 3)
                    for m in range(KT):
                        split_until(U_XQ + m + 4)
                        empty("xq", m, q_x[:, m, :])

                    def x_hi(head):
                        for c in range(2):
                            act.wait_ge(x_at["out"], 2 * head + c + 1)
                            act.activation(h_hi[:, 2 * head + c, :], outs[c][:, :], ACT.Copy)\
                               .then_inc(x_at["out_hi"], 1)

                    attention(x_at, X_HEADS, p_x, pt_x, lambda qb: N_MEM, 2, x_hi)
                    post("x_post", "xo", y_x)
                    make_rstd("x_post", D_MODEL)
                    for k in range(KT):
                        act.wait_ge(x_updated, KT + k + 1)
                        square("ffn_pre", k, x[:, k, :])
                    make_rstd("ffn_pre", D_MODEL)
                    for k in range(KT):
                        norm_hi("ffn_pre", k, h_hi[:, k, :])
                    split_until(U_FF + 3)

                    def ff_turn(j, first_turn):
                        for i in range(2):
                            split_unit(U_FF + 3 + 2 * i, j)
                            act.wait_ge(unit_used, j * 4 + (U_FF + 2 * i + 1))
                            if not first_turn:
                                act.wait_ge(ff_a, j * 2 + (i - 1))
                            act.activation(f_e[i][:, :], ff_bank[2 * i][:, :], ACT.Exp, scale=-1.0)\
                               .then_inc(ff_exp, 1)
                            split_unit(U_FF + 4 + 2 * i, j)
                            act.wait_ge(ff_a, j * 2 + (i + 1))
                            act.activation(a_hi[:, bass.ds(j * (2 * SEQ) + i * SEQ, SEQ)], f_a[:, i, :], ACT.Copy)\
                               .then_inc(ff_hi, 1)

                    ff_turn(0, True)
                    with act.Fori(1, FT // 2) as j:
                        ff_turn(j, False)
                    made[0] = U_DOWN + 3
                    act.wait_ge(ff_lo, FT)
                    post("ffn_post", "down", y_f)
                    make_rstd("ffn_post", D_MODEL)

                @block.vector
                def _(dve):
                    done = counter(dve)

                    def add_squares(name, n, width=SEQ):
                        for k in range(n):
                            dve.wait_ge(squared, squares_before(name) + k + 1)
                            s = (squares_before(name) + k) % 2
                            if k == 0:
                                if NORM_AT[name]:
                                    dve.wait_ge(norm_summed, NORM_AT[name])
                                ins = dve.tensor_copy(acc[:, 0:width], sq[:, s, 0:width])
                            else:
                                ins = dve.tensor_tensor(acc[:, 0:width], acc[:, 0:width], sq[:, s, 0:width], ALU.add)
                            done(ins, squares_added)

                    def norm(name, n, src, col, dst_hi, dst_lo, width=SEQ):
                        c0 = normed_before(name)
                        dve.wait_ge(rstd_ready, NORM_AT[name] + 1)
                        for k in range(n + 1):
                            if k < n:
                                done(dve.scalar_tensor_tensor(out=sq[:, (c0 + k) % 2, 0:width], in0=src(k),
                                                              scalar=gain(col + k), in1=rstd[:, 0:width],
                                                              op0=ALU.mult, op1=ALU.mult), normed)
                            if k >= 1:
                                dve.wait_ge(normed_hi, c0 + k)
                                done(dve.tensor_tensor(dst_lo(k - 1), sq[:, (c0 + k - 1) % 2, 0:width],
                                                       dst_hi(k - 1).bitcast(F32), ALU.subtract), normed_lo)

                    def residual(name, plan, y, col):
                        dve.wait_ge(rstd_ready, NORM_AT[name] + 1)
                        wait_emptied(dve, use_of(plan, KT - 1))
                        for k in range(KT):
                            done(dve.scalar_tensor_tensor(out=y[:, k, :], in0=y[:, k, :], scalar=gain(col + k),
                                                          in1=rstd[:, :], op0=ALU.mult, op1=ALU.mult), y_scaled)
                            done(dve.tensor_tensor(x[:, k, :], x[:, k, :], y[:, k, :], ALU.add), x_updated)

                    def tiles(t):
                        return lambda k: t[:, k, :]

                    add_squares("mix_pre", KT)
                    done(dve.memset(ml_v[:, :, :, 1, :], 1.0), pads_set)
                    done(dve.memset(conv_in[:, :, 0:3], 0.0), pads_set)
                    dve.wait_ge(gains_loaded, 16)
                    norm("mix_pre", KT, tiles(x), G_MIX_PRE, tiles(h_hi), tiles(h_lo))

                    add_squares("q", 2)
                    dve.wait_ge(emptied_act, MISC + 1)
                    misc = q_mla[:, MISC, :]
                    g4, f4 = slice(ROW_I, ROW_I + ML_HEADS), slice(ROW_F, ROW_F + ML_HEADS)
                    done(dve.tensor_scalar(gate[g4, 0, :], misc[g4, :], gain(G_GATE_B, g4), None, ALU.add), gate_biased)
                    done(dve.tensor_scalar(gate[g4, 1, :], misc[f4, :], gain(G_GATE_B, f4), None, ALU.add), gate_biased)
                    r0, r1 = slice(ROW_R, ROW_R + MLA_ROPE), slice(ROW_RS, ROW_RS + MLA_ROPE)
                    done(dve.tensor_tensor(misc[r1, :], misc[r1, :], const(C_ROPE_Q, SEQ, r1), ALU.mult), dve_step)
                    done(dve.tensor_tensor(misc[r0, :], misc[r0, :], const(C_ROPE_Q, SEQ, r0), ALU.mult), dve_step)
                    done(dve.tensor_copy(w_ml[r0, 0, :], misc[r1, :]), dve_step)
                    done(dve.tensor_tensor(k_pe[r0, :], misc[r0, :], w_ml[r0, 0, :], ALU.add), dve_step)
                    norm("q", 2, tiles(q_mla), G_Q, tiles(c_hi), tiles(c_lo))

                    def convolve(j):
                        dve.wait_ge(emptied_act, MLQK + j + 1)
                        src, dst = conv_in[:, j % 2, :], ml_qk[:, j, :]
                        w = G_CONV_W + j * ML_CONV
                        done(dve.tensor_scalar(dst, src[:, 3:3 + SEQ], gain(w + 3), gain(G_CONV_B + j), ALU.mult,
                                               ALU.add), dve_step)
                        for tap in range(3):
                            done(dve.scalar_tensor_tensor(out=dst, in0=src[:, tap:tap + SEQ], scalar=gain(w + tap),
                                                          in1=dst, op0=ALU.mult, op1=ALU.add),
                                 conv_done if tap == 2 else dve_step)

                    def silu(j):
                        dve.wait_ge(conv_exp, j + 1)
                        e = conv_in[:, j % 2, 3:3 + SEQ]
                        done(dve.tensor_scalar(e, e, 1.0, None, ALU.add), dve_step)
                        done(dve.reciprocal(e, e), dve_step)
                        done(dve.tensor_tensor(ml_qk[:, j, :], ml_qk[:, j, :], e, ALU.mult), ml_qk_ready)

                    convolve(0)
                    add_squares("kv", 1)
                    convolve(1)
                    silu(0)
                    dve.wait_ge(gate_log, 3)
                    done(dve.tensor_scalar(gate[g4, 1, :], gate[g4, 1, :], 0.0, None, ALU.min), dve_step)
                    done(dve.tensor_tensor(gate[g4, 1, :], gate[g4, 1, :], gate[g4, 3, :], ALU.subtract), dve_step)
                    done(dve.tensor_tensor_scan(gate[g4, 2, :], const(C_ONE_ROWS, SEQ, g4), gate[g4, 1, :], 0.0,
                                                ALU.mult, ALU.add), dve_step)
                    done(dve.tensor_tensor(gate[g4, 0, :], gate[g4, 0, :], gate[g4, 2, :], ALU.subtract), gate_rows)
                    done(dve.tensor_tensor_scan(gate[g4, 3, :], gate[g4, 0, :], gate[g4, 0, :], NEG,
                                                ALU.max, ALU.max), dve_step)
                    done(dve.tensor_scalar(gate[g4, 1, :], gate[g4, 3, :], -1.0, None, ALU.mult), gate_rows)
                    done(dve.tensor_tensor(gate[g4, 2, :], gate[g4, 1, :], gate[g4, 2, :], ALU.subtract), gate_rows)
                    convolve(2)
                    silu(1)
                    norm("kv", 1, lambda k: q_mla[:, CKV, :], G_KV, lambda k: c_hi[:, 2, :], lambda k: c_lo[:, 2, :])
                    convolve(3)
                    silu(2)
                    silu(3)

                    for j in range(4):
                        dve.wait_ge(rotated, j + 1)
                        done(dve.tensor_tensor(w_ml[:, j % 2, :], rot_bank[j % 2][:, :], const(C_SW_SIN, SEQ),
                                               ALU.mult), rot_read)
                        done(dve.tensor_tensor(sw_qk[:, j, :], sw_qk[:, j, :], const(C_SW_COS, SEQ), ALU.mult),
                             dve_step)
                        done(dve.tensor_tensor(sw_qk[:, j, :], sw_qk[:, j, :], w_ml[:, j % 2, :], ALU.add), roped)
                    for j in range(2):
                        dve.wait_ge(emptied_act, OG + j + 1)
                        done(dve.tensor_scalar(o_gate[:, j, :], o_gate[:, j, :], 1.0, None, ALU.add), dve_step)
                        done(dve.reciprocal(o_gate[:, j, :], o_gate[:, j, :]), o_ready)
                    dve.wait_ge(unit_used, U_INV + 4)
                    for b in range(TB):
                        half = ML_HEADS * ML_DK
                        done(dve.tensor_copy(ml_v[:, b, :, 0, :],
                                             wide[b][:, 0:half].rearrange("p (h d) -> p h d", h=ML_HEADS)), dve_step)
                        done(dve.tensor_copy(sw_v[:, b, :], wide[b][:, half:SEQ]), v_ready)
                    for h in range(MLA_HEADS):
                        use = use_of("uq", h)
                        wait_tile(dve, use)
                        done(dve.tensor_tensor(q_mla[:, h, :], dense[use % 2][:, :], const(C_ROPE_Q, SEQ), ALU.mult),
                             emptied_dve)

                    dve.wait_ge(acol_turned, 1)
                    done(dve.tensor_copy(acol[:, :, :], outs[0][:, 0:TB * ML_HEADS]
                                         .rearrange("p (b h) -> p b h", h=ML_HEADS)), acol_ready)
                    ml_units = ML_HEADS * TB

                    def ml_finish(h):
                        r = slice(64 * (h % 2), 64 * (h % 2) + 64)
                        dve.wait_ge(ml_floor, h + 1)
                        dve.wait_ge(ml_abs, h + 1)
                        den = conv_in[64:128, 1, 0:SEQ]
                        done(dve.tensor_tensor(den, den, conv_in[64:128, 0, 0:SEQ], ALU.max), dve_step)
                        done(dve.reciprocal(conv_in[0:64, 1, 0:SEQ], den), dve_step)
                        done(dve.tensor_tensor(sq[r, 0, :], turned[h % 2][0:64, :], conv_in[0:64, 1, 0:SEQ],
                                               ALU.mult), dve_step)
                        done(dve.tensor_tensor(o_gate[r, h // 2, :], o_gate[r, h // 2, :], sq[r, 0, :], ALU.mult),
                             ml_out)

                    for u in range(ml_units + 5):
                        if u < ml_units:
                            h, kb, n = u // TB, u % TB, SEQ - u % TB * P
                            if kb == 0:
                                dve.wait_ge(spread, h + 1)
                            if u >= 2:
                                dve.wait_ge(ml_num, u - 1)
                            done(dve.scalar_tensor_tensor(out=w_ml[:, u % 2, 0:n], in0=outs[0][:, kb * P:SEQ],
                                                          scalar=acol[:, kb, h:h + 1], in1=const(C_CAUSAL_T, n),
                                                          op0=ALU.add, op1=ALU.add), ml_weight)
                        if 1 <= u <= ml_units:
                            v, n = u - 1, SEQ - (u - 1) % TB * P
                            dve.wait_ge(ml_exp, v + 1)
                            dve.wait_ge(ml_scored, v + 1)
                            done(dve.scalar_tensor_tensor(out=w_ml[:, v % 2, 0:n], in0=scores[v % 2][:, 0:n],
                                                          scalar=ML_DK ** -0.5, in1=w_ml[:, v % 2, 0:n],
                                                          op0=ALU.mult, op1=ALU.mult), ml_prob)
                        if TB <= u <= ml_units + 1 and u % TB == 1:
                            ml_finish(u // TB - 1)
                        if u in (2 * TB + 4, ml_units + 4):
                            t = u // (2 * TB) - 1
                            dve.wait_ge(ml_hi, t + 1)
                            done(dve.tensor_tensor(h_lo[:, 4 + t, :], o_gate[:, t, :],
                                                   h_hi[:, 4 + t, :].bitcast(F32), ALU.subtract), ml_lo)

                    k_pe_rows = k_pe[r0, :].unsqueeze(1)
                    for rows in (r0, r1):
                        done(dve.tensor_copy(k_mla[rows, :, :],
                                             k_pe_rows.broadcast_to([MLA_ROPE, MLA_HEADS, SEQ])), k_pe_spread)
                    for b in range(TB):
                        use = use_of("uv", b)
                        wait_tile(dve, use)
                        done(dve.tensor_copy(v_mla[:, b, :], dense[use % 2][:, :]), emptied_dve)

                    def attention(a, heads, probs, klen, mask, scale, emit_lo):
                        n_units = heads * TB
                        for u in range(n_units + 4):
                            if u < n_units:
                                n = klen(u % TB)
                                dve.wait_ge(a["scored"], u + 1)
                                if u >= 3:
                                    dve.wait_ge(a["turned"], u - 2)
                                done(dve.tensor_tensor_reduce(
                                    probs[:, u % 3, 0:n], scores[u % 2][:, 0:n],
                                    const(mask(u // TB) + SEQ - n, n), -scale(u // TB), 3e38, ALU.add, ALU.min,
                                    stat[:, 0, u:u + 1]), a["masked"])
                            v = u - 1
                            if 0 <= v < n_units:
                                n = klen(v % TB)
                                dve.wait_ge(a["exped"], v + 1)
                                done(dve.reciprocal(stat[:, 2, v:v + 1], stat[:, 1, v:v + 1]), dve_step)
                                done(dve.tensor_scalar(probs[:, v % 3, 0:n], probs[:, v % 3, 0:n],
                                                       stat[:, 2, v:v + 1], None, ALU.mult), a["probs"])
                            w = u - 4
                            if w >= 0 and w % TB == TB - 1:
                                emit_lo(w // TB)

                    def mix_lo(head):
                        hd = mix_head(head)
                        r = slice(hd["row"], hd["row"] + 64)
                        dve.wait_ge(mix_at["out_hi"], head + 1)
                        done(dve.tensor_tensor(h_lo[r, hd["tile"], :], outs[head % 2][0:64, :],
                                               h_hi[r, hd["tile"], :].bitcast(F32), ALU.subtract), mix_at["out_lo"])

                    attention(mix_at, MIX_HEADS, p_mix, causal_len, lambda h: mix_head(h)["mask"],
                              lambda h: mix_head(h)["scale"], mix_lo)

                    add_squares("mem", KT, N_MEM)
                    norm("mem", KT, tiles(mem), G_MEM, tiles(m_hi), tiles(m_lo), N_MEM)
                    add_squares("mix_post", KT)
                    residual("mix_post", "out", y_x, G_MIX_POST)
                    add_squares("x_pre", KT)
                    norm("x_pre", KT, tiles(x), G_X_PRE, tiles(h_hi), tiles(h_lo))
                    for half in range(2):
                        dve.wait_ge(unit_used, U_XV + 4 * half + 4)
                        for b in range(2):
                            done(dve.tensor_copy(v_x[:, b, half * SEQ:(half + 1) * SEQ], wide[2 * half + b][:, :]),
                                 xv_ready)

                    def x_lo(head):
                        for c in range(2):
                            dve.wait_ge(x_at["out_hi"], 2 * head + c + 1)
                            done(dve.tensor_tensor(h_lo[:, 2 * head + c, :], outs[c][:, :],
                                                   h_hi[:, 2 * head + c, :].bitcast(F32), ALU.subtract),
                                 x_at["out_lo"])

                    attention(x_at, X_HEADS, p_x, lambda qb: N_MEM, lambda h: C_CAUSAL - (SEQ - N_MEM),
                              lambda h: X_HD ** -0.5, x_lo)
                    add_squares("x_post", KT)
                    residual("x_post", "xo", y_x, G_X_POST)
                    add_squares("ffn_pre", KT)
                    norm("ffn_pre", KT, tiles(x), G_FFN_PRE, tiles(h_hi), tiles(h_lo))

                    def ff_turn(j):
                        for i in range(2):
                            e, n = f_e[i][:, :], 3 * i

                            def step(ins, k):
                                ins.then_inc(ff_step, 1)
                                dve.wait_ge(ff_step, j * 6 + (n + k))

                            dve.wait_ge(ff_exp, j * 2 + (i + 1))
                            step(dve.tensor_scalar(e, e, 1.0, None, ALU.add), 1)
                            step(dve.reciprocal(e, e), 2)
                            step(dve.tensor_tensor(e, ff_bank[2 * i][:, :], e, ALU.mult), 3)
                            dve.wait_ge(unit_used, j * 4 + (U_FF + 2 * i + 2))
                            dve.tensor_tensor(f_a[:, i, :], ff_bank[2 * i + 1][:, :], e, ALU.mult).then_inc(ff_a, 1)
                            dve.wait_ge(ff_hi, j * 2 + (i + 1))
                            at = bass.ds(j * (2 * SEQ) + i * SEQ, SEQ)
                            dve.tensor_tensor(a_lo[:, at], f_a[:, i, :], a_hi[:, at].bitcast(F32), ALU.subtract)\
                               .then_inc(ff_lo, 1)
                            dve.wait_ge(ff_lo, j * 2 + (i + 1))

                    ff_turn(0)
                    with dve.Fori(1, FT // 2) as j:
                        ff_turn(j)
                    add_squares("ffn_post", KT)
                    residual("ffn_post", "down", y_f, G_FFN_POST)

            with nc.Block() as block:
                @block.sync
                def _(sp):
                    for s in layer_sems:
                        sp.sem_clear(s)

        with nc.Block() as block:
            @block.sync
            def _(sp):
                sp.dma_start(out, x[:, :, :]).then_inc(stored, 16)
                sp.wait_ge(stored, 16)


def constants():
    c = np.zeros((P, N_CONST), np.float32)

    def tables(d):
        inv = np.float32(ROPE_THETA) ** (-np.arange(0, d, 2, dtype=np.float32) / np.float32(d))
        ang = inv.astype(np.float32)[:, None] * np.arange(SEQ, dtype=np.float32)[None, :]
        cos, sin = np.cos(ang).astype(np.float32), np.sin(ang).astype(np.float32)
        return np.concatenate([cos, cos]), np.concatenate([-sin, sin])

    cos, sin = tables(MLA_ROPE)
    c[0:MLA_NOPE, C_ROPE_Q:C_ROPE_Q + SEQ] = 1.0
    c[ROW_R:ROW_R + MLA_ROPE, C_ROPE_Q:C_ROPE_Q + SEQ] = cos
    c[ROW_RS:ROW_RS + MLA_ROPE, C_ROPE_Q:C_ROPE_Q + SEQ] = sin
    cos, sin = tables(SW_ROT)
    c[:, C_SW_COS:C_SW_COS + SEQ] = 1.0
    for r in (0, SW_HD):
        c[r:r + SW_ROT, C_SW_COS:C_SW_COS + SEQ] = cos
        c[r:r + SW_ROT, C_SW_SIN:C_SW_SIN + SEQ] = sin
        for i in range(SW_ROT):
            c[r + (i + SW_ROT // 2) % SW_ROT, C_ROT + r + i] = 1.0
    t, s = np.arange(P)[:, None] + SEQ - P, np.arange(SEQ)[None, :]
    d = t - s
    c[:, C_CAUSAL:C_CAUSAL + SEQ] = np.where(d >= 0, 0.0, NEG)
    count = sum(((d >= 0) & (d % dil == 0) & (d // dil <= win // dil)).astype(np.float64) for win, dil in SW_CONFIGS)
    c[:, C_DILATED:C_DILATED + SEQ] = np.where(count > 0, np.log(np.maximum(count, 1)) * SW_HD ** 0.5, NEG)
    c[:, C_CAUSAL_T:C_CAUSAL_T + SEQ] = np.where(np.arange(P)[:, None] <= np.arange(SEQ)[None, :], 0.0, NEG)
    c[:, C_IDENT:C_IDENT + P] = np.eye(P)
    c[:, C_ONES:C_ONES + P] = 1.0
    return c


def swap_halves(w):
    half = w.shape[-1] // 2
    return np.concatenate([w[..., half:], w[..., :half]], axis=-1)


def weight_stream(i):
    w = np.zeros((DEPTH, N_UNITS, P, UNIT), np.float32)

    def whole(u0, mat):
        n = mat.shape[2] // P
        w[:, u0:u0 + n] = mat.reshape(DEPTH, KT, P, n, P).transpose(0, 3, 2, 1, 4).reshape(DEPTH, n, P, UNIT)

    def token_major(u0, mat):
        w[:, u0:u0 + 4] = mat.reshape(DEPTH, 4, 2, P, SEQ).transpose(0, 1, 3, 2, 4).reshape(DEPTH, 4, P, UNIT)

    names = ("c_q", "c_kv", "k_rope", "ml_q", "ml_k", "ml_v", "ml_o", "ml_i", "ml_f", "sw_q", "sw_k", "sw_v")
    sizes = (MLA_Q_LORA, MLA_KV_LORA, MLA_ROPE, 256, 256, 256, 256, ML_HEADS, ML_HEADS, 256, 256, 256)
    part = dict(zip(names, np.split(i["w_in"], np.cumsum(sizes)[:-1], axis=2)))
    misc = np.zeros((DEPTH, D_MODEL, P), np.float32)
    misc[:, :, ROW_I:ROW_I + ML_HEADS] = part["ml_i"]
    misc[:, :, ROW_F:ROW_F + ML_HEADS] = part["ml_f"]
    misc[:, :, ROW_R:ROW_R + MLA_ROPE] = part["k_rope"]
    misc[:, :, ROW_RS:ROW_RS + MLA_ROPE] = swap_halves(part["k_rope"])
    whole(U_IN, np.concatenate([part["c_q"], part["c_kv"], misc, part["ml_q"], part["ml_k"], part["sw_q"],
                                part["sw_k"], part["ml_o"]], axis=2))
    token_major(U_INV, np.concatenate([part["ml_v"], part["sw_v"]], axis=2))
    uq = i["mla_w_uq"].reshape(DEPTH, 2, P, MLA_HEADS, MLA_NOPE + MLA_ROPE)
    uq = np.concatenate([uq, swap_halves(uq[..., MLA_NOPE:])], axis=4)
    w[:, U_UQ:U_UQ + 2] = uq.reshape(DEPTH, 2, P, 2, 4, P).transpose(0, 3, 2, 4, 1, 5).reshape(DEPTH, 2, P, UNIT)
    ukv = i["mla_w_ukv"].reshape(DEPTH, P, MLA_HEADS, MLA_NOPE + MLA_V)
    w[:, U_UK, :, 0:SEQ] = ukv[..., :MLA_NOPE].reshape(DEPTH, P, SEQ)
    w[:, U_UV, :, 0:SEQ] = ukv[..., MLA_NOPE:].reshape(DEPTH, P, SEQ)
    whole(U_OUT, i["w_out"])
    whole(U_XK, i["x_w_kv"][:, :, :D_MODEL])
    for half in range(2):
        a = D_MODEL + half * SEQ
        token_major(U_XV + 4 * half, i["x_w_kv"][:, :, a:a + SEQ])
    whole(U_XQ, i["x_w_q"])
    whole(U_XO, i["x_w_o"])
    gu = i["w_gate_up"].reshape(DEPTH, D_MODEL, 2, FT, P).transpose(0, 1, 3, 2, 4).reshape(DEPTH, D_MODEL, -1)
    whole(U_FF, gu)
    down = i["w_down"].reshape(DEPTH, FT, P, KT, P).transpose(0, 3, 1, 2, 4).reshape(DEPTH, FT, KT, P, P)
    w[:, U_DOWN:U_DOWN + FT] = down.transpose(0, 1, 3, 2, 4).reshape(DEPTH, FT, P, UNIT)
    return w


def gain_columns(i):
    g = np.zeros((DEPTH, P, N_GAINS), np.float32)

    def put(col, v):
        n = v.shape[1] // P
        g[:, :, col:col + n] = v.reshape(DEPTH, n, P).transpose(0, 2, 1)

    for col, name in ((G_MIX_PRE, "norm_mix_pre"), (G_MIX_POST, "norm_mix_post"), (G_MEM, "norm_mem"),
                      (G_X_PRE, "norm_x_pre"), (G_X_POST, "norm_x_post"), (G_FFN_PRE, "norm_ffn_pre"),
                      (G_FFN_POST, "norm_ffn_post"), (G_Q, "mla_q_norm"), (G_KV, "mla_kv_norm"),
                      (G_CONV_B, "ml_conv_b")):
        put(col, i[name])
    taps = i["ml_conv_w"].reshape(DEPTH, ML_CONV, 4, P).transpose(0, 3, 2, 1)
    g[:, :, G_CONV_W:G_CONV_W + 4 * ML_CONV] = taps.reshape(DEPTH, P, 4 * ML_CONV)
    g[:, ROW_I:ROW_I + ML_HEADS, G_GATE_B] = i["ml_b_i"]
    g[:, ROW_F:ROW_F + ML_HEADS, G_GATE_B] = i["ml_b_f"]
    return g


def feature_major(a):
    return np.ascontiguousarray(a[0].reshape(a.shape[1], KT, P).transpose(2, 1, 0))


def kernel(**inputs):
    import concourse.bacc as bacc
    from concourse.bass_utils import run_bass_kernel_spmd

    i = {k: np.asarray(v) for k, v in inputs.items()}
    nc = bacc.Bacc("TRN2", target_bir_lowering=False, num_devices=1)
    arrays = {"x_in": feature_major(i["x"]), "mem_in": feature_major(i["mem"]), "w_in": weight_stream(i),
              "g_in": gain_columns(i), "c_in": constants()}
    args = [nc.dram_tensor(n, a.shape, F32, kind="ExternalInput").ap() for n, a in arrays.items()]
    out = nc.dram_tensor("out", (P, KT, SEQ), F32, kind="ExternalOutput").ap()
    build(nc, *args, out)
    r = run_bass_kernel_spmd(nc, [arrays], core_ids=[0])
    y = r.results[0]["out"]
    return np.ascontiguousarray(y.transpose(2, 1, 0)).reshape(1, SEQ, D_MODEL)
```

```python
from contextlib import ExitStack

import numpy as np
import concourse.bass as bass
from concourse import mybir

F32 = mybir.dt.float32
F32R = mybir.dt.float32r
ALU = mybir.AluOpType
ACT = mybir.ActivationFunctionType

P = 128
D_MODEL = 1024
SEQ = 512
DEPTH = 2
N_MEM = 256
ROPE_THETA = 500000.0
EPS = 1e-6
NEG = -1e30

MLA_HEADS, MLA_NOPE, MLA_ROPE, MLA_V = 8, 64, 32, 64
MLA_Q_LORA, MLA_KV_LORA = 256, 128
ML_HEADS, ML_DK, ML_CONV = 4, 64, 4
SW_HEADS, SW_HD = 4, 64
SW_ROT = SW_HD // 4
SW_CONFIGS = ((128, 1), (512, 4), (2048, 16))
X_HEADS = 4
X_HD = D_MODEL // X_HEADS
D_FF = 2816

KT = D_MODEL // P
TB = SEQ // P
FT = D_FF // P
UNIT = KT * P

U_IN = 0
MISC, CKV, OG = 0, 6, 8
ML = (1, 3, 5, 7)
CQ = (2, 4)
IN_FM = 10
U_INV = U_IN + IN_FM
U_SW = U_INV + 4
U_UQ = U_SW + 4
U_UK = U_UQ + 2
U_UV = U_UK + 1
U_OUT = U_UV + 1
U_XK = U_OUT + 8
U_XV = U_XK + 8
U_XQ = U_XV + 8
U_XO = U_XQ + 8
U_FF = U_XO + 8
U_DOWN = U_FF + 2 * FT
N_UNITS = U_DOWN + FT
RING = 4
LAG = 3
PROBS = LAG + 1
OUT_LAG = 2

G_MIX_PRE, G_MIX_POST, G_MEM, G_X_PRE, G_X_POST, G_FFN_PRE, G_FFN_POST = (KT * i for i in range(7))
G_Q = 7 * KT
G_KV = G_Q + 2
G_CONV_W = G_KV + 1
G_CONV_B = G_CONV_W + 4 * ML_CONV
G_GATE_B = G_CONV_B + 4
N_GAINS = G_GATE_B + 1

C_ROPE_Q = 0
C_SW_COS = C_ROPE_Q + SEQ
C_SW_SIN = C_SW_COS + SEQ
C_CAUSAL = C_SW_SIN + SEQ
C_DILATED = C_CAUSAL + SEQ
C_CAUSAL_T = C_DILATED + SEQ
C_IDENT = C_CAUSAL_T + SEQ
C_ROT = C_IDENT + P
C_ONES = C_ROT + P
C_ONE_ROWS = C_ROPE_Q
N_CONST = C_ONES + P

ROW_I, ROW_F, ROW_R, ROW_RS = 0, 32, 64, 96


def tile_plan():
    plan, uses = {}, []

    def add(name, sub, engine):
        plan.setdefault(name, []).append((len(uses), sub))
        uses.append((sub, engine))

    def whole(name, u0, n, engine="act"):
        for m in range(n):
            add(name, [(u0 + m, k * P) for k in range(KT)], engine)

    def query(h):
        add("uq", [(U_UQ + h // 4, ((h % 4) * 2 + k) * P) for k in range(2)], "dve")

    def rotation():
        add("rot", [], "dve")

    whole("in", U_IN, IN_FM)
    whole("sw", U_SW, 2)
    rotation()
    whole("sw", U_SW + 2, 1)
    rotation()
    whole("sw", U_SW + 3, 1)
    rotation()
    query(0)
    rotation()
    for h in range(1, MLA_HEADS):
        query(h)
    for m in range(4):
        add("uk", [(U_UK, m * P)], "act")
    for _ in range(TB):
        add("uv", [(U_UV, 0)], "dve")
    whole("out", U_OUT, KT)
    whole("xk", U_XK, KT)
    whole("xq", U_XQ, KT)
    whole("xo", U_XO, KT)
    for m in range(KT):
        add("down", [(U_DOWN + (m * FT + k) // KT, (m * FT + k) % KT * P) for k in range(FT)], "act")
    return plan, uses


PLAN, USES = tile_plan()


def ends_unit(use):
    sub = USES[use][0]
    return bool(sub) and all(later[0][0] > sub[-1][0] for later, _ in USES[use + 1:] if later)


def tiles_done(use):
    return sum(not ends_unit(u) for u in range(use + 1))


def emptied(use):
    engine = USES[use][1]
    return engine, sum(e == engine for _, e in USES[:use + 1])


ML_STEPS = ML_HEADS * TB + 1
BETWEEN = [(name, m, k) for use in range(PLAN["sw"][1][0], PLAN["uk"][0][0])
           for name in ("sw", "rot", "uq") for m, (at, sub) in enumerate(PLAN[name]) if at == use
           for k in range(max(len(sub), 1))]


def between(step):
    return BETWEEN[len(BETWEEN) * step // ML_STEPS:len(BETWEEN) * (step + 1) // ML_STEPS]


def completed(step):
    return [(name, m) for name, m, k in between(step) if k + 1 == max(len(PLAN[name][m][1]), 1)]


def units_through(step):
    done = [USES[PLAN[name][m][0]][0][-1][0] + 1 for t in range(step + 1) for name, m in completed(t)
            if name != "rot" and ends_unit(PLAN[name][m][0])]
    return max(done, default=U_SW + 1)


NORMS = [("mix_pre", KT), ("q", 2), ("kv", 1), ("mix_post", KT), ("x_pre", KT), ("x_post", KT),
         ("ffn_pre", KT), ("ffn_post", KT)]
NORM_AT = {name: i for i, (name, _) in enumerate(NORMS)}
NORMED = [("mix_pre", KT), ("q", 2), ("kv", 1), ("mem", KT), ("x_pre", KT), ("ffn_pre", KT)]
POST = ("mix_post", "x_post", "ffn_post")
LATE_RMS = ("ffn_pre",)


def squares_before(name):
    return sum(k for _, k in NORMS[:NORM_AT[name]])


def normed_before(name):
    if name in POST:
        name = {"mix_post": "x_pre", "x_post": "ffn_pre"}.get(name)
        if name is None:
            return sum(k for _, k in NORMED)
    return sum(k for _, k in NORMED[:[n for n, _ in NORMED].index(name)])


def tn_before(name):
    first = normed_before(name)
    return first - sum(k for n, k in NORMED if n in LATE_RMS and normed_before(n) < first)


def scaled_before(name):
    return sum(k for n, k in NORMS[:NORM_AT[name]] if n in POST)


def build(nc, x_in, mem_in, w_in, g_in, c_in, out):
    with ExitStack() as ctx:
        layer_sems = []

        def sb(name, shape, dt=F32, stack=ctx):
            return stack.enter_context(nc.sbuf_tensor(name, shape, dt))

        def sem(name):
            s = ctx.enter_context(nc.semaphore(name))
            layer_sems.append(s)
            return s

        x = sb("x", [P, KT, SEQ])
        consts = sb("consts", [P, N_CONST])
        eps = sb("eps", [P, 1])
        one = sb("one", [P, 1])
        gains = sb("gains", [P, N_GAINS])
        raw = sb("raw", [P, RING, UNIT])
        w_hi = sb("w_hi", [P, RING, UNIT], F32R)
        w_lo = sb("w_lo", [P, RING, UNIT], F32R)
        with ExitStack() as late:
            y_f = sb("y_f", [P, KT, SEQ], F32, late)
        h_hi = sb("h_hi", [P, KT, SEQ], F32R)
        h_lo = sb("h_lo", [P, KT, SEQ], F32R)
        sq = sb("sq", [P, 2, SEQ])
        acc = sb("acc", [P, SEQ])
        rstd = sb("rstd", [P, SEQ])
        mem_rstd = sb("mem_rstd", [P, N_MEM])
        stat = sb("stat", [P, 3, 64])
        acol = sb("acol", [P, TB, ML_HEADS])

        with ExitStack() as room:
            tn_mix = sb("tn_mix", [P, 2, SEQ], F32, room)
            q_mla = sb("q_mla", [P, MLA_HEADS, SEQ], F32, room)
            with ExitStack() as early:
                ml_qk = sb("ml_qk", [P, 4, SEQ], F32, early)
                ml_v = sb("ml_v", [P, TB, ML_HEADS, 2, ML_DK], F32, early)
                gate = sb("gate", [P, 4, SEQ], F32, early)
            k_mla = sb("k_mla", [P, MLA_HEADS, SEQ], F32, room)
            v_mla = sb("v_mla", [P, TB, MLA_HEADS * MLA_V], F32, room)
            k_pe = sb("k_pe", [P, SEQ], F32, room)
            sw_qk = sb("sw_qk", [P, 4, SEQ], F32, room)
            sw_v = sb("sw_v", [P, TB, SW_HEADS * SW_HD], F32, room)
            o_gate = sb("o_gate", [P, 2, SEQ], F32, room)
            with ExitStack() as early:
                c_hi = sb("c_hi", [P, 3, SEQ], F32R, early)
                c_lo = sb("c_lo", [P, 3, SEQ], F32R, early)
                conv_in = sb("conv_in", [P, 2, SEQ + 4], F32, early)
                w_ml = sb("w_ml", [P, 2, SEQ], F32, early)
            p_mix = sb("p_mix", [P, PROBS, SEQ], F32, room)
            pt_mix = sb("pt_mix", [P, 2, TB, SEQ], F32, room)
        with ExitStack() as room:
            tn_x = sb("tn_x", [P, 2, SEQ], F32, room)
            y_x = sb("y_x", [P, KT, SEQ], F32, room)
            mem = sb("mem", [P, KT, N_MEM], F32, room)
            with ExitStack() as first:
                mem_sq = sb("mem_sq", [P, KT, N_MEM], F32, first)
                ones_first = sb("ones_first", [P, P], F32, first)
            m_hi = sb("m_hi", [P, KT, N_MEM], F32R, room)
            m_lo = sb("m_lo", [P, KT, N_MEM], F32R, room)
            q_x = sb("q_x", [P, KT, SEQ], F32, room)
            k_x = sb("k_x", [P, KT, N_MEM], F32, room)
            v_x = sb("v_x", [P, 2, D_MODEL], F32, room)
            p_x = sb("p_x", [P, PROBS, N_MEM], F32, room)
            pt_x = sb("pt_x", [P, 2, 2, SEQ], F32, room)
        with ExitStack() as room:
            a_hi = sb("a_hi", [P, FT * SEQ], F32R, room)
            a_lo = sb("a_lo", [P, FT * SEQ], F32R, room)
        tn_of = {"mix_pre": tn_mix, "q": tn_mix, "kv": tn_mix, "mem": tn_x, "x_pre": tn_x}
        f_e, f_a = acc, sq

        bank = [ctx.enter_context(nc.psum_tensor(f"bank{i}", [P, SEQ], F32)) for i in range(8)]
        dense = bank[0:2]
        wide = bank[2:6]
        scores, turned = bank[2:4], bank[4:6]
        score_ring = bank[0:4]
        outs = bank[6:8]
        norm_bank = bank[7]
        ff_bank = bank[0:4]

        mem_first, x_loaded, consts_loaded, mem_squared, mem_summed, mem_ln = (
            ctx.enter_context(nc.semaphore(n)) for n in ("mem_first", "x_loaded", "consts_loaded", "mem_squared",
                                                         "mem_summed", "mem_ln"))
        fixed_set = ctx.enter_context(nc.semaphore("fixed_set"))
        stored = ctx.enter_context(nc.semaphore("stored"))
        raw_loaded = [sem(f"raw_loaded{i}") for i in range(RING)]
        gains_loaded, mem_loaded = sem("gains_loaded"), sem("mem_loaded")
        split_hi, split_lo = sem("split_hi"), sem("split_lo")
        unit_used, tile_done = sem("unit_used"), sem("tile_done")
        emptied_act, emptied_dve = sem("emptied_act"), sem("emptied_dve")
        squared, squares_added = sem("squared"), sem("squares_added")
        norm_summed, ln_done, rstd_ready = sem("norm_summed"), sem("ln_done"), sem("rstd_ready")
        normed, normed_hi, normed_lo = sem("normed"), sem("normed_hi"), sem("normed_lo")
        y_scaled, x_updated = sem("y_scaled"), sem("x_updated")
        dve_step, act_step = sem("dve_step"), sem("act_step")
        pads_set = sem("pads_set")
        conv_done, conv_exp, ml_qk_ready = sem("conv_done"), sem("conv_exp"), sem("ml_qk_ready")
        gate_biased, gate_log, gate_rows = sem("gate_biased"), sem("gate_log"), sem("gate_rows")
        acol_turned, acol_ready = sem("acol_turned"), sem("acol_ready")
        k_pe_ready, k_pe_spread = sem("k_pe_ready"), sem("k_pe_spread")
        roped = sem("roped")
        o_ready, v_ready = sem("o_ready"), sem("v_ready")
        spread, ml_scored, ml_weight, ml_exp, ml_prob, ml_num = (
            sem("spread"), sem("ml_scored"), sem("ml_weight"), sem("ml_exp"), sem("ml_prob"), sem("ml_num"))
        ml_floor, ml_abs, ml_out, ml_hi, ml_lo = (
            sem("ml_floor"), sem("ml_abs"), sem("ml_out"), sem("ml_hi"), sem("ml_lo"))
        mix_at, x_at = ({n: sem(f"{c}_{n}") for n in ("scored", "masked", "exped", "probs", "turned", "copied",
                                                      "out", "out_hi", "out_lo")} for c in ("mix", "x"))
        xv_ready = sem("xv_ready")
        ff_gate, ff_exp, ff_step = sem("ff_gate"), sem("ff_exp"), sem("ff_step")
        ff_a, ff_hi, ff_lo = sem("ff_a"), sem("ff_hi"), sem("ff_lo")

        def const(col, n=P, rows=slice(0, P)):
            return consts[rows, col:col + n]

        def gain(col, rows=slice(0, P)):
            return gains[rows, col:col + 1]

        def use_of(name, m):
            return PLAN[name][m][0]

        def wait_tile(eng, use):
            if ends_unit(use):
                eng.wait_ge(unit_used, USES[use][0][-1][0] + 1)
            else:
                eng.wait_ge(tile_done, tiles_done(use))

        def wait_emptied(eng, use):
            engine, count = emptied(use)
            eng.wait_ge(emptied_act if engine == "act" else emptied_dve, count)

        def counter(eng):
            counts = {}

            def done(ins, s):
                counts[s.name] = counts.get(s.name, 0) + 1
                ins.then_inc(s, 1)
                eng.wait_ge(s, counts[s.name])
            return done

        def c_tile(m):
            return q_mla[:, m // 2, :]

        MIX_HEADS = MLA_HEADS + SW_HEADS

        def mix_head(n):
            if n < MLA_HEADS:
                return dict(q=q_mla[:, n, :], k=k_mla[:, n, :], v=lambda kb: v_mla[:, kb, n * MLA_V:(n + 1) * MLA_V],
                            mask=C_CAUSAL, scale=(MLA_NOPE + MLA_ROPE) ** -0.5, tile=n // 2, row=64 * (n % 2))
            h = n - MLA_HEADS
            r = slice(64 * (h % 2), 64 * (h % 2) + 64)
            return dict(q=sw_qk[r, h // 2, :], k=sw_qk[r, 2 + h // 2, :],
                        v=lambda kb: sw_v[:, kb, h * SW_HD:(h + 1) * SW_HD],
                        mask=C_DILATED, scale=SW_HD ** -0.5, tile=6 + h // 2, row=64 * (h % 2))

        def causal_len(qb):
            return (qb + 1) * P

        with nc.Block() as block:
            @block.sync
            def _(sp):
                sp.dma_start(mem[:, :, :], mem_in).then_inc(mem_first, 16)
                sp.dma_start(x[:, :, :], x_in).then_inc(x_loaded, 16)
                sp.dma_start(consts[:, :], c_in).then_inc(consts_loaded, 16)

            @block.vector
            def _(dve):
                dve.memset(eps[:, :], EPS).then_inc(fixed_set, 1)
                dve.memset(one[:, :], 1.0).then_inc(fixed_set, 1)
                dve.memset(ones_first[:, :], 1.0).then_inc(fixed_set, 1)
                dve.wait_ge(fixed_set, 3)

            @block.scalar
            def _(act):
                act.preload_act_table_set("natural_log_exp_and_others")
                act.wait_ge(mem_first, 16)
                act.activation(mem_sq[:, :, :], mem[:, :, :], ACT.Square).then_inc(mem_squared, 1)
                act.wait_ge(fixed_set, 3)
                act.wait_ge(mem_summed, 1)
                act.activation(mem_rstd[:, :], bank[0][:, 0:N_MEM], ACT.Ln, bias=eps[:, :], scale=1.0 / D_MODEL)\
                   .then_inc(mem_ln, 1)
                act.wait_ge(mem_ln, 1)
                act.activation(mem_rstd[:, :], mem_rstd[:, :], ACT.Exp, scale=-0.5).then_inc(mem_ln, 1)
                act.wait_ge(mem_ln, 2)

            @block.tensor
            def _(pe):
                pe.wait_ge(fixed_set, 3)
                pe.wait_ge(mem_squared, 1)
                for k in range(KT):
                    mm = pe.matmul(bank[0][:, 0:N_MEM], ones_first[:, :], mem_sq[:, k, :], start=(k == 0),
                                   stop=(k == KT - 1))
                mm.then_inc(mem_summed, 1)

        with nc.Fori(0, DEPTH) as layer:
            with nc.Block() as block:

                @block.sync
                def _(sp):
                    sp.dma_start(gains[:, :], g_in[layer, :, :]).then_inc(gains_loaded, 16)
                    for s in range(RING):
                        sp.dma_start(raw[:, s, :], w_in[layer, s, :, :]).then_inc(raw_loaded[s], 16)

                    def stream(a, b):
                        with sp.Fori(a // RING, b // RING) as j:
                            for s in range(RING):
                                sp.wait_ge(split_lo, j * RING + (s + 1 - RING))
                                sp.dma_start(raw[:, s, :], w_in[layer, j * RING + s, :, :])\
                                  .then_inc(raw_loaded[s], 16)
                    mid = -(-U_OUT // RING) * RING + RING
                    stream(RING, mid)
                    sp.wait_ge(mix_at["out_lo"], MIX_HEADS)
                    sp.dma_start(mem[:, :, :], mem_in).then_inc(mem_loaded, 16)
                    stream(mid, N_UNITS)

                @block.gpsimd
                def _(pool):
                    with pool.Fori(0, N_UNITS // RING) as j:
                        for s in range(RING):
                            pool.wait_ge(split_hi, j * RING + (s + 1))
                            pool.tensor_tensor(w_lo[:, s, :], raw[:, s, :], w_hi[:, s, :].bitcast(F32),
                                               ALU.subtract).then_inc(split_lo, 1)

                @block.tensor
                def _(pe):
                    def three(out_ap, l_hi, l_lo, r_hi, r_lo, start, stop):
                        pe.matmul(out_ap, l_hi, r_hi, start=start, stop=False)
                        pe.matmul(out_ap, l_hi, r_lo, start=False, stop=False)
                        return pe.matmul(out_ap, l_lo, r_hi, start=False, stop=stop)

                    def project_step(name, m, k, act_hi, act_lo, width=SEQ):
                        use, subs = PLAN[name][m]
                        (u, col), last = subs[k], k == len(subs) - 1
                        if k == 0 and use >= 2:
                            wait_emptied(pe, use - 2)
                        if k == 0 or subs[k - 1][0] != u:
                            pe.wait_ge(split_lo, u + 1)
                        w = slice(col, col + P)
                        mm = three(dense[use % 2][:, 0:width], w_hi[:, u % RING, w], w_lo[:, u % RING, w], act_hi(k),
                                   act_lo(k), k == 0, last)
                        if last and not ends_unit(use):
                            mm.then_inc(tile_done, 1)
                        elif last or subs[k + 1][0] != u:
                            mm.then_inc(unit_used, 1)

                    def project(name, m, act_hi, act_lo, width=SEQ, before=None):
                        for k in range(len(PLAN[name][m][1])):
                            if before is not None:
                                before(k)
                            project_step(name, m, k, act_hi, act_lo, width)

                    def project_tokens(u0, banks, act_hi, act_lo):
                        for j in range(4):
                            s = (u0 + j) % RING
                            pe.wait_ge(split_lo, u0 + j + 1)
                            for i in range(2):
                                k, w = 2 * j + i, slice(i * SEQ, (i + 1) * SEQ)
                                for b, bank_t in enumerate(banks):
                                    mm = three(bank_t[:, :], act_hi(k, b), act_lo(k, b), w_hi[:, s, w],
                                               w_lo[:, s, w], k == 0, k == KT - 1)
                            mm.then_inc(unit_used, 1)

                    def norm_sum(name, width=SEQ):
                        i = NORM_AT[name]
                        pe.wait_ge(squares_added, squares_before(name) + NORMS[i][1])
                        if i >= 1:
                            pe.wait_ge(ln_done, i)
                        pe.matmul(norm_bank[:, 0:width], const(C_ONES), acc[:, 0:width], start=True, stop=True)\
                          .then_inc(norm_summed, 1)

                    def after_norm(name):
                        return lambda k: pe.wait_ge(normed_lo, normed_before(name) + k + 1)

                    def tiles(t):
                        return lambda k: t[:, k, :]

                    pe.wait_ge(consts_loaded, 16)
                    norm_sum("mix_pre")
                    for m in range(IN_FM):
                        project("in", m, tiles(h_hi), tiles(h_lo), before=after_norm("mix_pre") if m == 0 else None)
                        if m == CQ[1] + 1:
                            norm_sum("q")
                        if m == CKV + 1:
                            norm_sum("kv")
                    project_tokens(U_INV, wide, lambda k, b: h_hi[:, k, b * P:(b + 1) * P],
                                   lambda k, b: h_lo[:, k, b * P:(b + 1) * P])
                    project("sw", 0, tiles(h_hi), tiles(h_lo))

                    def do_between(step):
                        for name, m, k in between(step):
                            if name == "sw":
                                project_step("sw", m, k, tiles(h_hi), tiles(h_lo))
                            elif name == "uq":
                                if m == 0:
                                    after_norm("q")(k)
                                project_step("uq", m, k, tiles(c_hi), tiles(c_lo))
                            else:
                                use = use_of("rot", m)
                                wait_emptied(pe, use - 2)
                                wait_emptied(pe, use_of("sw", m))
                                pe.matmul(dense[use % 2][:, :], const(C_ROT), sw_qk[:, m, :], start=True, stop=True)\
                                  .then_inc(tile_done, 1)

                    g4 = slice(0, ML_HEADS)
                    pe.wait_ge(gate_rows, 3)
                    pe.wait_ge(v_ready, TB)
                    for kb in range(TB):
                        mm = pe.matmul(outs[0][:, 4 * kb:4 * kb + 4], gate[g4, 0, kb * P:(kb + 1) * P],
                                       const(C_IDENT, 4, g4), start=True, stop=True)
                    mm.then_inc(acol_turned, 1)
                    pe.wait_ge(acol_ready, 1)
                    pe.wait_ge(ln_done, 3)
                    pe.wait_ge(ml_qk_ready, 4)
                    units = [(h, kb) for h in range(ML_HEADS) for kb in range(TB)]

                    def ml_scores(u):
                        h, kb = units[u]
                        r = slice(64 * (h % 2), 64 * (h % 2) + 64)
                        if kb == 0:
                            if h:
                                pe.wait_ge(ml_weight, TB * h)
                                pe.wait_ge(ml_floor, h)
                            sel = const(C_IDENT + h, 1, g4).broadcast_to([ML_HEADS, P])
                            pe.matmul(outs[0][:, :], sel, gate[g4, 1, :], start=True, stop=True)
                            pe.matmul(outs[1][:, :], sel, gate[g4, 2, :], start=True, stop=True)\
                              .then_inc(spread, 1)
                        if u >= 2:
                            pe.wait_ge(ml_prob, u - 1)
                        pe.matmul(scores[u % 2][:, 0:SEQ - kb * P], ml_qk[r, 2 + h // 2, kb * P:(kb + 1) * P],
                                  ml_qk[r, h // 2, kb * P:SEQ], start=True, stop=True).then_inc(ml_scored, 1)

                    def ml_numerator(u):
                        h, kb = units[u]
                        pe.wait_ge(ml_prob, u + 1)
                        if kb == 0 and h >= 2:
                            pe.wait_ge(ml_out, h - 1)
                        pe.matmul(turned[h % 2][:, kb * P:SEQ], ml_v[:, kb, h, :, :].rearrange("p a d -> p (a d)"),
                                  w_ml[:, u % 2, 0:SEQ - kb * P], start=(kb == 0), stop=(kb == TB - 1))\
                          .then_inc(ml_num, 1)

                    for u in range(len(units) + 1):
                        if u < len(units):
                            ml_scores(u)
                        if u >= 1:
                            ml_numerator(u - 1)
                        do_between(u)

                    for m in range(4):
                        project("uk", m, lambda k: c_hi[:, 2, :], lambda k: c_lo[:, 2, :],
                                before=after_norm("kv") if m == 0 else None)
                    pe.wait_ge(split_lo, U_UV + 1)
                    for b in range(TB):
                        use, s, t = use_of("uv", b), U_UV % RING, slice(b * P, (b + 1) * P)
                        wait_emptied(pe, use - 2)
                        mm = three(dense[use % 2][:, :], c_hi[:, 2, t], c_lo[:, 2, t], w_hi[:, s, 0:SEQ],
                                   w_lo[:, s, 0:SEQ], True, True)
                        mm.then_inc(unit_used if ends_unit(use) else tile_done, 1)

                    def attention(a, heads, probs, klen, emit_scores, emit_out):
                        n_units = heads * TB
                        for u in range(n_units + LAG + OUT_LAG):
                            if u < n_units:
                                if u >= 4:
                                    pe.wait_ge(a["masked"], u - 3)
                                emit_scores(u // TB, u % TB, score_ring[u % 4]).then_inc(a["scored"], 1)
                            v = u - LAG
                            if 0 <= v < n_units:
                                pe.wait_ge(a["probs"], v + 1)
                                if v >= 2:
                                    pe.wait_ge(a["copied"], v - 1)
                                for kb in range(klen(v % TB) // P):
                                    mm = pe.transpose(turned[v % 2][:, kb * P:(kb + 1) * P],
                                                      probs[:, v % PROBS, kb * P:(kb + 1) * P], const(C_IDENT))
                                mm.then_inc(a["turned"], 1)
                            w = u - LAG - OUT_LAG
                            if w >= 0 and w % TB == TB - 1:
                                pe.wait_ge(a["copied"], w + 1)
                                emit_out(w // TB)

                    def mix_scores(head, qb, bank_t):
                        hd = mix_head(head)
                        if head == 0 and qb == 0:
                            wait_emptied(pe, use_of("uq", MLA_HEADS - 1))
                            wait_emptied(pe, use_of("uk", 3))
                            wait_emptied(pe, use_of("uv", TB - 1))
                            pe.wait_ge(k_pe_spread, 2)
                            pe.wait_ge(roped, 4)
                            pe.wait_ge(ml_out, ML_HEADS)
                        n = causal_len(qb)
                        return pe.matmul(bank_t[:, 0:n], hd["q"][:, qb * P:n], hd["k"][:, 0:n], start=True, stop=True)

                    def mix_out(head):
                        if head >= 2:
                            pe.wait_ge(mix_at["out_lo"], head - 1)
                        for kb in range(TB):
                            mm = pe.matmul(outs[head % 2][0:64, kb * P:SEQ], mix_head(head)["v"](kb),
                                           pt_mix[:, head % 2, kb, kb * P:SEQ], start=(kb == 0), stop=(kb == TB - 1))
                        mm.then_inc(mix_at["out"], 1)

                    attention(mix_at, MIX_HEADS, p_mix, causal_len, mix_scores, mix_out)

                    pe.wait_ge(mix_at["out_lo"], MIX_HEADS)
                    pe.wait_ge(ml_lo, 2)
                    for m in range(KT):
                        project("out", m, tiles(h_hi), tiles(h_lo))
                    norm_sum("mix_post")
                    for m in range(KT):
                        project("xk", m, tiles(m_hi), tiles(m_lo), N_MEM, before=after_norm("mem") if m == 0 else None)
                    for half in range(2):
                        project_tokens(U_XV + 4 * half, wide[2 * half:2 * half + 2],
                                       lambda k, b: m_hi[:, k, b * P:(b + 1) * P],
                                       lambda k, b: m_lo[:, k, b * P:(b + 1) * P])
                        if half == 0:
                            norm_sum("x_pre")
                    for m in range(KT):
                        project("xq", m, tiles(h_hi), tiles(h_lo), before=after_norm("x_pre") if m == 0 else None)

                    def x_scores(head, qb, bank_t):
                        if head == 0 and qb == 0:
                            wait_emptied(pe, use_of("xq", KT - 1))
                            pe.wait_ge(xv_ready, 4)
                        for c in range(2):
                            mm = pe.matmul(bank_t[:, 0:N_MEM], q_x[:, 2 * head + c, qb * P:(qb + 1) * P],
                                           k_x[:, 2 * head + c, :], start=(c == 0), stop=(c == 1))
                        return mm

                    def x_out(head):
                        for c in range(2):
                            if head >= 1:
                                pe.wait_ge(x_at["out_lo"], 2 * head - 1 + c)
                            for kb in range(2):
                                col = head * X_HD + c * P
                                mm = pe.matmul(outs[c][:, :], v_x[:, kb, col:col + P], pt_x[:, head % 2, kb, :],
                                               start=(kb == 0), stop=(kb == 1))
                            mm.then_inc(x_at["out"], 1)

                    attention(x_at, X_HEADS, p_x, lambda qb: N_MEM, x_scores, x_out)
                    pe.wait_ge(x_at["out_lo"], KT)
                    for m in range(KT):
                        project("xo", m, tiles(h_hi), tiles(h_lo))
                    norm_sum("x_post")

                    def gate_up_step(i, k):
                        s, w = (U_FF + i) % RING, slice(k * P, (k + 1) * P)
                        return three(ff_bank[i][:, :], w_hi[:, s, w], w_lo[:, s, w], h_hi[:, k, :], h_lo[:, k, :],
                                     k == 0, k == KT - 1)

                    wait_emptied(pe, use_of("xo", KT - 1))
                    pe.wait_ge(split_lo, U_FF + 4)
                    for k in range(KT):
                        after_norm("ffn_pre")(k)
                        for i in range(4):
                            mm = gate_up_step(i, k)
                            if k == KT - 1:
                                mm.then_inc(unit_used, 1)
                                if i == 0:
                                    norm_sum("ffn_pre")
                    with pe.Fori(1, FT // 2) as j:
                        for i in range(4):
                            pe.wait_ge(ff_a if i % 2 else ff_gate, j * 2 + (i // 2 - 1))
                            pe.wait_ge(split_lo, j * 4 + (U_FF + i + 1))
                            for k in range(KT):
                                mm = gate_up_step(i, k)
                            mm.then_inc(unit_used, 1)

                    for m in range(KT):
                        project("down", m, lambda k: a_hi[:, k * SEQ:(k + 1) * SEQ],
                                lambda k: a_lo[:, k * SEQ:(k + 1) * SEQ],
                                before=(lambda k: pe.wait_ge(ff_lo, k + 1)) if m == 0 else None)
                    norm_sum("ffn_post")

                @block.scalar
                def _(act):
                    done = counter(act)
                    act.preload_act_table_set("natural_log_exp_and_others")
                    made = [0]

                    def split_unit(n, j=0):
                        s = n % RING
                        act.wait_ge(raw_loaded[s], j * 16 + 16 * (n // RING + 1))
                        if n >= RING:
                            act.wait_ge(unit_used, j * RING + (n - RING + 1))
                        act.activation(w_hi[:, s, :], raw[:, s, :], ACT.Copy).then_inc(split_hi, 1)

                    def split_until(n):
                        while made[0] < min(n, N_UNITS):
                            split_unit(made[0])
                            made[0] += 1

                    def square(name, k, src, width=SEQ):
                        c = squares_before(name) + k
                        if c >= 2:
                            act.wait_ge(squares_added, c - 1)
                        act.activation(sq[:, c % 2, 0:width], src, ACT.Square).then_inc(squared, 1)

                    def make_rstd(name, features, width=SEQ):
                        act.wait_ge(norm_summed, NORM_AT[name] + 1)
                        if tn_before(name):
                            act.wait_ge(normed, tn_before(name))
                        if scaled_before(name):
                            act.wait_ge(y_scaled, scaled_before(name))
                        done(act.activation(rstd[:, 0:width], norm_bank[:, 0:width], ACT.Ln, bias=eps[:, :],
                                            scale=1.0 / features), ln_done)
                        act.activation(rstd[:, 0:width], rstd[:, 0:width], ACT.Exp, scale=-0.5)\
                           .then_inc(rstd_ready, 1)

                    def norm_hi(name, k, dst, width=SEQ):
                        c = tn_before(name) + k
                        act.wait_ge(normed, c + 1)
                        act.activation(dst, tn_of[name][:, c % 2, 0:width], ACT.Copy).then_inc(normed_hi, 1)

                    def scaled_hi(k, col):
                        act.activation(h_hi[:, k, :], x[:, k, :], ACT.Copy, scale=gain(col + k))\
                           .then_inc(normed_hi, 1)

                    def empty(name, m, dst, width=SEQ, func=ACT.Copy, scale=1.0):
                        use = use_of(name, m)
                        wait_tile(act, use)
                        done(act.activation(dst, dense[use % 2][:, 0:width], func, scale=scale), emptied_act)

                    act.wait_ge(x_loaded, 16)
                    for k in range(KT):
                        square("mix_pre", k, x[:, k, :])
                    split_until(2)
                    make_rstd("mix_pre", D_MODEL)
                    split_until(3)
                    for k in range(KT):
                        norm_hi("mix_pre", k, h_hi[:, k, :])

                    g4 = slice(0, ML_HEADS)
                    def conv_exponential(j):
                        act.wait_ge(conv_done, j + 1)
                        act.activation(conv_in[:, j % 2, 3:3 + SEQ], ml_qk[:, j, :], ACT.Exp, scale=-1.0)\
                           .then_inc(conv_exp, 1)

                    for m in range(IN_FM):
                        split_until(m + 4)
                        if m in ML:
                            j = ML.index(m)
                            if j == 0:
                                act.wait_ge(pads_set, 2)
                            if j >= 2:
                                act.wait_ge(ml_qk_ready, j - 1)
                            empty("in", m, conv_in[:, j % 2, 3:3 + SEQ])
                        elif m >= OG:
                            empty("in", m, o_gate[:, m - OG, :], func=ACT.Exp, scale=-1.0)
                        else:
                            empty("in", m, c_tile(m))
                        if m == ML[0]:
                            act.wait_ge(gate_biased, 2)
                            done(act.activation(gate[g4, 3, :], gate[g4, 1, :], ACT.Abs), gate_log)
                            done(act.activation(gate[g4, 3, :], gate[g4, 3, :], ACT.Exp, scale=-1.0), gate_log)
                            done(act.activation(gate[g4, 3, :], gate[g4, 3, :], ACT.Ln, bias=one[g4, :]), gate_log)
                        if m == CQ[1]:
                            for k in range(2):
                                square("q", k, c_tile(CQ[k]))
                        if m - 1 in ML:
                            conv_exponential(ML.index(m - 1))
                        if m == CKV:
                            square("kv", 0, c_tile(CKV))
                            make_rstd("q", MLA_Q_LORA)
                            for k in range(2):
                                norm_hi("q", k, c_hi[:, k, :])
                        if m == OG:
                            make_rstd("kv", MLA_KV_LORA)
                            norm_hi("kv", 0, c_hi[:, 2, :])
                    split_until(U_SW + 3)
                    empty("sw", 0, sw_qk[:, 0, :])

                    ml_units = ML_HEADS * TB
                    for u in range(ml_units + 4):
                        h = u // TB
                        if 1 <= u <= ML_STEPS:
                            for name, m in completed(u - 1):
                                if name == "sw":
                                    empty("sw", m, sw_qk[:, m, :])
                            split_until(units_through(u - 1) + 4)
                        if u < ml_units:
                            n = SEQ - u % TB * P
                            act.wait_ge(ml_weight, u + 1)
                            act.activation(w_ml[:, u % 2, 0:n], w_ml[:, u % 2, 0:n], ACT.Exp).then_inc(ml_exp, 1)
                            if u % TB == TB - 1:
                                act.wait_ge(spread, h + 1)
                                if h:
                                    act.wait_ge(ml_out, h)
                                act.activation(conv_in[64:128, 0, 0:SEQ], outs[1][64:128, :], ACT.Exp)\
                                   .then_inc(ml_floor, 1)
                        if u >= TB and u % TB == 1:
                            act.wait_ge(ml_num, TB * h)
                            act.activation(conv_in[64:128, 1, 0:SEQ], turned[(h - 1) % 2][64:128, :], ACT.Abs)\
                               .then_inc(ml_abs, 1)
                        if u >= TB and u % TB == 3 and h % 2 == 0:
                            act.wait_ge(ml_out, h)
                            act.activation(h_hi[:, 3 + h // 2, :], o_gate[:, h // 2 - 1, :], ACT.Copy)\
                               .then_inc(ml_hi, 1)
                    split_until(U_UK + 4)
                    for m in range(4):
                        use = use_of("uk", m)
                        wait_tile(act, use)
                        for i in range(2):
                            done(act.activation(k_mla[0:64, 2 * m + i, :], dense[use % 2][64 * i:64 * i + 64, :],
                                                ACT.Copy), emptied_act if i else act_step)
                    split_until(U_UV + 4)

                    def attention(a, heads, probs, probs_t, klen, banks, emit_hi):
                        n_units = heads * TB
                        for u in range(n_units + LAG + OUT_LAG):
                            if u < n_units:
                                n = klen(u % TB)
                                act.wait_ge(a["masked"], u + 1)
                                act.activation(probs[:, u % PROBS, 0:n], probs[:, u % PROBS, 0:n], ACT.Exp, scale=-1.0,
                                               bias=stat[:, 0, u:u + 1], accum_out=stat[:, 1, u:u + 1])\
                                   .then_inc(a["exped"], 1)
                            v = u - LAG
                            if 0 <= v < n_units:
                                head, qb, m = v // TB, v % TB, klen(v % TB) // P
                                act.wait_ge(a["turned"], v + 1)
                                if qb == 0 and head >= 2:
                                    act.wait_ge(a["out"], banks * (head - 1))
                                act.activation(probs_t[:, head % 2, 0:m, qb * P:(qb + 1) * P],
                                               turned[v % 2][:, 0:m * P].rearrange("p (b q) -> p b q", q=P),
                                               ACT.Copy).then_inc(a["copied"], 1)
                            w = u - LAG - OUT_LAG
                            if w >= 0 and w % TB == TB - 1:
                                emit_hi(w // TB)

                    def mix_hi(head):
                        hd = mix_head(head)
                        act.wait_ge(mix_at["out"], head + 1)
                        act.activation(h_hi[hd["row"]:hd["row"] + 64, hd["tile"], :], outs[head % 2][0:64, :],
                                       ACT.Copy).then_inc(mix_at["out_hi"], 1)

                    attention(mix_at, MIX_HEADS, p_mix, pt_mix, causal_len, 1, mix_hi)

                    def post(name, plan, y, between=None):
                        for m in range(KT):
                            use = use_of(plan, m)
                            split_until(USES[use][0][-1][0] + 4)
                            wait_tile(act, use)
                            square(name, m, dense[use % 2][:, :])
                            act.activation(y[:, m, :], dense[use % 2][:, :], ACT.Copy).then_inc(emptied_act, 1)
                            if between is not None:
                                between(m)

                    post("mix_post", "out", y_x, lambda m: norm_hi("mem", m, m_hi[:, m, :], N_MEM))
                    make_rstd("mix_post", D_MODEL)
                    for m in range(KT):
                        split_until(U_XK + m + 4)
                        empty("xk", m, k_x[:, m, :], width=N_MEM)
                        act.wait_ge(x_updated, m + 1)
                        square("x_pre", m, x[:, m, :])
                    split_until(U_XV + 4 + 3)
                    make_rstd("x_pre", D_MODEL)
                    for k in range(KT):
                        split_until(U_XV + 8 + k // 2)
                        norm_hi("x_pre", k, h_hi[:, k, :])
                    split_until(U_XQ + 3)
                    for m in range(KT):
                        split_until(U_XQ + m + 4)
                        empty("xq", m, q_x[:, m, :])

                    def x_hi(head):
                        for c in range(2):
                            act.wait_ge(x_at["out"], 2 * head + c + 1)
                            act.activation(h_hi[:, 2 * head + c, :], outs[c][:, :], ACT.Copy)\
                               .then_inc(x_at["out_hi"], 1)

                    attention(x_at, X_HEADS, p_x, pt_x, lambda qb: N_MEM, 2, x_hi)
                    post("x_post", "xo", y_x)
                    split_until(U_FF + 4)
                    make_rstd("x_post", D_MODEL)
                    for k in range(KT):
                        act.wait_ge(x_updated, KT + k + 1)
                        scaled_hi(k, G_FFN_PRE)
                        square("ffn_pre", k, x[:, k, :])
                    make_rstd("ffn_pre", D_MODEL)

                    def ff_turn(j, first_turn):
                        for i in range(2):
                            if not (first_turn and i == 0):
                                split_unit(U_FF + 3 + 2 * i, j)
                            act.wait_ge(ff_gate, j * 2 + (i + 1))
                            act.activation(f_e[:, :], f_a[:, i, :], ACT.Exp, scale=-1.0).then_inc(ff_exp, 1)
                            split_unit(U_FF + 4 + 2 * i, j)
                            act.wait_ge(ff_a, j * 2 + (i + 1))
                            act.activation(a_hi[:, bass.ds(j * (2 * SEQ) + i * SEQ, SEQ)], f_a[:, i, :], ACT.Copy)\
                               .then_inc(ff_hi, 1)

                    ff_turn(0, True)
                    with act.Fori(1, FT // 2) as j:
                        ff_turn(j, False)
                    made[0] = U_DOWN + 3
                    act.wait_ge(ff_lo, FT)
                    post("ffn_post", "down", y_f)
                    make_rstd("ffn_post", D_MODEL)

                @block.vector
                def _(dve):
                    done = counter(dve)

                    def add_square(name, k):
                        dve.wait_ge(squared, squares_before(name) + k + 1)
                        s = (squares_before(name) + k) % 2
                        if k == 0:
                            if NORM_AT[name]:
                                dve.wait_ge(norm_summed, NORM_AT[name])
                            ins = dve.tensor_copy(acc[:, :], sq[:, s, :])
                        else:
                            ins = dve.tensor_tensor(acc[:, :], acc[:, :], sq[:, s, :], ALU.add)
                        done(ins, squares_added)

                    def add_squares(name, n, between=None):
                        for k in range(n):
                            add_square(name, k)
                            if between is not None:
                                between(k)

                    def norm_step(name, k, n, src, col, dst_hi, dst_lo):
                        c, tn = tn_before(name) + k, tn_of[name]
                        r, width = (mem_rstd, N_MEM) if name == "mem" else (rstd, SEQ)
                        if k < n:
                            done(dve.scalar_tensor_tensor(out=tn[:, c % 2, 0:width], in0=src(k),
                                                          scalar=gain(col + k), in1=r[:, 0:width],
                                                          op0=ALU.mult, op1=ALU.mult), normed)
                        if k >= 1:
                            dve.wait_ge(normed_hi, normed_before(name) + k)
                            done(dve.tensor_tensor(dst_lo(k - 1), tn[:, (c - 1) % 2, 0:width],
                                                   dst_hi(k - 1).bitcast(F32), ALU.subtract), normed_lo)

                    def norm(name, n, *operands):
                        dve.wait_ge(rstd_ready, NORM_AT[name] + 1)
                        for k in range(n + 1):
                            norm_step(name, k, n, *operands)

                    def scaled_lo(name, k, col):
                        dve.wait_ge(normed_hi, normed_before(name) + k + 1)
                        done(dve.scalar_tensor_tensor(out=h_lo[:, k, :], in0=x[:, k, :], scalar=gain(col + k),
                                                      in1=h_hi[:, k, :].bitcast(F32), op0=ALU.mult,
                                                      op1=ALU.subtract), normed_lo)

                    def residual(name, plan, y, col, between=None):
                        dve.wait_ge(rstd_ready, NORM_AT[name] + 1)
                        wait_emptied(dve, use_of(plan, KT - 1))
                        for k in range(KT):
                            done(dve.scalar_tensor_tensor(out=y[:, k, :], in0=y[:, k, :], scalar=gain(col + k),
                                                          in1=rstd[:, :], op0=ALU.mult, op1=ALU.mult), y_scaled)
                            done(dve.tensor_tensor(x[:, k, :], x[:, k, :], y[:, k, :], ALU.add), x_updated)
                            if between is not None:
                                between(k)

                    def tiles(t):
                        return lambda k: t[:, k, :]

                    dve.wait_ge(x_loaded, 16)
                    dve.wait_ge(consts_loaded, 16)
                    add_squares("mix_pre", KT)
                    done(dve.memset(ml_v[:, :, :, 1, :], 1.0), pads_set)
                    done(dve.memset(conv_in[:, :, 0:3], 0.0), pads_set)
                    dve.wait_ge(gains_loaded, 16)
                    norm("mix_pre", KT, tiles(x), G_MIX_PRE, tiles(h_hi), tiles(h_lo))

                    wait_emptied(dve, use_of("in", MISC))
                    misc = c_tile(MISC)
                    g4, f4 = slice(ROW_I, ROW_I + ML_HEADS), slice(ROW_F, ROW_F + ML_HEADS)
                    done(dve.tensor_scalar(gate[g4, 0, :], misc[g4, :], gain(G_GATE_B, g4), None, ALU.add), gate_biased)
                    done(dve.tensor_scalar(gate[g4, 1, :], misc[f4, :], gain(G_GATE_B, f4), None, ALU.add), gate_biased)
                    r0, r1 = slice(ROW_R, ROW_R + MLA_ROPE), slice(ROW_RS, ROW_RS + MLA_ROPE)
                    done(dve.tensor_tensor(misc[r1, :], misc[r1, :], const(C_ROPE_Q, SEQ, r1), ALU.mult), dve_step)
                    done(dve.tensor_tensor(misc[r0, :], misc[r0, :], const(C_ROPE_Q, SEQ, r0), ALU.mult), dve_step)
                    done(dve.tensor_copy(w_ml[r0, 0, :], misc[r1, :]), dve_step)
                    done(dve.tensor_tensor(k_pe[r0, :], misc[r0, :], w_ml[r0, 0, :], ALU.add), dve_step)

                    def convolve(j):
                        wait_emptied(dve, use_of("in", ML[j]))
                        src, dst = conv_in[:, j % 2, :], ml_qk[:, j, :]
                        w = G_CONV_W + j * ML_CONV
                        done(dve.tensor_scalar(dst, src[:, 3:3 + SEQ], gain(w + 3), gain(G_CONV_B + j), ALU.mult,
                                               ALU.add), dve_step)
                        for tap in range(3):
                            done(dve.scalar_tensor_tensor(out=dst, in0=src[:, tap:tap + SEQ], scalar=gain(w + tap),
                                                          in1=dst, op0=ALU.mult, op1=ALU.add),
                                 conv_done if tap == 2 else dve_step)

                    def silu(j):
                        dve.wait_ge(conv_exp, j + 1)
                        e = conv_in[:, j % 2, 3:3 + SEQ]
                        done(dve.tensor_scalar(e, e, 1.0, None, ALU.add), dve_step)
                        done(dve.reciprocal(e, e), dve_step)
                        done(dve.tensor_tensor(ml_qk[:, j, :], ml_qk[:, j, :], e, ALU.mult), ml_qk_ready)

                    convolve(0)
                    dve.wait_ge(gate_log, 3)
                    done(dve.tensor_scalar(gate[g4, 1, :], gate[g4, 1, :], 0.0, None, ALU.min), dve_step)
                    done(dve.tensor_tensor(gate[g4, 1, :], gate[g4, 1, :], gate[g4, 3, :], ALU.subtract), dve_step)
                    done(dve.tensor_tensor_scan(gate[g4, 2, :], const(C_ONE_ROWS, SEQ, g4), gate[g4, 1, :], 0.0,
                                                ALU.mult, ALU.add), dve_step)
                    done(dve.tensor_tensor(gate[g4, 0, :], gate[g4, 0, :], gate[g4, 2, :], ALU.subtract), gate_rows)
                    done(dve.tensor_tensor_scan(gate[g4, 3, :], gate[g4, 0, :], gate[g4, 0, :], NEG,
                                                ALU.max, ALU.max), dve_step)
                    done(dve.tensor_scalar(gate[g4, 1, :], gate[g4, 3, :], -1.0, None, ALU.mult), gate_rows)
                    done(dve.tensor_tensor(gate[g4, 2, :], gate[g4, 1, :], gate[g4, 2, :], ALU.subtract), gate_rows)
                    silu(0)
                    convolve(1)
                    add_squares("q", 2)
                    silu(1)
                    convolve(2)
                    silu(2)
                    add_squares("kv", 1)
                    norm("q", 2, lambda k: c_tile(CQ[k]), G_Q, tiles(c_hi), tiles(c_lo))
                    convolve(3)
                    silu(3)
                    norm("kv", 1, lambda k: c_tile(CKV), G_KV, lambda k: c_hi[:, 2, :], lambda k: c_lo[:, 2, :])
                    for j in range(2):
                        wait_emptied(dve, use_of("in", OG + j))
                        done(dve.tensor_scalar(o_gate[:, j, :], o_gate[:, j, :], 1.0, None, ALU.add), dve_step)
                        done(dve.reciprocal(o_gate[:, j, :], o_gate[:, j, :]), dve_step)
                    dve.wait_ge(unit_used, U_INV + 4)
                    for b in range(TB):
                        half = ML_HEADS * ML_DK
                        done(dve.tensor_copy(ml_v[:, b, :, 0, :],
                                             wide[b][:, 0:half].rearrange("p (h d) -> p h d", h=ML_HEADS)), dve_step)
                        done(dve.tensor_copy(sw_v[:, b, :], wide[b][:, half:SEQ]), v_ready)

                    def rope_tile(j):
                        use = use_of("rot", j)
                        wait_tile(dve, use)
                        t = tn_mix[:, j % 2, :]
                        done(dve.tensor_tensor(t, dense[use % 2][:, :], const(C_SW_SIN, SEQ), ALU.mult), emptied_dve)
                        done(dve.tensor_tensor(sw_qk[:, j, :], sw_qk[:, j, :], const(C_SW_COS, SEQ), ALU.mult),
                             dve_step)
                        done(dve.tensor_tensor(sw_qk[:, j, :], sw_qk[:, j, :], t, ALU.add), roped)

                    def query_tile(h):
                        use = use_of("uq", h)
                        wait_tile(dve, use)
                        done(dve.tensor_tensor(q_mla[:, h, :], dense[use % 2][:, :], const(C_ROPE_Q, SEQ), ALU.mult),
                             emptied_dve)

                    dve.wait_ge(acol_turned, 1)
                    done(dve.tensor_copy(acol[:, :, :], outs[0][:, 0:TB * ML_HEADS]
                                         .rearrange("p (b h) -> p b h", h=ML_HEADS)), acol_ready)
                    ml_units = ML_HEADS * TB

                    def ml_finish(h):
                        r = slice(64 * (h % 2), 64 * (h % 2) + 64)
                        dve.wait_ge(ml_floor, h + 1)
                        dve.wait_ge(ml_abs, h + 1)
                        den = conv_in[64:128, 1, 0:SEQ]
                        done(dve.tensor_tensor(den, den, conv_in[64:128, 0, 0:SEQ], ALU.max), dve_step)
                        done(dve.reciprocal(conv_in[0:64, 1, 0:SEQ], den), dve_step)
                        done(dve.tensor_tensor(sq[r, 0, :], turned[h % 2][0:64, :], conv_in[0:64, 1, 0:SEQ],
                                               ALU.mult), dve_step)
                        done(dve.tensor_tensor(o_gate[r, h // 2, :], o_gate[r, h // 2, :], sq[r, 0, :], ALU.mult),
                             ml_out)

                    for u in range(ml_units + 5):
                        if 1 <= u <= ml_units:
                            v, n = u - 1, SEQ - (u - 1) % TB * P
                            dve.wait_ge(ml_exp, v + 1)
                            dve.wait_ge(ml_scored, v + 1)
                            done(dve.scalar_tensor_tensor(out=w_ml[:, v % 2, 0:n], in0=scores[v % 2][:, 0:n],
                                                          scalar=ML_DK ** -0.5, in1=w_ml[:, v % 2, 0:n],
                                                          op0=ALU.mult, op1=ALU.mult), ml_prob)
                        if 1 <= u <= ML_STEPS:
                            for name, m in completed(u - 1):
                                if name == "rot":
                                    rope_tile(m)
                                if name == "uq":
                                    query_tile(m)
                        if u < ml_units:
                            h, kb, n = u // TB, u % TB, SEQ - u % TB * P
                            if kb == 0:
                                dve.wait_ge(spread, h + 1)
                            if u >= 2:
                                dve.wait_ge(ml_num, u - 1)
                            done(dve.scalar_tensor_tensor(out=w_ml[:, u % 2, 0:n], in0=outs[0][:, kb * P:SEQ],
                                                          scalar=acol[:, kb, h:h + 1], in1=const(C_CAUSAL_T, n),
                                                          op0=ALU.add, op1=ALU.add), ml_weight)
                        if TB <= u <= ml_units + 1 and u % TB == 1:
                            ml_finish(u // TB - 1)
                        if u in (2 * TB + 4, ml_units + 4):
                            t = u // (2 * TB) - 1
                            dve.wait_ge(ml_hi, t + 1)
                            done(dve.tensor_tensor(h_lo[:, 4 + t, :], o_gate[:, t, :],
                                                   h_hi[:, 4 + t, :].bitcast(F32), ALU.subtract), ml_lo)

                    k_pe_rows = k_pe[r0, :].unsqueeze(1)
                    for rows in (r0, r1):
                        done(dve.tensor_copy(k_mla[rows, :, :],
                                             k_pe_rows.broadcast_to([MLA_ROPE, MLA_HEADS, SEQ])), k_pe_spread)
                    for b in range(TB):
                        use = use_of("uv", b)
                        wait_tile(dve, use)
                        done(dve.tensor_copy(v_mla[:, b, :], dense[use % 2][:, :]), emptied_dve)

                    def attention(a, heads, probs, klen, mask, scale, emit_lo):
                        n_units = heads * TB
                        for u in range(n_units + LAG + OUT_LAG):
                            if u < n_units:
                                n = klen(u % TB)
                                dve.wait_ge(a["scored"], u + 1)
                                if u >= PROBS:
                                    dve.wait_ge(a["turned"], u - PROBS + 1)
                                done(dve.tensor_tensor_reduce(
                                    probs[:, u % PROBS, 0:n], score_ring[u % 4][:, 0:n],
                                    const(mask(u // TB) + SEQ - n, n), -scale(u // TB), 3e38, ALU.add, ALU.min,
                                    stat[:, 0, u:u + 1]), a["masked"])
                            v = u - 1
                            if 0 <= v < n_units:
                                n = klen(v % TB)
                                dve.wait_ge(a["exped"], v + 1)
                                done(dve.reciprocal(stat[:, 2, v:v + 1], stat[:, 1, v:v + 1]), dve_step)
                                done(dve.tensor_scalar(probs[:, v % PROBS, 0:n], probs[:, v % PROBS, 0:n],
                                                       stat[:, 2, v:v + 1], None, ALU.mult), a["probs"])
                            w = u - LAG - OUT_LAG
                            if w >= 0 and w % TB == TB - 1:
                                emit_lo(w // TB)

                    def mix_lo(head):
                        hd = mix_head(head)
                        r = slice(hd["row"], hd["row"] + 64)
                        dve.wait_ge(mix_at["out_hi"], head + 1)
                        done(dve.tensor_tensor(h_lo[r, hd["tile"], :], outs[head % 2][0:64, :],
                                               h_hi[r, hd["tile"], :].bitcast(F32), ALU.subtract), mix_at["out_lo"])

                    attention(mix_at, MIX_HEADS, p_mix, causal_len, lambda h: mix_head(h)["mask"],
                              lambda h: mix_head(h)["scale"], mix_lo)

                    dve.wait_ge(mem_loaded, 16)
                    mem_norm = (KT, tiles(mem), G_MEM, tiles(m_hi), tiles(m_lo))
                    add_squares("mix_post", KT, between=lambda m: norm_step("mem", m, *mem_norm))
                    norm_step("mem", KT, *mem_norm)
                    residual("mix_post", "out", y_x, G_MIX_POST)
                    add_squares("x_pre", KT)
                    norm("x_pre", KT, tiles(x), G_X_PRE, tiles(h_hi), tiles(h_lo))
                    for half in range(2):
                        dve.wait_ge(unit_used, U_XV + 4 * half + 4)
                        for b in range(2):
                            done(dve.tensor_copy(v_x[:, b, half * SEQ:(half + 1) * SEQ], wide[2 * half + b][:, :]),
                                 xv_ready)

                    def x_lo(head):
                        for c in range(2):
                            dve.wait_ge(x_at["out_hi"], 2 * head + c + 1)
                            done(dve.tensor_tensor(h_lo[:, 2 * head + c, :], outs[c][:, :],
                                                   h_hi[:, 2 * head + c, :].bitcast(F32), ALU.subtract),
                                 x_at["out_lo"])

                    attention(x_at, X_HEADS, p_x, lambda qb: N_MEM, lambda h: C_CAUSAL - (SEQ - N_MEM),
                              lambda h: X_HD ** -0.5, x_lo)
                    add_squares("x_post", KT)

                    def ffn_input(k):
                        if k >= 1:
                            scaled_lo("ffn_pre", k - 1, G_FFN_PRE)
                            add_square("ffn_pre", k - 1)

                    residual("x_post", "xo", y_x, G_X_POST, ffn_input)
                    ffn_input(KT)

                    def ff_turn(j):
                        for i in range(2):
                            e, gate_up = f_e[:, :], f_a[:, i, :]

                            def step(ins, k):
                                ins.then_inc(ff_step, 1)
                                dve.wait_ge(ff_step, j * 8 + (4 * i + k))

                            dve.wait_ge(unit_used, j * 4 + (U_FF + 2 * i + 1))
                            dve.tensor_tensor(gate_up, ff_bank[2 * i][:, :], rstd[:, :], ALU.mult)\
                               .then_inc(ff_gate, 1)
                            dve.wait_ge(ff_exp, j * 2 + (i + 1))
                            step(dve.tensor_scalar(e, e, 1.0, None, ALU.add), 1)
                            step(dve.reciprocal(e, e), 2)
                            step(dve.tensor_tensor(e, gate_up, e, ALU.mult), 3)
                            step(dve.tensor_tensor(e, e, rstd[:, :], ALU.mult), 4)
                            dve.wait_ge(unit_used, j * 4 + (U_FF + 2 * i + 2))
                            dve.tensor_tensor(gate_up, ff_bank[2 * i + 1][:, :], e, ALU.mult).then_inc(ff_a, 1)
                            dve.wait_ge(ff_hi, j * 2 + (i + 1))
                            at = bass.ds(j * (2 * SEQ) + i * SEQ, SEQ)
                            dve.tensor_tensor(a_lo[:, at], gate_up, a_hi[:, at].bitcast(F32), ALU.subtract)\
                               .then_inc(ff_lo, 1)
                            dve.wait_ge(ff_lo, j * 2 + (i + 1))

                    dve.wait_ge(rstd_ready, NORM_AT["ffn_pre"] + 1)
                    ff_turn(0)
                    with dve.Fori(1, FT // 2) as j:
                        ff_turn(j)
                    add_squares("ffn_post", KT)
                    residual("ffn_post", "down", y_f, G_FFN_POST)

            with nc.Block() as block:
                @block.sync
                def _(sp):
                    for s in layer_sems:
                        sp.sem_clear(s)

        with nc.Block() as block:
            @block.sync
            def _(sp):
                sp.dma_start(out, x[:, :, :]).then_inc(stored, 16)
                sp.wait_ge(stored, 16)


def constants():
    c = np.zeros((P, N_CONST), np.float32)

    def tables(d):
        inv = np.float32(ROPE_THETA) ** (-np.arange(0, d, 2, dtype=np.float32) / np.float32(d))
        ang = inv.astype(np.float32)[:, None] * np.arange(SEQ, dtype=np.float32)[None, :]
        cos, sin = np.cos(ang).astype(np.float32), np.sin(ang).astype(np.float32)
        return np.concatenate([cos, cos]), np.concatenate([-sin, sin])

    cos, sin = tables(MLA_ROPE)
    c[0:MLA_NOPE, C_ROPE_Q:C_ROPE_Q + SEQ] = 1.0
    c[ROW_R:ROW_R + MLA_ROPE, C_ROPE_Q:C_ROPE_Q + SEQ] = cos
    c[ROW_RS:ROW_RS + MLA_ROPE, C_ROPE_Q:C_ROPE_Q + SEQ] = sin
    cos, sin = tables(SW_ROT)
    c[:, C_SW_COS:C_SW_COS + SEQ] = 1.0
    for r in (0, SW_HD):
        c[r:r + SW_ROT, C_SW_COS:C_SW_COS + SEQ] = cos
        c[r:r + SW_ROT, C_SW_SIN:C_SW_SIN + SEQ] = sin
        for i in range(SW_ROT):
            c[r + (i + SW_ROT // 2) % SW_ROT, C_ROT + r + i] = 1.0
    t, s = np.arange(P)[:, None] + SEQ - P, np.arange(SEQ)[None, :]
    d = t - s
    c[:, C_CAUSAL:C_CAUSAL + SEQ] = np.where(d >= 0, 0.0, NEG)
    count = sum(((d >= 0) & (d % dil == 0) & (d // dil <= win // dil)).astype(np.float64) for win, dil in SW_CONFIGS)
    c[:, C_DILATED:C_DILATED + SEQ] = np.where(count > 0, np.log(np.maximum(count, 1)) * SW_HD ** 0.5, NEG)
    c[:, C_CAUSAL_T:C_CAUSAL_T + SEQ] = np.where(np.arange(P)[:, None] <= np.arange(SEQ)[None, :], 0.0, NEG)
    c[:, C_IDENT:C_IDENT + P] = np.eye(P)
    c[:, C_ONES:C_ONES + P] = 1.0
    return c


def swap_halves(w):
    half = w.shape[-1] // 2
    return np.concatenate([w[..., half:], w[..., :half]], axis=-1)


def weight_stream(i):
    w = np.zeros((DEPTH, N_UNITS, P, UNIT), np.float32)

    def whole(u0, mat):
        n = mat.shape[2] // P
        w[:, u0:u0 + n] = mat.reshape(DEPTH, KT, P, n, P).transpose(0, 3, 2, 1, 4).reshape(DEPTH, n, P, UNIT)

    def token_major(u0, mat):
        w[:, u0:u0 + 4] = mat.reshape(DEPTH, 4, 2, P, SEQ).transpose(0, 1, 3, 2, 4).reshape(DEPTH, 4, P, UNIT)

    names = ("c_q", "c_kv", "k_rope", "ml_q", "ml_k", "ml_v", "ml_o", "ml_i", "ml_f", "sw_q", "sw_k", "sw_v")
    sizes = (MLA_Q_LORA, MLA_KV_LORA, MLA_ROPE, 256, 256, 256, 256, ML_HEADS, ML_HEADS, 256, 256, 256)
    part = dict(zip(names, np.split(i["w_in"], np.cumsum(sizes)[:-1], axis=2)))
    misc = np.zeros((DEPTH, D_MODEL, P), np.float32)
    misc[:, :, ROW_I:ROW_I + ML_HEADS] = part["ml_i"]
    misc[:, :, ROW_F:ROW_F + ML_HEADS] = part["ml_f"]
    misc[:, :, ROW_R:ROW_R + MLA_ROPE] = part["k_rope"]
    misc[:, :, ROW_RS:ROW_RS + MLA_ROPE] = swap_halves(part["k_rope"])
    order = {MISC: misc, CKV: part["c_kv"]}
    for tiles_at, mat in ((CQ, part["c_q"]), (ML, np.concatenate([part["ml_q"], part["ml_k"]], axis=2)),
                          ((OG, OG + 1), part["ml_o"])):
        for n, m in enumerate(tiles_at):
            order[m] = mat[:, :, n * P:(n + 1) * P]
    whole(U_IN, np.concatenate([order[m] for m in range(IN_FM)], axis=2))
    whole(U_SW, np.concatenate([part["sw_q"], part["sw_k"]], axis=2))
    token_major(U_INV, np.concatenate([part["ml_v"], part["sw_v"]], axis=2))
    uq = i["mla_w_uq"].reshape(DEPTH, 2, P, MLA_HEADS, MLA_NOPE + MLA_ROPE)
    uq = np.concatenate([uq, swap_halves(uq[..., MLA_NOPE:])], axis=4)
    w[:, U_UQ:U_UQ + 2] = uq.reshape(DEPTH, 2, P, 2, 4, P).transpose(0, 3, 2, 4, 1, 5).reshape(DEPTH, 2, P, UNIT)
    ukv = i["mla_w_ukv"].reshape(DEPTH, P, MLA_HEADS, MLA_NOPE + MLA_V)
    w[:, U_UK, :, 0:SEQ] = ukv[..., :MLA_NOPE].reshape(DEPTH, P, SEQ)
    w[:, U_UV, :, 0:SEQ] = ukv[..., MLA_NOPE:].reshape(DEPTH, P, SEQ)
    whole(U_OUT, i["w_out"])
    whole(U_XK, i["x_w_kv"][:, :, :D_MODEL])
    for half in range(2):
        a = D_MODEL + half * SEQ
        token_major(U_XV + 4 * half, i["x_w_kv"][:, :, a:a + SEQ])
    whole(U_XQ, i["x_w_q"])
    whole(U_XO, i["x_w_o"])
    gu = i["w_gate_up"].reshape(DEPTH, D_MODEL, 2, FT, P).transpose(0, 1, 3, 2, 4).reshape(DEPTH, D_MODEL, -1)
    whole(U_FF, gu)
    down = i["w_down"].reshape(DEPTH, FT, P, KT, P).transpose(0, 3, 1, 2, 4).reshape(DEPTH, FT, KT, P, P)
    w[:, U_DOWN:U_DOWN + FT] = down.transpose(0, 1, 3, 2, 4).reshape(DEPTH, FT, P, UNIT)
    return w


def gain_columns(i):
    g = np.zeros((DEPTH, P, N_GAINS), np.float32)

    def put(col, v):
        n = v.shape[1] // P
        g[:, :, col:col + n] = v.reshape(DEPTH, n, P).transpose(0, 2, 1)

    for col, name in ((G_MIX_PRE, "norm_mix_pre"), (G_MIX_POST, "norm_mix_post"), (G_MEM, "norm_mem"),
                      (G_X_PRE, "norm_x_pre"), (G_X_POST, "norm_x_post"), (G_FFN_PRE, "norm_ffn_pre"),
                      (G_FFN_POST, "norm_ffn_post"), (G_Q, "mla_q_norm"), (G_KV, "mla_kv_norm"),
                      (G_CONV_B, "ml_conv_b")):
        put(col, i[name])
    taps = i["ml_conv_w"].reshape(DEPTH, ML_CONV, 4, P).transpose(0, 3, 2, 1)
    g[:, :, G_CONV_W:G_CONV_W + 4 * ML_CONV] = taps.reshape(DEPTH, P, 4 * ML_CONV)
    g[:, ROW_I:ROW_I + ML_HEADS, G_GATE_B] = i["ml_b_i"]
    g[:, ROW_F:ROW_F + ML_HEADS, G_GATE_B] = i["ml_b_f"]
    return g


def feature_major(a):
    return np.ascontiguousarray(a[0].reshape(a.shape[1], KT, P).transpose(2, 1, 0))


def kernel(**inputs):
    import concourse.bacc as bacc
    from concourse.bass_utils import run_bass_kernel_spmd

    i = {k: np.asarray(v) for k, v in inputs.items()}
    nc = bacc.Bacc("TRN2", target_bir_lowering=False, num_devices=1)
    arrays = {"x_in": feature_major(i["x"]), "mem_in": feature_major(i["mem"]), "w_in": weight_stream(i),
              "g_in": gain_columns(i), "c_in": constants()}
    args = [nc.dram_tensor(n, a.shape, F32, kind="ExternalInput").ap() for n, a in arrays.items()]
    out = nc.dram_tensor("out", (P, KT, SEQ), F32, kind="ExternalOutput").ap()
    build(nc, *args, out)
    r = run_bass_kernel_spmd(nc, [arrays], core_ids=[0])
    y = r.results[0]["out"]
    return np.ascontiguousarray(y.transpose(2, 1, 0)).reshape(1, SEQ, D_MODEL)
```

```python
from contextlib import ExitStack

import numpy as np
import concourse.bass as bass
from concourse import mybir

F32 = mybir.dt.float32
F32R = mybir.dt.float32r
ALU = mybir.AluOpType
ACT = mybir.ActivationFunctionType

P = 128
D_MODEL = 1024
SEQ = 512
DEPTH = 2
N_MEM = 256
ROPE_THETA = 500000.0
EPS = 1e-6
NEG = -1e30

MLA_HEADS, MLA_NOPE, MLA_ROPE, MLA_V = 8, 64, 32, 64
MLA_Q_LORA, MLA_KV_LORA = 256, 128
ML_HEADS, ML_DK, ML_CONV = 4, 64, 4
SW_HEADS, SW_HD = 4, 64
SW_ROT = SW_HD // 4
SW_CONFIGS = ((128, 1), (512, 4), (2048, 16))
X_HEADS = 4
X_HD = D_MODEL // X_HEADS
D_FF = 2816

KT = D_MODEL // P
TB = SEQ // P
FT = D_FF // P
UNIT = KT * P

U_IN = 0
MISC, CKV, OG = 0, 6, 8
ML = (1, 3, 5, 7)
CQ = (2, 4)
IN_FM = 10
U_INV = U_IN + IN_FM
U_SW = U_INV + 4
U_UQ = U_SW + 4
U_UK = U_UQ + 2
U_UV = U_UK + 1
U_OUT = U_UV + 1
U_XK = U_OUT + 8
U_XV = U_XK + 8
U_XQ = U_XV + 8
U_XO = U_XQ + 8
U_FF = U_XO + 8
U_DOWN = U_FF + 2 * FT
N_UNITS = U_DOWN + FT
RING = 4
AHEAD = 2
POOL_ADDS = (1, 3, 4, 6)
LAG = 3
PROBS = LAG + 1
OUT_LAG = 2

G_MIX_POST, G_MEM, G_X_PRE, G_X_POST, G_FFN_PRE, G_FFN_POST = (KT * i for i in range(6))
G_Q = 6 * KT
G_KV = G_Q + 2
G_CONV_W = G_KV + 1
G_CONV_B = G_CONV_W + 4 * ML_CONV
G_GATE_B = G_CONV_B + 4
N_GAINS = G_GATE_B + 1

C_ROPE_Q = 0
C_SW_COS = C_ROPE_Q + SEQ
C_SW_SIN = C_SW_COS + SEQ
C_CAUSAL = C_SW_SIN + SEQ
C_DILATED = C_CAUSAL + SEQ
C_CAUSAL_T = C_DILATED + SEQ
C_IDENT = C_CAUSAL_T + SEQ
C_ROT = C_IDENT + P
C_ONES = C_ROT + P
N_CONST = C_ONES + P

ROW_I, ROW_F, ROW_R, ROW_RS = 0, 32, 64, 96
K_PE_ROWS = slice(ROW_R, ROW_R + MLA_ROPE), slice(ROW_RS, ROW_RS + MLA_ROPE)


def tile_plan():
    plan, uses = {}, []

    def add(name, sub, engine):
        plan.setdefault(name, []).append((len(uses), sub))
        uses.append((sub, engine))

    def whole(name, u0, n, engine="act"):
        for m in range(n):
            add(name, [(u0 + m, k * P) for k in range(KT)], engine)

    def query(h):
        add("uq", [(U_UQ + h // 4, ((h % 4) * 2 + k) * P) for k in range(2)], "dve")

    def rotation():
        add("rot", [], "dve")

    whole("in", U_IN, IN_FM, "dve")
    whole("sw", U_SW, 2, "dve")
    rotation()
    whole("sw", U_SW + 2, 1, "dve")
    rotation()
    whole("sw", U_SW + 3, 1, "dve")
    rotation()
    query(0)
    rotation()
    for h in range(1, MLA_HEADS):
        query(h)
    for m in range(4):
        add("uk", [(U_UK, m * P)], "act")
    for _ in range(TB):
        add("uv", [(U_UV, 0)], "dve")
    whole("out", U_OUT, KT)
    whole("xk", U_XK, KT)
    whole("xq", U_XQ, KT)
    whole("xo", U_XO, KT)
    for m in range(KT):
        add("down", [(U_DOWN + (m * FT + k) // KT, (m * FT + k) % KT * P) for k in range(FT)], "act")
    return plan, uses


PLAN, USES = tile_plan()


def ends_unit(use):
    sub = USES[use][0]
    return bool(sub) and all(later[0][0] > sub[-1][0] for later, _ in USES[use + 1:] if later)


def tiles_done(use):
    return sum(not ends_unit(u) for u in range(use + 1))


def emptied(use):
    engine = USES[use][1]
    return engine, sum(e == engine for _, e in USES[:use + 1])


ML_STEPS = ML_HEADS * TB + 1
BETWEEN = [(name, m, k) for use in range(PLAN["sw"][1][0], PLAN["uk"][0][0])
           for name in ("sw", "rot", "uq") for m, (at, sub) in enumerate(PLAN[name]) if at == use
           for k in range(max(len(sub), 1))]


def between(step):
    return BETWEEN[len(BETWEEN) * step // ML_STEPS:len(BETWEEN) * (step + 1) // ML_STEPS]


def completed(step):
    return [(name, m) for name, m, k in between(step) if k + 1 == max(len(PLAN[name][m][1]), 1)]


def units_through(step):
    done = [USES[PLAN[name][m][0]][0][-1][0] + 1 for t in range(step + 1) for name, m in completed(t)
            if name != "rot" and ends_unit(PLAN[name][m][0])]
    return max(done, default=U_SW + 1)


NORMS = [("mix_pre", KT), ("q", 2), ("kv", 1), ("mix_post", KT), ("x_pre", KT), ("x_post", KT),
         ("ffn_pre", KT), ("ffn_post", KT)]
NORM_AT = {name: i for i, (name, _) in enumerate(NORMS)}
NORMED = [("mix_pre", KT), ("q", 2), ("kv", 1), ("mem", KT), ("x_pre", KT), ("ffn_pre", KT)]
POST = ("mix_post", "x_post", "ffn_post")
LATE_RMS = ("mix_pre", "ffn_pre")


def squares_before(name):
    return sum(k for _, k in NORMS[:NORM_AT[name]])


def normed_before(name):
    if name in POST:
        name = {"mix_post": "x_pre", "x_post": "ffn_pre"}.get(name)
        if name is None:
            return sum(k for _, k in NORMED)
    return sum(k for _, k in NORMED[:[n for n, _ in NORMED].index(name)])


def tn_before(name):
    first = normed_before(name)
    return first - sum(k for n, k in NORMED if n in LATE_RMS and normed_before(n) < first)


def scaled_before(name):
    return sum(k for n, k in NORMS[:NORM_AT[name]] if n in POST)


def each_unit(eng, first, end, emit):
    a, b = -(-first // RING) * RING, end // RING * RING
    for n in range(first, min(a, end)):
        emit(0, n)
    if b > a:
        with eng.Fori(a // RING, b // RING) as j:
            for n in range(RING):
                emit(j, n)
    for n in range(max(a, b), end):
        emit(0, n)


def build(nc, x_in, mem_in, first_in, first_g_in, w_in, g_in, c_in, out):
    with ExitStack() as ctx:
        layer_sems = []

        def sb(name, shape, dt=F32, stack=ctx):
            return stack.enter_context(nc.sbuf_tensor(name, shape, dt))

        def sem(name):
            s = ctx.enter_context(nc.semaphore(name))
            layer_sems.append(s)
            return s

        x = sb("x", [P, KT, SEQ])
        consts = sb("consts", [P, N_CONST])
        eps = sb("eps", [P, 1])
        one = sb("one", [P, 1])
        first_g = sb("first_g", [P, KT])
        rcol = sb("rcol", [P, TB])
        gains = sb("gains", [P, N_GAINS])
        raw = sb("raw", [P, RING, UNIT])
        w_hi = sb("w_hi", [P, RING, UNIT], F32R)
        w_lo = sb("w_lo", [P, RING, UNIT], F32R)
        with ExitStack() as late:
            y_f = sb("y_f", [P, KT, SEQ], F32, late)
        h_hi = sb("h_hi", [P, KT, SEQ], F32R)
        h_lo = sb("h_lo", [P, KT, SEQ], F32R)
        sq = sb("sq", [P, 2, SEQ])
        acc = sb("acc", [P, SEQ])
        rstd = sb("rstd", [P, SEQ])
        mem_rstd = sb("mem_rstd", [P, N_MEM])
        stat = sb("stat", [P, 3, 64])
        acol = sb("acol", [P, TB, ML_HEADS])

        with ExitStack() as room:
            tn_mix = sb("tn_mix", [P, 2, SEQ], F32, room)
            q_mla = sb("q_mla", [P, MLA_HEADS, SEQ], F32, room)
            with ExitStack() as early:
                ml_qk = sb("ml_qk", [P, 4, SEQ], F32, early)
                ml_v = sb("ml_v", [P, TB, ML_HEADS, 2, ML_DK], F32, early)
                gate = sb("gate", [P, 4, SEQ], F32, early)
            k_mla = sb("k_mla", [P, MLA_HEADS, SEQ], F32, room)
            v_mla = sb("v_mla", [P, TB, MLA_HEADS * MLA_V], F32, room)
            k_pe = sb("k_pe", [P, SEQ], F32, room)
            mix_rstd = sb("mix_rstd", [P, SEQ], F32, room)
            sw_qk = sb("sw_qk", [P, 4, SEQ], F32, room)
            sw_v = sb("sw_v", [P, TB, SW_HEADS * SW_HD], F32, room)
            o_gate = sb("o_gate", [P, 2, SEQ], F32, room)
            with ExitStack() as early:
                c_hi = sb("c_hi", [P, 3, SEQ], F32R, early)
                c_lo = sb("c_lo", [P, 3, SEQ], F32R, early)
                conv_in = sb("conv_in", [P, 2, SEQ + 4], F32, early)
                w_ml = sb("w_ml", [P, 2, SEQ], F32, early)
                ml_den = sb("ml_den", [P, SEQ // 2], F32, early)
            p_mix = sb("p_mix", [P, PROBS, SEQ], F32, room)
            pt_mix = sb("pt_mix", [P, 2, TB, SEQ], F32, room)
        with ExitStack() as room:
            tn_x = sb("tn_x", [P, 2, SEQ], F32, room)
            y_x = sb("y_x", [P, KT, SEQ], F32, room)
            mem = sb("mem", [P, KT, N_MEM], F32, room)
            with ExitStack() as first:
                mem_sq = sb("mem_sq", [P, KT, N_MEM], F32, first)
                ones_first = sb("ones_first", [P, P], F32, first)
            m_hi = sb("m_hi", [P, KT, N_MEM], F32R, room)
            m_lo = sb("m_lo", [P, KT, N_MEM], F32R, room)
            q_x = sb("q_x", [P, KT, SEQ], F32, room)
            k_x = sb("k_x", [P, KT, N_MEM], F32, room)
            v_x = sb("v_x", [P, 2, D_MODEL], F32, room)
            p_x = sb("p_x", [P, PROBS, N_MEM], F32, room)
            pt_x = sb("pt_x", [P, 2, 2, SEQ], F32, room)
        with ExitStack() as room:
            a_hi = sb("a_hi", [P, FT * SEQ], F32R, room)
            a_lo = sb("a_lo", [P, FT * SEQ], F32R, room)
        tn_of = {"mix_pre": tn_mix, "q": tn_mix, "kv": tn_mix, "mem": tn_x, "x_pre": tn_x}
        f_e, f_a = acc, sq

        bank = [ctx.enter_context(nc.psum_tensor(f"bank{i}", [P, SEQ], F32)) for i in range(8)]
        dense = bank[0:2]
        wide = bank[2:6]
        scores, turned = bank[2:4], bank[4:6]
        score_ring = bank[2:4] + bank[0:2]
        outs = bank[6:8]
        norm_bank = bank[7]
        ff_bank = bank[0:4]

        mem_first, x_loaded, consts_loaded, mem_squared, mem_summed, mem_ln = (
            ctx.enter_context(nc.semaphore(n)) for n in ("mem_first", "x_loaded", "consts_loaded", "mem_squared",
                                                         "mem_summed", "mem_ln"))
        fixed_set = ctx.enter_context(nc.semaphore("fixed_set"))
        stored = ctx.enter_context(nc.semaphore("stored"))
        first_loaded = [ctx.enter_context(nc.semaphore(f"first_loaded{i}")) for i in range(RING)]
        first_g_loaded, first_hi, first_lo = (ctx.enter_context(nc.semaphore(n)) for n in (
            "first_g_loaded", "first_hi", "first_lo"))
        raw_loaded = [sem(f"raw_loaded{i}") for i in range(RING)]
        gains_loaded, mem_loaded = sem("gains_loaded"), sem("mem_loaded")
        split_hi, split_lo = sem("split_hi"), sem("split_lo")
        unit_used, tile_done = sem("unit_used"), sem("tile_done")
        emptied_act, emptied_dve = sem("emptied_act"), sem("emptied_dve")
        squared, squares_added = sem("squared"), sem("squares_added")
        norm_summed, ln_done, rstd_ready = sem("norm_summed"), sem("ln_done"), sem("rstd_ready")
        normed, normed_hi, normed_lo = sem("normed"), sem("normed_hi"), sem("normed_lo")
        y_scaled, x_updated, x_added = sem("y_scaled"), sem("x_updated"), sem("x_added")
        dve_step, act_step = sem("dve_step"), sem("act_step")
        pads_set = sem("pads_set")
        conv_done, conv_exp, ml_qk_ready = sem("conv_done"), sem("conv_exp"), sem("ml_qk_ready")
        gate_biased, gate_log, gate_rows = sem("gate_biased"), sem("gate_log"), sem("gate_rows")
        acol_turned, acol_ready = sem("acol_turned"), sem("acol_ready")
        rcol_turned, rcol_ready = sem("rcol_turned"), sem("rcol_ready")
        k_pe_ready, k_pe_spread, k_pe_rest = sem("k_pe_ready"), sem("k_pe_spread"), sem("k_pe_rest")
        k_pe_copied = sem("k_pe_copied")
        roped, o_exp, v_ready = sem("roped"), sem("o_exp"), sem("v_ready")
        spread, ml_scored, ml_weight, ml_exp, ml_prob, ml_num = (
            sem("spread"), sem("ml_scored"), sem("ml_weight"), sem("ml_exp"), sem("ml_prob"), sem("ml_num"))
        ml_floor, ml_abs, ml_out, ml_hi, ml_lo = (
            sem("ml_floor"), sem("ml_abs"), sem("ml_out"), sem("ml_hi"), sem("ml_lo"))
        mix_at, x_at = ({n: sem(f"{c}_{n}") for n in ("scored", "masked", "exped", "probs", "turned", "copied",
                                                      "out", "out_hi", "out_lo")} for c in ("mix", "x"))
        xv_ready = sem("xv_ready")
        ff_gate, ff_exp, ff_step = sem("ff_gate"), sem("ff_exp"), sem("ff_step")
        ff_a, ff_hi, ff_lo = sem("ff_a"), sem("ff_hi"), sem("ff_lo")

        def const(col, n=P, rows=slice(0, P)):
            return consts[rows, col:col + n]

        def gain(col, rows=slice(0, P)):
            return gains[rows, col:col + 1]

        def use_of(name, m):
            return PLAN[name][m][0]

        def wait_tile(eng, use):
            if ends_unit(use):
                eng.wait_ge(unit_used, USES[use][0][-1][0] + 1)
            else:
                eng.wait_ge(tile_done, tiles_done(use))

        def wait_emptied(eng, use):
            engine, count = emptied(use)
            eng.wait_ge(emptied_act if engine == "act" else emptied_dve, count)

        def wait_split(eng, layer, u, j=0):
            if isinstance(j, int) and u < AHEAD:
                eng.wait_ge(first_lo, layer * AHEAD + (u + 1))
            else:
                eng.wait_ge(split_lo, j * RING + (u + 1 - AHEAD))

        def wait_x(eng, name, k):
            if name == "mix_post":
                eng.wait_ge(x_updated, k + 1)
            elif k in POOL_ADDS:
                eng.wait_ge(x_added, POOL_ADDS.index(k) + 1)
            else:
                eng.wait_ge(x_updated, KT + sum(i not in POOL_ADDS for i in range(k + 1)))

        def counter(eng):
            counts = {}

            def done(ins, s):
                counts[s.name] = counts.get(s.name, 0) + 1
                ins.then_inc(s, 1)
                eng.wait_ge(s, counts[s.name])
            return done

        def c_tile(m):
            return q_mla[:, m // 2, :]

        MIX_HEADS = MLA_HEADS + SW_HEADS

        def mix_head(n):
            if n < MLA_HEADS:
                return dict(q=q_mla[:, n, :], k=k_mla[:, n, :], v=lambda kb: v_mla[:, kb, n * MLA_V:(n + 1) * MLA_V],
                            mask=C_CAUSAL, scale=(MLA_NOPE + MLA_ROPE) ** -0.5, tile=n // 2, row=64 * (n % 2))
            h = n - MLA_HEADS
            r = slice(64 * (h % 2), 64 * (h % 2) + 64)
            return dict(q=sw_qk[r, h // 2, :], k=sw_qk[r, 2 + h // 2, :],
                        v=lambda kb: sw_v[:, kb, h * SW_HD:(h + 1) * SW_HD],
                        mask=C_DILATED, scale=SW_HD ** -0.5, tile=6 + h // 2, row=64 * (h % 2))

        def causal_len(qb):
            return (qb + 1) * P

        with nc.Block() as block:
            @block.sync
            def _(sp):
                sp.dma_start(mem[:, :, :], mem_in).then_inc(mem_first, 16)
                sp.dma_start(first_g[:, :], first_g_in[0, :, :]).then_inc(first_g_loaded, 16)
                for s in range(AHEAD):
                    sp.dma_start(raw[:, s, :], first_in[0, s, :, :]).then_inc(first_loaded[s], 16)
                sp.dma_start(x[:, :, :], x_in).then_inc(x_loaded, 16)
                sp.dma_start(consts[:, :], c_in).then_inc(consts_loaded, 16)
                for s in range(AHEAD, RING):
                    sp.dma_start(raw[:, s, :], first_in[0, s, :, :]).then_inc(first_loaded[s], 16)

            @block.gpsimd
            def _(pool):
                for s in range(AHEAD):
                    pool.wait_ge(first_hi, s + 1)
                    pool.tensor_tensor(w_lo[:, s, :], raw[:, s, :], w_hi[:, s, :].bitcast(F32), ALU.subtract)\
                        .then_inc(first_lo, 1)

            @block.vector
            def _(dve):
                dve.memset(eps[:, :], EPS).then_inc(fixed_set, 1)
                dve.memset(one[:, :], 1.0).then_inc(fixed_set, 1)
                dve.memset(ones_first[:, :], 1.0).then_inc(fixed_set, 1)
                dve.wait_ge(fixed_set, 3)

            @block.scalar
            def _(act):
                act.preload_act_table_set("natural_log_exp_and_others")
                act.wait_ge(mem_first, 16)
                act.activation(mem_sq[:, :, :], mem[:, :, :], ACT.Square).then_inc(mem_squared, 1)
                for s in range(AHEAD):
                    act.wait_ge(first_loaded[s], 16)
                    act.activation(w_hi[:, s, :], raw[:, s, :], ACT.Copy).then_inc(first_hi, 1)
                act.wait_ge(fixed_set, 3)
                act.wait_ge(mem_summed, 1)
                act.activation(mem_rstd[:, :], bank[0][:, 0:N_MEM], ACT.Ln, bias=eps[:, :], scale=1.0 / D_MODEL)\
                   .then_inc(mem_ln, 1)
                act.wait_ge(mem_ln, 1)
                act.activation(mem_rstd[:, :], mem_rstd[:, :], ACT.Exp, scale=-0.5).then_inc(mem_ln, 1)
                act.wait_ge(mem_ln, 2)

            @block.tensor
            def _(pe):
                pe.wait_ge(fixed_set, 3)
                pe.wait_ge(mem_squared, 1)
                for k in range(KT):
                    mm = pe.matmul(bank[0][:, 0:N_MEM], ones_first[:, :], mem_sq[:, k, :], start=(k == 0),
                                   stop=(k == KT - 1))
                mm.then_inc(mem_summed, 1)

        with nc.Fori(0, DEPTH) as layer:
            with nc.Block() as block:

                @block.sync
                def _(sp):
                    sp.dma_start(gains[:, :], g_in[layer, :, :]).then_inc(gains_loaded, 16)

                    def load(j, n):
                        if n >= RING + AHEAD or not isinstance(j, int):
                            wait_split(sp, layer, n - RING, j)
                        sp.dma_start(raw[:, n % RING, :], w_in[layer, j * RING + (n - RING), :, :])\
                          .then_inc(raw_loaded[n % RING], 16)

                    mid = -(-U_OUT // RING) * RING + RING
                    for n in range(RING, 2 * RING):
                        load(0, n)
                    each_unit(sp, 2 * RING, mid, load)
                    sp.wait_ge(mix_at["out_lo"], MIX_HEADS)
                    sp.dma_start(mem[:, :, :], mem_in).then_inc(mem_loaded, 16)
                    each_unit(sp, mid, N_UNITS, load)
                    for s in range(RING):
                        wait_split(sp, layer, N_UNITS - RING + s)
                        sp.dma_start(raw[:, s, :], first_in[layer + 1, s, :, :]).then_inc(first_loaded[s], 16)
                    sp.dma_start(first_g[:, :], first_g_in[layer + 1, :, :]).then_inc(first_g_loaded, 16)

                @block.gpsimd
                def _(pool):
                    def make_lo(j, n):
                        pool.wait_ge(split_hi, j * RING + (n + 1 - AHEAD))
                        s = n % RING
                        pool.tensor_tensor(w_lo[:, s, :], raw[:, s, :], w_hi[:, s, :].bitcast(F32),
                                           ALU.subtract).then_inc(split_lo, 1)

                    def add_tiles(name, y):
                        for k in POOL_ADDS:
                            pool.wait_ge(y_scaled, scaled_before(name) + k + 1)
                            pool.tensor_tensor(x[:, k, :], x[:, k, :], y[:, k, :], ALU.add).then_inc(x_added, 1)

                    each_unit(pool, AHEAD, U_OUT + 2, make_lo)
                    pool.wait_ge(k_pe_ready, 1)
                    pool.wait_ge(ml_num, ML_HEADS * TB)
                    wait_split(pool, layer, U_OUT + 1)
                    pool.tensor_copy(k_mla[K_PE_ROWS[0], 2:MLA_HEADS, :], k_pe[K_PE_ROWS[0], :].unsqueeze(1)
                                     .broadcast_to([MLA_ROPE, MLA_HEADS - 2, SEQ])).then_inc(k_pe_copied, 1)
                    pool.wait_ge(k_pe_copied, 1)
                    each_unit(pool, U_OUT + 2, U_FF + RING, make_lo)
                    add_tiles("x_post", y_x)
                    each_unit(pool, U_FF + RING, N_UNITS, make_lo)
                    for s in range(AHEAD):
                        pool.wait_ge(first_hi, layer * AHEAD + (AHEAD + s + 1))
                        pool.tensor_tensor(w_lo[:, s, :], raw[:, s, :], w_hi[:, s, :].bitcast(F32),
                                           ALU.subtract).then_inc(first_lo, 1)
                    add_tiles("ffn_post", y_f)

                @block.tensor
                def _(pe):
                    def three(out_ap, l_hi, l_lo, r_hi, r_lo, start, stop):
                        pe.matmul(out_ap, l_hi, r_hi, start=start, stop=False)
                        pe.matmul(out_ap, l_hi, r_lo, start=False, stop=False)
                        return pe.matmul(out_ap, l_lo, r_hi, start=False, stop=stop)

                    def project_step(name, m, k, act_hi, act_lo, width=SEQ):
                        use, subs = PLAN[name][m]
                        (u, col), last = subs[k], k == len(subs) - 1
                        if k == 0 and use >= 2:
                            wait_emptied(pe, use - 2)
                        if k == 0 or subs[k - 1][0] != u:
                            wait_split(pe, layer, u)
                        w = slice(col, col + P)
                        mm = three(dense[use % 2][:, 0:width], w_hi[:, u % RING, w], w_lo[:, u % RING, w], act_hi(k),
                                   act_lo(k), k == 0, last)
                        if last and not ends_unit(use):
                            mm.then_inc(tile_done, 1)
                        elif last or subs[k + 1][0] != u:
                            mm.then_inc(unit_used, 1)

                    def project(name, m, act_hi, act_lo, width=SEQ, before=None):
                        for k in range(len(PLAN[name][m][1])):
                            if before is not None:
                                before(k)
                            project_step(name, m, k, act_hi, act_lo, width)

                    def project_tokens(u0, banks, act_hi, act_lo):
                        for j in range(4):
                            s = (u0 + j) % RING
                            wait_split(pe, layer, u0 + j)
                            for i in range(2):
                                k, w = 2 * j + i, slice(i * SEQ, (i + 1) * SEQ)
                                for b, bank_t in enumerate(banks):
                                    mm = three(bank_t[:, :], act_hi(k, b), act_lo(k, b), w_hi[:, s, w],
                                               w_lo[:, s, w], k == 0, k == KT - 1)
                            mm.then_inc(unit_used, 1)

                    def norm_sum(name):
                        i = NORM_AT[name]
                        pe.wait_ge(squares_added, squares_before(name) + NORMS[i][1])
                        if i >= 1:
                            pe.wait_ge(ln_done, i)
                        pe.matmul(norm_bank[:, :], const(C_ONES), acc[:, :], start=True, stop=True)\
                          .then_inc(norm_summed, 1)

                    def after_norm(name):
                        return lambda k: pe.wait_ge(normed_lo, normed_before(name) + k + 1)

                    def tiles(t):
                        return lambda k: t[:, k, :]

                    for k in range(KT):
                        after_norm("mix_pre")(k)
                        for m in range(2):
                            project_step("in", m, k, tiles(h_hi), tiles(h_lo))
                            if k == KT - 1 and m == 0:
                                pe.wait_ge(consts_loaded, 16)
                                norm_sum("mix_pre")
                    for m in range(2, IN_FM):
                        project("in", m, tiles(h_hi), tiles(h_lo))
                        if m == 2:
                            pe.wait_ge(rstd_ready, 1)
                            for b in range(TB):
                                mm = pe.matmul(outs[0][:, b:b + 1], mix_rstd[0:1, b * P:(b + 1) * P],
                                               const(C_ONES, 1, slice(0, 1)), start=True, stop=True)
                            mm.then_inc(rcol_turned, 1)
                        if m == ML[3]:
                            norm_sum("q")
                    project_tokens(U_INV, wide, lambda k, b: h_hi[:, k, b * P:(b + 1) * P],
                                   lambda k, b: h_lo[:, k, b * P:(b + 1) * P])
                    norm_sum("kv")
                    project("sw", 0, tiles(h_hi), tiles(h_lo))

                    def do_between(step):
                        for name, m, k in between(step):
                            if name == "sw":
                                project_step("sw", m, k, tiles(h_hi), tiles(h_lo))
                            elif name == "uq":
                                if m == 0:
                                    after_norm("q")(k)
                                project_step("uq", m, k, tiles(c_hi), tiles(c_lo))
                            else:
                                use = use_of("rot", m)
                                wait_emptied(pe, use - 2)
                                wait_emptied(pe, use_of("sw", m))
                                pe.matmul(dense[use % 2][:, :], const(C_ROT), sw_qk[:, m, :], start=True, stop=True)\
                                  .then_inc(tile_done, 1)

                    g4 = slice(0, ML_HEADS)
                    pe.wait_ge(gate_rows, 3)
                    pe.wait_ge(v_ready, TB)
                    pe.wait_ge(rcol_ready, 1)
                    for kb in range(TB):
                        mm = pe.matmul(outs[0][:, 4 * kb:4 * kb + 4], gate[g4, 0, kb * P:(kb + 1) * P],
                                       const(C_IDENT, 4, g4), start=True, stop=True)
                    mm.then_inc(acol_turned, 1)
                    pe.wait_ge(acol_ready, 1)
                    pe.wait_ge(ln_done, 3)
                    pe.wait_ge(ml_qk_ready, 4)
                    units = [(h, kb) for h in range(ML_HEADS) for kb in range(TB)]

                    def ml_scores(u):
                        h, kb = units[u]
                        r = slice(64 * (h % 2), 64 * (h % 2) + 64)
                        if kb == 0:
                            if h:
                                pe.wait_ge(ml_weight, TB * h)
                                pe.wait_ge(ml_floor, h)
                            sel = const(C_IDENT + h, 1, g4).broadcast_to([ML_HEADS, P])
                            pe.matmul(outs[0][:, :], sel, gate[g4, 1, :], start=True, stop=True)
                            pe.matmul(outs[1][:, :], sel, gate[g4, 2, :], start=True, stop=True)\
                              .then_inc(spread, 1)
                        if u >= 2:
                            pe.wait_ge(ml_prob, u - 1)
                        pe.matmul(scores[u % 2][:, 0:SEQ - kb * P], ml_qk[r, 2 + h // 2, kb * P:(kb + 1) * P],
                                  ml_qk[r, h // 2, kb * P:SEQ], start=True, stop=True).then_inc(ml_scored, 1)

                    def ml_numerator(u):
                        h, kb = units[u]
                        pe.wait_ge(ml_prob, u + 1)
                        if kb == 0 and h >= 2:
                            pe.wait_ge(ml_out, h - 1)
                        pe.matmul(turned[h % 2][:, kb * P:SEQ], ml_v[:, kb, h, :, :].rearrange("p a d -> p (a d)"),
                                  w_ml[:, u % 2, 0:SEQ - kb * P], start=(kb == 0), stop=(kb == TB - 1))\
                          .then_inc(ml_num, 1)

                    for u in range(len(units) + 1):
                        if u < len(units):
                            ml_scores(u)
                        if u >= 1:
                            ml_numerator(u - 1)
                        do_between(u)

                    for m in range(4):
                        project("uk", m, lambda k: c_hi[:, 2, :], lambda k: c_lo[:, 2, :],
                                before=after_norm("kv") if m == 0 else None)
                    wait_split(pe, layer, U_UV)
                    for b in range(TB):
                        use, s, t = use_of("uv", b), U_UV % RING, slice(b * P, (b + 1) * P)
                        wait_emptied(pe, use - 2)
                        mm = three(dense[use % 2][:, :], c_hi[:, 2, t], c_lo[:, 2, t], w_hi[:, s, 0:SEQ],
                                   w_lo[:, s, 0:SEQ], True, True)
                        mm.then_inc(unit_used if ends_unit(use) else tile_done, 1)

                    def attention(a, heads, probs, klen, emit_scores, emit_out):
                        n_units = heads * TB
                        for u in range(n_units + LAG + OUT_LAG):
                            if u < n_units:
                                if u >= 4:
                                    pe.wait_ge(a["masked"], u - 3)
                                emit_scores(u // TB, u % TB, score_ring[u % 4]).then_inc(a["scored"], 1)
                            v = u - LAG
                            if 0 <= v < n_units:
                                if v < 2:
                                    pe.wait_ge(ml_out, ML_HEADS - 1 + v)
                                pe.wait_ge(a["probs"], v + 1)
                                if v >= 2:
                                    pe.wait_ge(a["copied"], v - 1)
                                for kb in range(klen(v % TB) // P):
                                    mm = pe.transpose(turned[v % 2][:, kb * P:(kb + 1) * P],
                                                      probs[:, v % PROBS, kb * P:(kb + 1) * P], const(C_IDENT))
                                mm.then_inc(a["turned"], 1)
                            w = u - LAG - OUT_LAG
                            if w >= 0 and w % TB == TB - 1:
                                pe.wait_ge(a["copied"], w + 1)
                                emit_out(w // TB)

                    def mix_scores(head, qb, bank_t):
                        hd = mix_head(head)
                        if head == 0 and qb == 0:
                            wait_emptied(pe, use_of("uq", MLA_HEADS - 1))
                            wait_emptied(pe, use_of("uk", 3))
                            pe.wait_ge(k_pe_spread, 2)
                            pe.wait_ge(roped, 4)
                        if head == 0 and qb >= 2:
                            wait_emptied(pe, use_of("uv", TB - 4 + qb))
                        if head == 2 and qb == 0:
                            pe.wait_ge(k_pe_rest, 1)
                            pe.wait_ge(k_pe_copied, 1)
                        n = causal_len(qb)
                        return pe.matmul(bank_t[:, 0:n], hd["q"][:, qb * P:n], hd["k"][:, 0:n], start=True, stop=True)

                    def mix_out(head):
                        if head >= 2:
                            pe.wait_ge(mix_at["out_lo"], head - 1)
                        for kb in range(TB):
                            mm = pe.matmul(outs[head % 2][0:64, kb * P:SEQ], mix_head(head)["v"](kb),
                                           pt_mix[:, head % 2, kb, kb * P:SEQ], start=(kb == 0), stop=(kb == TB - 1))
                        mm.then_inc(mix_at["out"], 1)

                    attention(mix_at, MIX_HEADS, p_mix, causal_len, mix_scores, mix_out)

                    pe.wait_ge(mix_at["out_lo"], MIX_HEADS)
                    pe.wait_ge(ml_lo, 2)
                    for m in range(KT):
                        project("out", m, tiles(h_hi), tiles(h_lo))
                    for m in range(KT):
                        project("xk", m, tiles(m_hi), tiles(m_lo), N_MEM, before=after_norm("mem") if m == 0 else None)
                        if m == 0:
                            norm_sum("mix_post")
                    for half in range(2):
                        project_tokens(U_XV + 4 * half, wide[2 * half:2 * half + 2],
                                       lambda k, b: m_hi[:, k, b * P:(b + 1) * P],
                                       lambda k, b: m_lo[:, k, b * P:(b + 1) * P])
                        if half == 0:
                            norm_sum("x_pre")
                    for m in range(KT):
                        project("xq", m, tiles(h_hi), tiles(h_lo), before=after_norm("x_pre") if m == 0 else None)

                    def x_scores(head, qb, bank_t):
                        if head == 0 and qb == 0:
                            wait_emptied(pe, use_of("xq", KT - 1))
                            pe.wait_ge(xv_ready, 4)
                        for c in range(2):
                            mm = pe.matmul(bank_t[:, 0:N_MEM], q_x[:, 2 * head + c, qb * P:(qb + 1) * P],
                                           k_x[:, 2 * head + c, :], start=(c == 0), stop=(c == 1))
                        return mm

                    def x_out(head):
                        for c in range(2):
                            if head >= 1:
                                pe.wait_ge(x_at["out_lo"], 2 * head - 1 + c)
                            for kb in range(2):
                                col = head * X_HD + c * P
                                mm = pe.matmul(outs[c][:, :], v_x[:, kb, col:col + P], pt_x[:, head % 2, kb, :],
                                               start=(kb == 0), stop=(kb == 1))
                            mm.then_inc(x_at["out"], 1)

                    attention(x_at, X_HEADS, p_x, lambda qb: N_MEM, x_scores, x_out)
                    pe.wait_ge(x_at["out_lo"], KT)
                    for m in range(KT):
                        project("xo", m, tiles(h_hi), tiles(h_lo))
                    norm_sum("x_post")

                    def gate_up_step(i, k):
                        s, w = (U_FF + i) % RING, slice(k * P, (k + 1) * P)
                        return three(ff_bank[i][:, :], w_hi[:, s, w], w_lo[:, s, w], h_hi[:, k, :], h_lo[:, k, :],
                                     k == 0, k == KT - 1)

                    wait_emptied(pe, use_of("xo", KT - 1))
                    wait_split(pe, layer, U_FF + 3)
                    for k in range(KT):
                        after_norm("ffn_pre")(k)
                        for i in range(4):
                            mm = gate_up_step(i, k)
                            if k == KT - 1:
                                mm.then_inc(unit_used, 1)
                                if i == 0:
                                    norm_sum("ffn_pre")
                    with pe.Fori(1, FT // 2) as j:
                        for i in range(4):
                            pe.wait_ge(ff_a if i % 2 else ff_gate, j * 2 + (i // 2 - 1))
                            wait_split(pe, layer, U_FF + i, j)
                            for k in range(KT):
                                mm = gate_up_step(i, k)
                            mm.then_inc(unit_used, 1)

                    for m in range(KT):
                        project("down", m, lambda k: a_hi[:, k * SEQ:(k + 1) * SEQ],
                                lambda k: a_lo[:, k * SEQ:(k + 1) * SEQ],
                                before=(lambda k: pe.wait_ge(ff_lo, k + 1)) if m == 0 else None)
                    norm_sum("ffn_post")

                @block.scalar
                def _(act):
                    done = counter(act)
                    act.preload_act_table_set("natural_log_exp_and_others")
                    made = [AHEAD]

                    def split_unit(n, j=0):
                        s = n % RING
                        if n < RING:
                            act.wait_ge(first_loaded[s], layer * 16 + 16)
                        elif n >= N_UNITS:
                            act.wait_ge(first_loaded[s], layer * 16 + 32)
                        else:
                            act.wait_ge(raw_loaded[s], j * 16 + 16 * (n // RING))
                        if n >= RING:
                            act.wait_ge(unit_used, j * RING + (n - RING + 1))
                        act.activation(w_hi[:, s, :], raw[:, s, :], ACT.Copy)\
                           .then_inc(first_hi if n >= N_UNITS else split_hi, 1)

                    def split_until(n):
                        while made[0] < min(n, N_UNITS + AHEAD):
                            split_unit(made[0])
                            made[0] += 1

                    def square(name, k, src):
                        c = squares_before(name) + k
                        if c >= 2:
                            act.wait_ge(squares_added, c - 1)
                        act.activation(sq[:, c % 2, :], src, ACT.Square).then_inc(squared, 1)

                    def make_rstd(name, features, dst=rstd):
                        act.wait_ge(norm_summed, NORM_AT[name] + 1)
                        if tn_before(name):
                            act.wait_ge(normed, tn_before(name))
                        if scaled_before(name):
                            act.wait_ge(y_scaled, scaled_before(name))
                        done(act.activation(dst[:, :], norm_bank[:, :], ACT.Ln, bias=eps[:, :],
                                            scale=1.0 / features), ln_done)
                        act.activation(dst[:, :], dst[:, :], ACT.Exp, scale=-0.5).then_inc(rstd_ready, 1)

                    def norm_hi(name, k, dst, width=SEQ):
                        c = tn_before(name) + k
                        act.wait_ge(normed, c + 1)
                        act.activation(dst, tn_of[name][:, c % 2, 0:width], ACT.Copy).then_inc(normed_hi, 1)

                    def scaled_hi(k, g):
                        act.activation(h_hi[:, k, :], x[:, k, :], ACT.Copy, scale=g).then_inc(normed_hi, 1)

                    def empty(name, m, dst, width=SEQ):
                        use = use_of(name, m)
                        wait_tile(act, use)
                        done(act.activation(dst, dense[use % 2][:, 0:width], ACT.Copy), emptied_act)

                    act.wait_ge(x_loaded, 16)
                    act.wait_ge(first_g_loaded, layer * 16 + 16)
                    for k in range(KT):
                        scaled_hi(k, first_g[:, k:k + 1])
                        square("mix_pre", k, x[:, k, :])
                        if k >= RING:
                            split_until(AHEAD + (k - RING + 1) // 2)
                    make_rstd("mix_pre", D_MODEL, mix_rstd)

                    g4 = slice(0, ML_HEADS)
                    def conv_exponential(j):
                        act.wait_ge(conv_done, j + 1)
                        act.activation(conv_in[:, j % 2, 3:3 + SEQ], ml_qk[:, j, :], ACT.Exp, scale=-1.0)\
                           .then_inc(conv_exp, 1)

                    for m in range(IN_FM):
                        split_until(m + 4)
                        if m == 2:
                            act.wait_ge(gate_biased, 2)
                            done(act.activation(gate[g4, 3, :], gate[g4, 1, :], ACT.Abs), gate_log)
                            done(act.activation(gate[g4, 3, :], gate[g4, 3, :], ACT.Exp, scale=-1.0), gate_log)
                            done(act.activation(gate[g4, 3, :], gate[g4, 3, :], ACT.Ln, bias=one[g4, :]), gate_log)
                        if m == 3:
                            conv_exponential(0)
                        if m == 6:
                            conv_exponential(1)
                            wait_emptied(act, use_of("in", CQ[1]))
                            for k in range(2):
                                square("q", k, c_tile(CQ[k]))
                        if m == 8:
                            conv_exponential(2)
                            wait_emptied(act, use_of("in", CKV))
                            square("kv", 0, c_tile(CKV))
                    make_rstd("q", MLA_Q_LORA)
                    split_until(U_INV + 4)
                    conv_exponential(3)
                    for j in range(2):
                        wait_emptied(act, use_of("in", OG + j))
                        act.activation(o_gate[:, j, :], o_gate[:, j, :], ACT.Exp, scale=-1.0).then_inc(o_exp, 1)
                    for k in range(2):
                        norm_hi("q", k, c_hi[:, k, :])
                    split_until(U_SW + 4)
                    make_rstd("kv", MLA_KV_LORA)

                    ml_units = ML_HEADS * TB
                    def ml_abs_of(h):
                        act.wait_ge(ml_num, TB * (h + 1))
                        act.activation(conv_in[64:128, 1, 0:SEQ], turned[h % 2][64:128, :], ACT.Abs)\
                           .then_inc(ml_abs, 1)

                    def ml_output_hi(t):
                        act.wait_ge(ml_out, 2 * t + 2)
                        act.activation(h_hi[:, 4 + t, :], o_gate[:, t, :], ACT.Copy).then_inc(ml_hi, 1)

                    for u in range(ml_units + 1):
                        h = u // TB
                        if u < ml_units:
                            n = SEQ - u % TB * P
                            act.wait_ge(ml_weight, u + 1)
                            act.activation(w_ml[:, u % 2, 0:n], w_ml[:, u % 2, 0:n], ACT.Exp).then_inc(ml_exp, 1)
                            if u % TB == TB - 1:
                                act.wait_ge(spread, h + 1)
                                if h:
                                    act.wait_ge(ml_out, h)
                                act.activation(conv_in[64:128, 0, 0:SEQ], outs[1][64:128, :], ACT.Exp)\
                                   .then_inc(ml_floor, 1)
                        if u >= 1:
                            split_until(units_through(u - 1) + 4)
                        if u == 1:
                            norm_hi("kv", 0, c_hi[:, 2, :])
                        if u == 2 * TB + 3:
                            ml_output_hi(0)
                        if TB <= u < ml_units and u % TB == 1:
                            ml_abs_of(h - 1)
                    split_until(units_through(ML_STEPS - 1) + 4)
                    ml_abs_of(ML_HEADS - 1)
                    split_until(U_UK + 4)
                    for m in range(4):
                        use = use_of("uk", m)
                        wait_tile(act, use)
                        for i in range(2):
                            done(act.activation(k_mla[0:64, 2 * m + i, :], dense[use % 2][64 * i:64 * i + 64, :],
                                                ACT.Copy), emptied_act if i else act_step)
                    act.wait_ge(k_pe_ready, 1)
                    act.activation(k_mla[K_PE_ROWS[1], 2:MLA_HEADS, :], k_pe[K_PE_ROWS[0], :].unsqueeze(1)
                                   .broadcast_to([MLA_ROPE, MLA_HEADS - 2, SEQ]), ACT.Copy).then_inc(k_pe_rest, 1)
                    ml_output_hi(1)
                    split_until(U_UV + 4)

                    def attention(a, heads, probs, probs_t, klen, banks, emit_hi):
                        n_units = heads * TB
                        for u in range(n_units + LAG + OUT_LAG + 1):
                            w = u - LAG - OUT_LAG - 1
                            if w >= 0 and w % TB == TB - 1:
                                emit_hi(w // TB)
                            v = u - LAG
                            if 0 <= v < n_units:
                                head, qb, m = v // TB, v % TB, klen(v % TB) // P
                                act.wait_ge(a["turned"], v + 1)
                                if qb == 0 and head >= 2:
                                    act.wait_ge(a["out"], banks * (head - 1))
                                act.activation(probs_t[:, head % 2, 0:m, qb * P:(qb + 1) * P],
                                               turned[v % 2][:, 0:m * P].rearrange("p (b q) -> p b q", q=P),
                                               ACT.Copy).then_inc(a["copied"], 1)
                            if u < n_units:
                                n = klen(u % TB)
                                act.wait_ge(a["masked"], u + 1)
                                act.activation(probs[:, u % PROBS, 0:n], probs[:, u % PROBS, 0:n], ACT.Exp, scale=-1.0,
                                               bias=stat[:, 0, u:u + 1], accum_out=stat[:, 1, u:u + 1])\
                                   .then_inc(a["exped"], 1)

                    def mix_hi(head):
                        hd = mix_head(head)
                        act.wait_ge(mix_at["out"], head + 1)
                        act.activation(h_hi[hd["row"]:hd["row"] + 64, hd["tile"], :], outs[head % 2][0:64, :],
                                       ACT.Copy).then_inc(mix_at["out_hi"], 1)

                    attention(mix_at, MIX_HEADS, p_mix, pt_mix, causal_len, 1, mix_hi)

                    def post(name, plan, y, col, between=None):
                        for m in range(KT):
                            use = use_of(plan, m)
                            split_until(USES[use][0][-1][0] + 4)
                            wait_tile(act, use)
                            square(name, m, dense[use % 2][:, :])
                            act.activation(y[:, m, :], dense[use % 2][:, :], ACT.Copy, scale=gain(col + m))\
                               .then_inc(emptied_act, 1)
                            if between is not None:
                                between(m)

                    post("mix_post", "out", y_x, G_MIX_POST, lambda m: norm_hi("mem", m, m_hi[:, m, :], N_MEM))
                    make_rstd("mix_post", D_MODEL)
                    for m in range(KT + 3):
                        if m < KT:
                            split_until(U_XK + m + 4)
                            empty("xk", m, k_x[:, m, :], width=N_MEM)
                        if m >= 3:
                            wait_x(act, "mix_post", m - 3)
                            square("x_pre", m - 3, x[:, m - 3, :])
                    split_until(U_XV + 4 + 3)
                    make_rstd("x_pre", D_MODEL)
                    for k in range(KT):
                        split_until(U_XV + 8 + k // 2)
                        norm_hi("x_pre", k, h_hi[:, k, :])
                    split_until(U_XQ + 3)
                    for m in range(KT):
                        split_until(U_XQ + m + 4)
                        empty("xq", m, q_x[:, m, :])

                    def x_hi(head):
                        for c in range(2):
                            act.wait_ge(x_at["out"], 2 * head + c + 1)
                            act.activation(h_hi[:, 2 * head + c, :], outs[c][:, :], ACT.Copy)\
                               .then_inc(x_at["out_hi"], 1)

                    attention(x_at, X_HEADS, p_x, pt_x, lambda qb: N_MEM, 2, x_hi)
                    post("x_post", "xo", y_x, G_X_POST)
                    split_until(U_FF + 4)
                    make_rstd("x_post", D_MODEL)
                    for k in range(KT):
                        wait_x(act, "x_post", k)
                        scaled_hi(k, gain(G_FFN_PRE + k))
                        square("ffn_pre", k, x[:, k, :])
                    split_until(U_FF + 5)
                    make_rstd("ffn_pre", D_MODEL)
                    split_until(U_FF + 6)

                    def ff_turn(j, first_turn):
                        for i in range(2):
                            act.wait_ge(ff_gate, j * 2 + (i + 1))
                            act.activation(f_e[:, :], f_a[:, i, :], ACT.Exp, scale=-1.0).then_inc(ff_exp, 1)
                            split_unit(U_FF + (6 + i if first_turn else 4 + 2 * i), j)
                            act.wait_ge(ff_a, j * 2 + (i + 1))
                            act.activation(a_hi[:, bass.ds(j * (2 * SEQ) + i * SEQ, SEQ)], f_a[:, i, :], ACT.Copy)\
                               .then_inc(ff_hi, 1)
                            if not first_turn:
                                split_unit(U_FF + 5 + 2 * i, j)

                    ff_turn(0, True)
                    with act.Fori(1, FT // 2) as j:
                        ff_turn(j, False)
                    made[0] = U_DOWN + 4
                    act.wait_ge(ff_lo, FT)
                    post("ffn_post", "down", y_f, G_FFN_POST)
                    make_rstd("ffn_post", D_MODEL)

                @block.vector
                def _(dve):
                    done = counter(dve)

                    def add_square(name, k):
                        dve.wait_ge(squared, squares_before(name) + k + 1)
                        s = (squares_before(name) + k) % 2
                        if k == 0:
                            if NORM_AT[name]:
                                dve.wait_ge(norm_summed, NORM_AT[name])
                            ins = dve.tensor_copy(acc[:, :], sq[:, s, :])
                        else:
                            ins = dve.tensor_tensor(acc[:, :], acc[:, :], sq[:, s, :], ALU.add)
                        done(ins, squares_added)

                    def add_squares(name, n, between=None):
                        for k in range(n):
                            add_square(name, k)
                            if between is not None:
                                between(k)

                    def norm_step(name, k, n, src, col, dst_hi, dst_lo):
                        c, tn = tn_before(name) + k, tn_of[name]
                        r, width = (mem_rstd, N_MEM) if name == "mem" else (rstd, SEQ)
                        if k < n:
                            done(dve.scalar_tensor_tensor(out=tn[:, c % 2, 0:width], in0=src(k),
                                                          scalar=gain(col + k), in1=r[:, 0:width],
                                                          op0=ALU.mult, op1=ALU.mult), normed)
                        if k >= 1:
                            dve.wait_ge(normed_hi, normed_before(name) + k)
                            done(dve.tensor_tensor(dst_lo(k - 1), tn[:, (c - 1) % 2, 0:width],
                                                   dst_hi(k - 1).bitcast(F32), ALU.subtract), normed_lo)

                    def norm(name, n, *operands):
                        dve.wait_ge(rstd_ready, NORM_AT[name] + 1)
                        for k in range(n + 1):
                            norm_step(name, k, n, *operands)

                    def take(name, m, dst):
                        use = use_of(name, m)
                        wait_tile(dve, use)
                        done(dve.tensor_tensor(dst, dense[use % 2][:, :], mix_rstd[:, :], ALU.mult), emptied_dve)

                    def scaled_lo(name, k, g):
                        dve.wait_ge(normed_hi, normed_before(name) + k + 1)
                        done(dve.scalar_tensor_tensor(out=h_lo[:, k, :], in0=x[:, k, :], scalar=g,
                                                      in1=h_hi[:, k, :].bitcast(F32), op0=ALU.mult,
                                                      op1=ALU.subtract), normed_lo)

                    def residual(name, plan, y, between=None):
                        dve.wait_ge(rstd_ready, NORM_AT[name] + 1)
                        wait_emptied(dve, use_of(plan, KT - 1))
                        first = scaled_before(name)
                        for k in range(KT + 1):
                            if k < KT:
                                dve.tensor_tensor(y[:, k, :], y[:, k, :], rstd[:, :], ALU.mult)\
                                   .then_inc(y_scaled, 1)
                            if k >= 1:
                                if name == "mix_post" or k - 1 not in POOL_ADDS:
                                    dve.wait_ge(y_scaled, first + k)
                                    done(dve.tensor_tensor(x[:, k - 1, :], x[:, k - 1, :], y[:, k - 1, :], ALU.add),
                                         x_updated)
                                if between is not None:
                                    between(k - 1)

                    def tiles(t):
                        return lambda k: t[:, k, :]

                    for k in range(KT):
                        scaled_lo("mix_pre", k, first_g[:, k:k + 1])
                        add_square("mix_pre", k)
                    done(dve.memset(ml_v[:, :, :, 1, :], 1.0), pads_set)
                    done(dve.memset(conv_in[:, :, 0:3], 0.0), pads_set)
                    dve.wait_ge(gains_loaded, 16)
                    dve.wait_ge(consts_loaded, 16)
                    dve.wait_ge(rstd_ready, 1)

                    misc = c_tile(MISC)
                    take("in", MISC, misc)
                    g4, f4 = slice(ROW_I, ROW_I + ML_HEADS), slice(ROW_F, ROW_F + ML_HEADS)
                    done(dve.tensor_scalar(gate[g4, 0, :], misc[g4, :], gain(G_GATE_B, g4), None, ALU.add), gate_biased)
                    done(dve.tensor_scalar(gate[g4, 1, :], misc[f4, :], gain(G_GATE_B, f4), None, ALU.add), gate_biased)
                    def convolve(j):
                        src, dst = conv_in[:, j % 2, :], ml_qk[:, j, :]
                        w = G_CONV_W + j * ML_CONV
                        done(dve.tensor_scalar(dst, src[:, 3:3 + SEQ], gain(w + 3), gain(G_CONV_B + j), ALU.mult,
                                               ALU.add), dve_step)
                        for tap in range(3):
                            done(dve.scalar_tensor_tensor(out=dst, in0=src[:, tap:tap + SEQ], scalar=gain(w + tap),
                                                          in1=dst, op0=ALU.mult, op1=ALU.add),
                                 conv_done if tap == 2 else dve_step)

                    def silu(j):
                        dve.wait_ge(conv_exp, j + 1)
                        e = conv_in[:, j % 2, 3:3 + SEQ]
                        done(dve.tensor_scalar(e, e, 1.0, None, ALU.add), dve_step)
                        done(dve.reciprocal(e, e), dve_step)
                        done(dve.tensor_tensor(ml_qk[:, j, :], ml_qk[:, j, :], e, ALU.mult), ml_qk_ready)

                    take("in", ML[0], conv_in[:, 0, 3:3 + SEQ])
                    convolve(0)
                    take("in", CQ[0], c_tile(CQ[0]))
                    dve.wait_ge(gate_log, 3)
                    done(dve.tensor_scalar(gate[g4, 1, :], gate[g4, 1, :], 0.0, None, ALU.min), dve_step)
                    done(dve.tensor_tensor(gate[g4, 1, :], gate[g4, 1, :], gate[g4, 3, :], ALU.subtract), dve_step)
                    ones = const(C_ROPE_Q, SEQ, g4)
                    done(dve.tensor_tensor_scan(gate[g4, 2, :], ones, gate[g4, 1, :], 0.0, ALU.mult, ALU.add), dve_step)
                    take("in", ML[1], conv_in[:, 1, 3:3 + SEQ])
                    done(dve.tensor_tensor(gate[g4, 0, :], gate[g4, 0, :], gate[g4, 2, :], ALU.subtract), gate_rows)
                    silu(0)
                    take("in", CQ[1], c_tile(CQ[1]))
                    convolve(1)
                    take("in", ML[2], conv_in[:, 0, 3:3 + SEQ])
                    silu(1)
                    add_squares("q", 2)
                    take("in", CKV, c_tile(CKV))
                    convolve(2)
                    take("in", ML[3], conv_in[:, 1, 3:3 + SEQ])
                    silu(2)
                    add_squares("kv", 1)
                    take("in", OG, o_gate[:, 0, :])
                    convolve(3)
                    take("in", OG + 1, o_gate[:, 1, :])
                    silu(3)
                    norm("q", 2, lambda k: c_tile(CQ[k]), G_Q, tiles(c_hi), tiles(c_lo))
                    done(dve.tensor_tensor_scan(gate[g4, 3, :], gate[g4, 0, :], gate[g4, 0, :], NEG,
                                                ALU.max, ALU.max), dve_step)
                    done(dve.tensor_scalar(gate[g4, 1, :], gate[g4, 3, :], -1.0, None, ALU.mult), gate_rows)
                    done(dve.tensor_tensor(gate[g4, 2, :], gate[g4, 1, :], gate[g4, 2, :], ALU.subtract), gate_rows)
                    dve.wait_ge(rcol_turned, 1)
                    done(dve.tensor_copy(rcol[:, :], outs[0][:, 0:TB]), rcol_ready)
                    dve.wait_ge(unit_used, U_INV + 4)
                    for b in range(TB):
                        half = ML_HEADS * ML_DK
                        r = rcol[:, b:b + 1]
                        done(dve.tensor_scalar(ml_v[:, b, :, 0, :],
                                               wide[b][:, 0:half].rearrange("p (h d) -> p h d", h=ML_HEADS), r, None,
                                               ALU.mult), dve_step)
                        done(dve.tensor_scalar(sw_v[:, b, :], wide[b][:, half:SEQ], r, None, ALU.mult), v_ready)
                    take("sw", 0, sw_qk[:, 0, :])

                    def rope_tile(j):
                        use = use_of("rot", j)
                        wait_tile(dve, use)
                        t = tn_mix[:, j % 2, :]
                        done(dve.tensor_tensor(t, dense[use % 2][:, :], const(C_SW_SIN, SEQ), ALU.mult), emptied_dve)
                        done(dve.tensor_tensor(sw_qk[:, j, :], sw_qk[:, j, :], const(C_SW_COS, SEQ), ALU.mult),
                             dve_step)
                        done(dve.tensor_tensor(sw_qk[:, j, :], sw_qk[:, j, :], t, ALU.add), roped)

                    def query_tile(h):
                        use = use_of("uq", h)
                        wait_tile(dve, use)
                        done(dve.tensor_tensor(q_mla[:, h, :], dense[use % 2][:, :], const(C_ROPE_Q, SEQ), ALU.mult),
                             emptied_dve)

                    dve.wait_ge(acol_turned, 1)
                    done(dve.tensor_copy(acol[:, :, :], outs[0][:, 0:TB * ML_HEADS]
                                         .rearrange("p (b h) -> p b h", h=ML_HEADS)), acol_ready)
                    ml_units = ML_HEADS * TB

                    def take_completed(step):
                        if 0 <= step < ML_STEPS:
                            for name, m in completed(step):
                                if name == "sw":
                                    take("sw", m, sw_qk[:, m, :])
                                if name == "rot":
                                    rope_tile(m)
                                if name == "uq":
                                    query_tile(m)

                    halves = [(slice(0, 64), slice(0, SEQ // 2)), (slice(64, 128), slice(SEQ // 2, SEQ))]

                    def ml_denominator(h):
                        dve.wait_ge(ml_floor, h + 1)
                        dve.wait_ge(ml_abs, h + 1)
                        for rows, t in halves:
                            done(dve.tensor_tensor(ml_den[rows, :], conv_in[64:128, 1, t], conv_in[64:128, 0, t],
                                                   ALU.max), dve_step)
                        done(dve.reciprocal(ml_den[:, :], ml_den[:, :]), dve_step)

                    def ml_finish(h):
                        r = slice(64 * (h % 2), 64 * (h % 2) + 64)
                        for rows, t in halves:
                            done(dve.tensor_tensor(sq[r, 0, t], turned[h % 2][0:64, t], ml_den[rows, :], ALU.mult),
                                 dve_step)
                        done(dve.tensor_tensor(o_gate[r, h // 2, :], o_gate[r, h // 2, :], sq[r, 0, :], ALU.mult),
                             ml_out)

                    def ml_output_lo(t):
                        dve.wait_ge(ml_hi, t + 1)
                        done(dve.tensor_tensor(h_lo[:, 4 + t, :], o_gate[:, t, :], h_hi[:, 4 + t, :].bitcast(F32),
                                               ALU.subtract), ml_lo)

                    def output_gate(j):
                        dve.wait_ge(o_exp, j + 1)
                        done(dve.tensor_scalar(o_gate[:, j, :], o_gate[:, j, :], 1.0, None, ALU.add), dve_step)
                        done(dve.reciprocal(o_gate[:, j, :], o_gate[:, j, :]), dve_step)


                    def rotary_key():
                        r0, r1 = K_PE_ROWS
                        done(dve.tensor_tensor(misc[r1, :], misc[r1, :], const(C_ROPE_Q, SEQ, r1), ALU.mult), dve_step)
                        done(dve.tensor_tensor(misc[r0, :], misc[r0, :], const(C_ROPE_Q, SEQ, r0), ALU.mult), dve_step)
                        done(dve.tensor_copy(sq[r0, 0, :], misc[r1, :]), dve_step)
                        done(dve.tensor_tensor(k_pe[r0, :], misc[r0, :], sq[r0, 0, :], ALU.add), k_pe_ready)

                    for u in range(ml_units + 1):
                        if 1 <= u <= ml_units:
                            v, n = u - 1, SEQ - (u - 1) % TB * P
                            dve.wait_ge(ml_exp, v + 1)
                            dve.wait_ge(ml_scored, v + 1)
                            done(dve.scalar_tensor_tensor(out=w_ml[:, v % 2, 0:n], in0=scores[v % 2][:, 0:n],
                                                          scalar=ML_DK ** -0.5, in1=w_ml[:, v % 2, 0:n],
                                                          op0=ALU.mult, op1=ALU.mult), ml_prob)
                        if u % TB == 0:
                            take_completed(u - 1)
                        if u < ml_units:
                            h, kb, n = u // TB, u % TB, SEQ - u % TB * P
                            if kb == 0:
                                dve.wait_ge(spread, h + 1)
                            if u >= 2:
                                dve.wait_ge(ml_num, u - 1)
                            done(dve.scalar_tensor_tensor(out=w_ml[:, u % 2, 0:n], in0=outs[0][:, kb * P:SEQ],
                                                          scalar=acol[:, kb, h:h + 1], in1=const(C_CAUSAL_T, n),
                                                          op0=ALU.add, op1=ALU.add), ml_weight)
                        if u % TB:
                            take_completed(u - 1)
                        if u == 1:
                            norm("kv", 1, lambda k: c_tile(CKV), G_KV, lambda k: c_hi[:, 2, :],
                                 lambda k: c_lo[:, 2, :])
                        if u == 2:
                            output_gate(0)
                        if u == 3:
                            rotary_key()
                        if u == 7:
                            output_gate(1)
                        if u == 2 * TB + 4:
                            ml_output_lo(0)
                        if TB <= u < ml_units and u % TB == 1:
                            ml_denominator(u // TB - 1)
                        if TB <= u < ml_units and u % TB == 2:
                            ml_finish(u // TB - 1)
                    take_completed(ML_STEPS - 1)
                    for rows in K_PE_ROWS:
                        done(dve.tensor_copy(k_mla[rows, 0:2, :], k_pe[K_PE_ROWS[0], :].unsqueeze(1)
                                             .broadcast_to([MLA_ROPE, 2, SEQ])), k_pe_spread)

                    def take_value(b):
                        use = use_of("uv", b)
                        wait_tile(dve, use)
                        done(dve.tensor_copy(v_mla[:, b, :], dense[use % 2][:, :]), emptied_dve)

                    ml_denominator(ML_HEADS - 1)
                    ml_finish(ML_HEADS - 1)
                    for b in range(TB):
                        take_value(b)
                    ml_output_lo(1)

                    def attention(a, heads, probs, klen, mask, scale, emit_lo):
                        n_units = heads * TB
                        for u in range(n_units + LAG + OUT_LAG + 2):
                            if u < n_units:
                                n = klen(u % TB)
                                dve.wait_ge(a["scored"], u + 1)
                                if u >= PROBS:
                                    dve.wait_ge(a["turned"], u - PROBS + 1)
                                done(dve.tensor_tensor_reduce(
                                    probs[:, u % PROBS, 0:n], score_ring[u % 4][:, 0:n],
                                    const(mask(u // TB) + SEQ - n, n), -scale(u // TB), 3e38, ALU.add, ALU.min,
                                    stat[:, 0, u:u + 1]), a["masked"])
                            v = u - 1
                            if 0 <= v < n_units:
                                n = klen(v % TB)
                                dve.wait_ge(a["exped"], v + 1)
                                done(dve.reciprocal(stat[:, 2, v:v + 1], stat[:, 1, v:v + 1]), dve_step)
                                done(dve.tensor_scalar(probs[:, v % PROBS, 0:n], probs[:, v % PROBS, 0:n],
                                                       stat[:, 2, v:v + 1], None, ALU.mult), a["probs"])
                            w = u - LAG - OUT_LAG - 2
                            if w >= 0 and w % TB == TB - 1:
                                emit_lo(w // TB)

                    def mix_lo(head):
                        hd = mix_head(head)
                        r = slice(hd["row"], hd["row"] + 64)
                        dve.wait_ge(mix_at["out_hi"], head + 1)
                        done(dve.tensor_tensor(h_lo[r, hd["tile"], :], outs[head % 2][0:64, :],
                                               h_hi[r, hd["tile"], :].bitcast(F32), ALU.subtract), mix_at["out_lo"])

                    attention(mix_at, MIX_HEADS, p_mix, causal_len, lambda h: mix_head(h)["mask"],
                              lambda h: mix_head(h)["scale"], mix_lo)

                    dve.wait_ge(mem_loaded, 16)
                    mem_norm = (KT, tiles(mem), G_MEM, tiles(m_hi), tiles(m_lo))
                    add_squares("mix_post", KT, between=lambda m: norm_step("mem", m, *mem_norm))
                    norm_step("mem", KT, *mem_norm)
                    residual("mix_post", "out", y_x)
                    add_squares("x_pre", KT)
                    norm("x_pre", KT, tiles(x), G_X_PRE, tiles(h_hi), tiles(h_lo))
                    for half in range(2):
                        dve.wait_ge(unit_used, U_XV + 4 * half + 4)
                        for b in range(2):
                            done(dve.tensor_copy(v_x[:, b, half * SEQ:(half + 1) * SEQ], wide[2 * half + b][:, :]),
                                 xv_ready)

                    def x_lo(head):
                        for c in range(2):
                            dve.wait_ge(x_at["out_hi"], 2 * head + c + 1)
                            done(dve.tensor_tensor(h_lo[:, 2 * head + c, :], outs[c][:, :],
                                                   h_hi[:, 2 * head + c, :].bitcast(F32), ALU.subtract),
                                 x_at["out_lo"])

                    attention(x_at, X_HEADS, p_x, lambda qb: N_MEM, lambda h: C_CAUSAL - (SEQ - N_MEM),
                              lambda h: X_HD ** -0.5, x_lo)
                    add_squares("x_post", KT)

                    def ffn_input(k):
                        if k >= 1:
                            scaled_lo("ffn_pre", k - 1, gain(G_FFN_PRE + k - 1))
                            add_square("ffn_pre", k - 1)

                    residual("x_post", "xo", y_x, ffn_input)
                    ffn_input(KT)

                    def ff_turn(j):
                        for i in range(2):
                            e, gate_up = f_e[:, :], f_a[:, i, :]

                            def step(ins, k):
                                ins.then_inc(ff_step, 1)
                                dve.wait_ge(ff_step, j * 8 + (4 * i + k))

                            dve.wait_ge(unit_used, j * 4 + (U_FF + 2 * i + 1))
                            dve.tensor_tensor(gate_up, ff_bank[2 * i][:, :], rstd[:, :], ALU.mult)\
                               .then_inc(ff_gate, 1)
                            dve.wait_ge(ff_exp, j * 2 + (i + 1))
                            step(dve.tensor_scalar(e, e, 1.0, None, ALU.add), 1)
                            step(dve.reciprocal(e, e), 2)
                            step(dve.tensor_tensor(e, gate_up, e, ALU.mult), 3)
                            step(dve.tensor_tensor(e, e, rstd[:, :], ALU.mult), 4)
                            dve.wait_ge(unit_used, j * 4 + (U_FF + 2 * i + 2))
                            dve.tensor_tensor(gate_up, ff_bank[2 * i + 1][:, :], e, ALU.mult).then_inc(ff_a, 1)
                            dve.wait_ge(ff_hi, j * 2 + (i + 1))
                            at = bass.ds(j * (2 * SEQ) + i * SEQ, SEQ)
                            dve.tensor_tensor(a_lo[:, at], gate_up, a_hi[:, at].bitcast(F32), ALU.subtract)\
                               .then_inc(ff_lo, 1)
                            dve.wait_ge(ff_lo, j * 2 + (i + 1))

                    dve.wait_ge(rstd_ready, NORM_AT["ffn_pre"] + 1)
                    ff_turn(0)
                    with dve.Fori(1, FT // 2) as j:
                        ff_turn(j)
                    add_squares("ffn_post", KT)
                    residual("ffn_post", "down", y_f)

            with nc.Block() as block:
                @block.sync
                def _(sp):
                    for s in layer_sems[0::4]:
                        sp.sem_clear(s)

                @block.scalar
                def _(act):
                    for s in layer_sems[1::4]:
                        act.sem_clear(s)

                @block.vector
                def _(dve):
                    for s in layer_sems[2::4]:
                        dve.sem_clear(s)

                @block.tensor
                def _(pe):
                    for s in layer_sems[3::4]:
                        pe.sem_clear(s)

        with nc.Block() as block:
            @block.sync
            def _(sp):
                sp.dma_start(out, x[:, :, :]).then_inc(stored, 16)
                sp.wait_ge(stored, 16)
                for s in range(RING):
                    sp.wait_ge(first_loaded[s], (DEPTH + 1) * 16)
                sp.wait_ge(first_g_loaded, (DEPTH + 1) * 16)


def constants():
    c = np.zeros((P, N_CONST), np.float32)

    def tables(d):
        inv = np.float32(ROPE_THETA) ** (-np.arange(0, d, 2, dtype=np.float32) / np.float32(d))
        ang = inv.astype(np.float32)[:, None] * np.arange(SEQ, dtype=np.float32)[None, :]
        cos, sin = np.cos(ang).astype(np.float32), np.sin(ang).astype(np.float32)
        return np.concatenate([cos, cos]), np.concatenate([-sin, sin])

    cos, sin = tables(MLA_ROPE)
    c[0:MLA_NOPE, C_ROPE_Q:C_ROPE_Q + SEQ] = 1.0
    c[ROW_R:ROW_R + MLA_ROPE, C_ROPE_Q:C_ROPE_Q + SEQ] = cos
    c[ROW_RS:ROW_RS + MLA_ROPE, C_ROPE_Q:C_ROPE_Q + SEQ] = sin
    cos, sin = tables(SW_ROT)
    c[:, C_SW_COS:C_SW_COS + SEQ] = 1.0
    for r in (0, SW_HD):
        c[r:r + SW_ROT, C_SW_COS:C_SW_COS + SEQ] = cos
        c[r:r + SW_ROT, C_SW_SIN:C_SW_SIN + SEQ] = sin
        for i in range(SW_ROT):
            c[r + (i + SW_ROT // 2) % SW_ROT, C_ROT + r + i] = 1.0
    t, s = np.arange(P)[:, None] + SEQ - P, np.arange(SEQ)[None, :]
    d = t - s
    c[:, C_CAUSAL:C_CAUSAL + SEQ] = np.where(d >= 0, 0.0, NEG)
    count = sum(((d >= 0) & (d % dil == 0) & (d // dil <= win // dil)).astype(np.float64) for win, dil in SW_CONFIGS)
    c[:, C_DILATED:C_DILATED + SEQ] = np.where(count > 0, np.log(np.maximum(count, 1)) * SW_HD ** 0.5, NEG)
    c[:, C_CAUSAL_T:C_CAUSAL_T + SEQ] = np.where(np.arange(P)[:, None] <= np.arange(SEQ)[None, :], 0.0, NEG)
    c[:, C_IDENT:C_IDENT + P] = np.eye(P)
    c[:, C_ONES:C_ONES + P] = 1.0
    return c


def swap_halves(w):
    half = w.shape[-1] // 2
    return np.concatenate([w[..., half:], w[..., :half]], axis=-1)


def weight_stream(i):
    w = np.zeros((DEPTH, N_UNITS, P, UNIT), np.float32)

    def whole(u0, mat):
        n = mat.shape[2] // P
        w[:, u0:u0 + n] = mat.reshape(DEPTH, KT, P, n, P).transpose(0, 3, 2, 1, 4).reshape(DEPTH, n, P, UNIT)

    def token_major(u0, mat):
        w[:, u0:u0 + 4] = mat.reshape(DEPTH, 4, 2, P, SEQ).transpose(0, 1, 3, 2, 4).reshape(DEPTH, 4, P, UNIT)

    names = ("c_q", "c_kv", "k_rope", "ml_q", "ml_k", "ml_v", "ml_o", "ml_i", "ml_f", "sw_q", "sw_k", "sw_v")
    sizes = (MLA_Q_LORA, MLA_KV_LORA, MLA_ROPE, 256, 256, 256, 256, ML_HEADS, ML_HEADS, 256, 256, 256)
    part = dict(zip(names, np.split(i["w_in"], np.cumsum(sizes)[:-1], axis=2)))
    misc = np.zeros((DEPTH, D_MODEL, P), np.float32)
    misc[:, :, ROW_I:ROW_I + ML_HEADS] = part["ml_i"]
    misc[:, :, ROW_F:ROW_F + ML_HEADS] = part["ml_f"]
    misc[:, :, ROW_R:ROW_R + MLA_ROPE] = part["k_rope"]
    misc[:, :, ROW_RS:ROW_RS + MLA_ROPE] = swap_halves(part["k_rope"])
    order = {MISC: misc, CKV: part["c_kv"]}
    for tiles_at, mat in ((CQ, part["c_q"]), (ML, np.concatenate([part["ml_q"], part["ml_k"]], axis=2)),
                          ((OG, OG + 1), part["ml_o"])):
        for n, m in enumerate(tiles_at):
            order[m] = mat[:, :, n * P:(n + 1) * P]
    whole(U_IN, np.concatenate([order[m] for m in range(IN_FM)], axis=2))
    whole(U_SW, np.concatenate([part["sw_q"], part["sw_k"]], axis=2))
    token_major(U_INV, np.concatenate([part["ml_v"], part["sw_v"]], axis=2))
    uq = i["mla_w_uq"].reshape(DEPTH, 2, P, MLA_HEADS, MLA_NOPE + MLA_ROPE)
    uq = np.concatenate([uq, swap_halves(uq[..., MLA_NOPE:])], axis=4)
    w[:, U_UQ:U_UQ + 2] = uq.reshape(DEPTH, 2, P, 2, 4, P).transpose(0, 3, 2, 4, 1, 5).reshape(DEPTH, 2, P, UNIT)
    ukv = i["mla_w_ukv"].reshape(DEPTH, P, MLA_HEADS, MLA_NOPE + MLA_V)
    w[:, U_UK, :, 0:SEQ] = ukv[..., :MLA_NOPE].reshape(DEPTH, P, SEQ)
    w[:, U_UV, :, 0:SEQ] = ukv[..., MLA_NOPE:].reshape(DEPTH, P, SEQ)
    whole(U_OUT, i["w_out"])
    whole(U_XK, i["x_w_kv"][:, :, :D_MODEL])
    for half in range(2):
        a = D_MODEL + half * SEQ
        token_major(U_XV + 4 * half, i["x_w_kv"][:, :, a:a + SEQ])
    whole(U_XQ, i["x_w_q"])
    whole(U_XO, i["x_w_o"])
    gu = i["w_gate_up"].reshape(DEPTH, D_MODEL, 2, FT, P).transpose(0, 1, 3, 2, 4).reshape(DEPTH, D_MODEL, -1)
    whole(U_FF, gu)
    down = i["w_down"].reshape(DEPTH, FT, P, KT, P).transpose(0, 3, 1, 2, 4).reshape(DEPTH, FT, KT, P, P)
    w[:, U_DOWN:U_DOWN + FT] = down.transpose(0, 1, 3, 2, 4).reshape(DEPTH, FT, P, UNIT)
    first = np.zeros((DEPTH + 1, RING, P, UNIT), np.float32)
    first[:DEPTH] = w[:, :RING]
    return first, np.ascontiguousarray(w[:, RING:])


def gain_columns(i):
    g = np.zeros((DEPTH, P, N_GAINS), np.float32)

    def put(col, v):
        n = v.shape[1] // P
        g[:, :, col:col + n] = v.reshape(DEPTH, n, P).transpose(0, 2, 1)

    for col, name in ((G_MIX_POST, "norm_mix_post"), (G_MEM, "norm_mem"),
                      (G_X_PRE, "norm_x_pre"), (G_X_POST, "norm_x_post"), (G_FFN_PRE, "norm_ffn_pre"),
                      (G_FFN_POST, "norm_ffn_post"), (G_Q, "mla_q_norm"), (G_KV, "mla_kv_norm"),
                      (G_CONV_B, "ml_conv_b")):
        put(col, i[name])
    taps = i["ml_conv_w"].reshape(DEPTH, ML_CONV, 4, P).transpose(0, 3, 2, 1)
    g[:, :, G_CONV_W:G_CONV_W + 4 * ML_CONV] = taps.reshape(DEPTH, P, 4 * ML_CONV)
    g[:, ROW_I:ROW_I + ML_HEADS, G_GATE_B] = i["ml_b_i"]
    g[:, ROW_F:ROW_F + ML_HEADS, G_GATE_B] = i["ml_b_f"]
    return g


def first_gains(i):
    g = np.zeros((DEPTH + 1, P, KT), np.float32)
    g[:DEPTH] = i["norm_mix_pre"].reshape(DEPTH, KT, P).transpose(0, 2, 1)
    return g


def feature_major(a):
    return np.ascontiguousarray(a[0].reshape(a.shape[1], KT, P).transpose(2, 1, 0))


def kernel(**inputs):
    import concourse.bacc as bacc
    from concourse.bass_utils import run_bass_kernel_spmd

    i = {k: np.asarray(v) for k, v in inputs.items()}
    nc = bacc.Bacc("TRN2", target_bir_lowering=False, num_devices=1)
    first, stream = weight_stream(i)
    arrays = {"x_in": feature_major(i["x"]), "mem_in": feature_major(i["mem"]), "first_in": first,
              "first_g_in": first_gains(i), "w_in": stream, "g_in": gain_columns(i), "c_in": constants()}
    args = [nc.dram_tensor(n, a.shape, F32, kind="ExternalInput").ap() for n, a in arrays.items()]
    out = nc.dram_tensor("out", (P, KT, SEQ), F32, kind="ExternalOutput").ap()
    build(nc, *args, out)
    r = run_bass_kernel_spmd(nc, [arrays], core_ids=[0])
    y = r.results[0]["out"]
    return np.ascontiguousarray(y.transpose(2, 1, 0)).reshape(1, SEQ, D_MODEL)
```
